# Optimizing a Trainium2 kernel written in Bass

```python
import math
import jax
import jax.numpy as jnp
from jax import lax
import numpy as np
import jax, jax.numpy as jnp

D_MODEL = 1024
BATCH = 1
SEQ = 256
DEPTH = 1

GRID_W = 64
CTX_LEN = 256
N_MIXERS = 4
N_MOD = 6
EPS = 1e-6
FFN_HIDDEN = -(-8 * D_MODEL // (3 * 256)) * 256

GLA_HEADS = 4
GLA_QK = D_MODEL // 2
GLA_VD = D_MODEL
GLA_DK = GLA_QK // GLA_HEADS
GLA_DV = GLA_VD // GLA_HEADS
GLA_RANK = 16
GLA_GATE_NORM = 16.0
GLA_CHUNK = 64
GLA_IN = 2 * GLA_QK + GLA_VD + D_MODEL + 2 * GLA_RANK

HY_SHORT = 3
HY_BANDS = 16
HY_EMB = 1 + 2 * HY_BANDS
HY_FILTER_DIM = 64
HY_DECAY_TARGET = 1e-2
HY_FAST_DECAY = 0.3
HY_SLOW_DECAY = 1.5

ML_HEADS = 4
ML_INNER = 2 * D_MODEL
ML_DH = ML_INNER // ML_HEADS
ML_BLOCK = 4
ML_NBLOCKS = ML_INNER // ML_BLOCK
ML_CONV = 3
ML_CHUNK = 64

S5_GROUP = 16
S5_GROUPS = D_MODEL // S5_GROUP
S5_STATE = 64
S5_DT_MIN = 1e-3
S5_DT_MAX = 1e-1

N_GLA = (DEPTH + 3) // N_MIXERS
N_HY = (DEPTH + 2) // N_MIXERS
N_ML = (DEPTH + 1) // N_MIXERS
N_S5 = DEPTH // N_MIXERS


def rms_norm(x, g):
    x = x.astype(jnp.float32)
    return x * lax.rsqrt(jnp.mean(x * x, axis=-1, keepdims=True) + EPS) * g.astype(jnp.float32)

def head_rms_norm(o, g):
    bsz, length, heads, d = o.shape
    o = o * lax.rsqrt(jnp.mean(o * o, axis=-1, keepdims=True) + EPS) * g
    return o.reshape(bsz, length, heads * d)

def multihead_layer_norm(o, g):
    bsz, length, heads, d = o.shape
    o = o - jnp.mean(o, axis=-1, keepdims=True)
    o = o * lax.rsqrt(jnp.mean(o * o, axis=-1, keepdims=True) + EPS)
    return o.reshape(bsz, length, heads * d) * g

def modulate(h, shift, scale):
    return h * (1.0 + scale) + shift

def flip_seq(t):
    return jnp.flip(t, axis=1)

def depthwise_conv_centred(x, w, b):
    k = w.shape[0]
    y = lax.conv_general_dilated(x, w.astype(x.dtype)[:, None, :], window_strides=(1,),
                                 padding=[(k // 2, k // 2)], dimension_numbers=('NWC', 'WIO', 'NWC'),
                                 feature_group_count=x.shape[-1])
    return y + b

def to_col_major(x, rows):
    bsz, length, ch = x.shape
    return x.reshape(bsz, rows, GRID_W, ch).transpose(0, 2, 1, 3).reshape(bsz, length, ch)

def from_col_major(x, rows):
    bsz, length, ch = x.shape
    return x.reshape(bsz, GRID_W, rows, ch).transpose(0, 2, 1, 3).reshape(bsz, length, ch)

def swiglu(h, w_in, w_out):
    gate, up = jnp.split(h @ w_in, 2, axis=-1)
    return (jax.nn.silu(gate) * up) @ w_out

def gla_chunk_scan(q, k, v, g, s0):
    bsz, length, heads, _ = q.shape
    dv = v.shape[-1]
    n_chunks = length // GLA_CHUNK

    def chunked(t):
        return t.reshape(bsz, n_chunks, GLA_CHUNK, heads, t.shape[-1]).swapaxes(0, 1)

    causal = jnp.tril(jnp.ones((GLA_CHUNK, GLA_CHUNK), dtype=bool))

    def step(s, inp):
        qc, kc, vc, gc = inp
        b = jnp.cumsum(gc, axis=1)
        b_end = b[:, -1]
        q_dec = qc * jnp.exp(b)
        scores = jnp.einsum('bihd,bjhd->bhij', q_dec, kc * jnp.exp(-b))
        scores = jnp.where(causal, scores, 0.0)
        o = jnp.einsum('bhij,bjhv->bihv', scores, vc) + jnp.einsum('bihd,bhdv->bihv', q_dec, s)
        k_end = kc * jnp.exp(b_end[:, None] - b)
        s = jnp.exp(b_end)[..., None] * s + jnp.einsum('bjhd,bjhv->bhdv', k_end, vc)
        return s, o

    s_end, o = lax.scan(step, s0, (chunked(q), chunked(k), chunked(v), chunked(g)))
    return o.swapaxes(0, 1).reshape(bsz, length, heads, dv), s_end

def gla_mixer(h_lat, h_ctx, w_in, w_gate, b_gate, norm_g, w_out):
    def project(h):
        bsz, length, _ = h.shape
        z = h.astype(jnp.float32) @ w_in
        q, k, v, r, glr = jnp.split(z, [GLA_QK, 2 * GLA_QK, 2 * GLA_QK + GLA_VD,
                                       2 * GLA_QK + GLA_VD + D_MODEL], axis=-1)
        glr = glr.reshape(bsz, length, 2, GLA_RANK)
        g = jax.nn.log_sigmoid(jnp.einsum('blzr,zrk->blzk', glr, w_gate) + b_gate) / GLA_GATE_NORM
        g = g.reshape(bsz, length, 2, GLA_HEADS, GLA_DK)
        q = q.reshape(bsz, length, GLA_HEADS, GLA_DK) * GLA_DK ** -0.5
        k = k.reshape(bsz, length, GLA_HEADS, GLA_DK)
        v = v.reshape(bsz, length, GLA_HEADS, GLA_DV)
        return q, k, v, r, g[:, :, 0], g[:, :, 1]

    def bidirectional(h, s_f0, s_b0):
        q, k, v, r, g_f, g_b = project(h)
        o_f, s_f = gla_chunk_scan(q, k, v, g_f, s_f0)
        o_b, s_b = gla_chunk_scan(flip_seq(q), flip_seq(k), flip_seq(v), flip_seq(g_b), s_b0)
        o = head_rms_norm(o_f + flip_seq(o_b), norm_g)
        return (o * jax.nn.silu(r)) @ w_out, s_f, s_b

    s0 = jnp.zeros((h_ctx.shape[0], GLA_HEADS, GLA_DK, GLA_DV), jnp.float32)
    y_ctx, s_f, s_b = bidirectional(h_ctx, s0, s0)
    y_lat, _, _ = bidirectional(h_lat, s_f, s_b)
    return y_lat, y_ctx

def hyena_filter(length, w1, b1, w2, b2, w3, freq):
    pos = jnp.arange(length, dtype=jnp.float32)
    t = pos / length
    bands = jnp.linspace(1e-4, HY_BANDS - 1, HY_BANDS, dtype=jnp.float32)
    ang = 2.0 * math.pi * t[:, None] * bands[None]
    feats = jnp.concatenate([t[:, None], jnp.cos(ang), -jnp.sin(ang)], axis=-1)
    z = jnp.sin(freq * (feats @ w1 + b1))
    z = jnp.sin(freq * (z @ w2 + b2))
    h = (z @ w3).reshape(length, 2, D_MODEL)
    log_target = math.log(HY_DECAY_TARGET)
    deltas = jnp.abs(jnp.linspace(log_target / HY_SLOW_DECAY, log_target / HY_FAST_DECAY, D_MODEL,
                                  dtype=jnp.float32))
    decay = jnp.exp(-t[:, None] * deltas)
    h = h * decay[:, None]
    return h[:, 0], h[:, 1]

def fft_long_conv(u, h_f, h_b, bias):
    length = u.shape[1]
    h2 = jnp.concatenate([h_f[:1] + h_b[:1], h_f[1:], jnp.zeros_like(h_f[:1]),
                          jnp.flip(h_b[1:], axis=0)], axis=0)
    u_hat = jnp.fft.rfft(u, n=2 * length, axis=1)
    h_hat = jnp.fft.rfft(h2, axis=0)
    y = jnp.fft.irfft(u_hat * h_hat[None], n=2 * length, axis=1)[:, :length]
    return y + u * bias

def hyena_mixer(h_lat, h_ctx, w_in, conv_w, conv_b, f_w1, f_b1, f_w2, f_b2, f_w3, f_freq, f_bias, w_out):
    def run(h):
        length = h.shape[1]
        u = depthwise_conv_centred(h.astype(jnp.float32) @ w_in, conv_w, conv_b)
        x0, x1, v = jnp.split(u, 3, axis=-1)
        h_f, h_b = hyena_filter(length, f_w1, f_b1, f_w2, f_b2, f_w3, f_freq)
        y = x0 * fft_long_conv(v * x1, h_f, h_b, f_bias)
        return y @ w_out

    return run(h_lat), run(h_ctx)

def mlstm_chunk_scan(q, k, v, i_pre, log_f, state):
    bsz, length, heads, _ = q.shape
    n_chunks = length // ML_CHUNK

    def chunked(t):
        return t.reshape((bsz, n_chunks, ML_CHUNK) + t.shape[2:]).swapaxes(0, 1)

    causal = jnp.tril(jnp.ones((ML_CHUNK, ML_CHUNK), dtype=bool))[None, :, :, None]

    def step(carry, inp):
        c_mat, n_vec, m = carry
        qc, kc, vc, ic, fc = inp
        b = jnp.cumsum(fc, axis=1)
        b_end = b[:, -1]
        d_intra = jnp.where(causal, b[:, :, None] - b[:, None] + ic[:, None], -jnp.inf)
        d_inter = b + m[:, None]
        m_tok = jnp.maximum(jnp.max(d_intra, axis=2), d_inter)
        w_inter = jnp.exp(d_inter - m_tok)
        s = jnp.einsum('bihd,bjhd->bijh', qc, kc) * jnp.exp(d_intra - m_tok[:, :, None])
        num = jnp.einsum('bijh,bjhv->bihv', s, vc) + w_inter[..., None] * jnp.einsum('bihd,bhdv->bihv', qc, c_mat)
        den = jnp.sum(s, axis=2) + w_inter * jnp.einsum('bihd,bhd->bih', qc, n_vec)
        h = num / jnp.maximum(jnp.abs(den), jnp.exp(-m_tok))[..., None]
        d_state = b_end[:, None] - b + ic
        m_new = jnp.maximum(b_end + m, jnp.max(d_state, axis=1))
        w_prev = jnp.exp(b_end + m - m_new)
        w_tok = jnp.exp(d_state - m_new[:, None])
        c_mat = w_prev[..., None, None] * c_mat + jnp.einsum('bjh,bjhd,bjhv->bhdv', w_tok, kc, vc)
        n_vec = w_prev[..., None] * n_vec + jnp.einsum('bjh,bjhd->bhd', w_tok, kc)
        return (c_mat, n_vec, m_new), h

    state, h = lax.scan(step, state, (chunked(q), chunked(k), chunked(v), chunked(i_pre), chunked(log_f)))
    return h.swapaxes(0, 1).reshape(bsz, length, heads, v.shape[-1]), state

def mlstm_mixer(h_lat, h_ctx, w_in, conv_w, conv_b, w_q, w_k, w_v, w_gates, b_gates, norm_g, skip, w_out):
    def project(h):
        bsz, length, _ = h.shape
        x_m, z = jnp.split(h.astype(jnp.float32) @ w_in, 2, axis=-1)
        x_c = jax.nn.silu(depthwise_conv_centred(x_m, conv_w, conv_b))

        def block_diag(t, w):
            t = t.reshape(bsz, length, ML_NBLOCKS, ML_BLOCK)
            return jnp.einsum('blnc,ncd->blnd', t, w).reshape(bsz, length, ML_INNER)

        q, k, v = block_diag(x_c, w_q), block_diag(x_c, w_k), block_diag(x_m, w_v)
        gates = jnp.einsum('blc,zcg->blzg', jnp.concatenate([q, k, v], axis=-1), w_gates) + b_gates
        i_pre = gates[..., :ML_HEADS]
        log_f = jax.nn.log_sigmoid(gates[..., ML_HEADS:])
        heads = lambda t: t.reshape(bsz, length, ML_HEADS, ML_DH)
        return heads(q), heads(k) * ML_DH ** -0.5, heads(v), i_pre, log_f, x_c, z

    def bidirectional(h, state_f, state_b):
        q, k, v, i_pre, log_f, x_c, z = project(h)
        h_f, state_f = mlstm_chunk_scan(q, k, v, i_pre[:, :, 0], log_f[:, :, 0], state_f)
        h_b, state_b = mlstm_chunk_scan(flip_seq(q), flip_seq(k), flip_seq(v), flip_seq(i_pre[:, :, 1]),
                                        flip_seq(log_f[:, :, 1]), state_b)
        h_n = multihead_layer_norm(h_f + flip_seq(h_b), norm_g)
        return ((h_n + skip * x_c) * jax.nn.silu(z)) @ w_out, state_f, state_b

    bsz = h_ctx.shape[0]
    state0 = (jnp.zeros((bsz, ML_HEADS, ML_DH, ML_DH), jnp.float32),
              jnp.zeros((bsz, ML_HEADS, ML_DH), jnp.float32),
              jnp.full((bsz, ML_HEADS), -jnp.inf, jnp.float32))
    y_ctx, st_f, st_b = bidirectional(h_ctx, state0, state0)
    y_lat, _, _ = bidirectional(h_lat, st_f, st_b)
    return y_lat, y_ctx

def _linear_recurrence_combine(left, right):
    a_l, b_l = left
    a_r, b_r = right
    return a_l * a_r, a_r * b_l + b_r

def s5_mixer(h_lat, h_ctx, lam_re, lam_im, log_dt, b_re, b_im, c_re, c_im, d_skip, w_glu):
    f32 = jnp.float32
    b_mat = lax.complex(b_re.astype(f32), b_im.astype(f32))
    c_mat = lax.complex(c_re.astype(f32), c_im.astype(f32))

    def discretise(direction):
        lam = lax.complex(lam_re[direction].astype(f32), lam_im[direction].astype(f32))
        lam_bar = jnp.exp(lam * jnp.exp(log_dt[direction].astype(f32))[:, None])
        return lam_bar, ((lam_bar - 1.0) / lam)[..., None] * b_mat

    disc = (discretise(0), discretise(1))

    def scan_readout(u_seq, lam_bar, b_bar, x0):
        bu = jnp.einsum('gpc,lbgc->lbgp', b_bar, u_seq)
        a = jnp.broadcast_to(lam_bar, (u_seq.shape[0], 1) + lam_bar.shape)
        a_cum, xs = lax.associative_scan(_linear_recurrence_combine, (a, bu), axis=0)
        xs = xs + a_cum * x0
        return jnp.real(jnp.einsum('gcp,lbgp->lbgc', c_mat, xs)), xs[-1]

    def bidirectional(h, x0_f, x0_b):
        bsz, length, _ = h.shape
        u = h.astype(f32)
        u_seq = u.swapaxes(0, 1).reshape(length, bsz, S5_GROUPS, S5_GROUP).astype(jnp.complex64)
        y_f, x_f = scan_readout(u_seq, disc[0][0], disc[0][1], x0_f)
        y_b, x_b = scan_readout(jnp.flip(u_seq, axis=0), disc[1][0], disc[1][1], x0_b)
        y = (y_f + jnp.flip(y_b, axis=0)).reshape(length, bsz, D_MODEL).swapaxes(0, 1) + d_skip * u
        val, gate = jnp.split(jax.nn.gelu(y) @ w_glu, 2, axis=-1)
        return val * jax.nn.sigmoid(gate), x_f, x_b

    x0 = jnp.zeros((h_ctx.shape[0], S5_GROUPS, S5_STATE), jnp.complex64)
    y_ctx, x_f, x_b = bidirectional(h_ctx, x0, x0)
    y_lat, _, _ = bidirectional(h_lat, x_f, x_b)
    return y_lat, y_ctx

def first_inputs(seed: int = 0) -> dict:
    key = jax.random.key(seed)
    keys = iter(jax.random.split(key, 96))
    f32 = jnp.float32

    def normal(shape, scale=1.0):
        return scale * jax.random.normal(next(keys), shape, f32)

    def gain(shape):
        return 1.0 + normal(shape, 0.02)

    D, F = D_MODEL, FFN_HIDDEN
    ml_b_i = normal((N_ML, 2, ML_HEADS), 0.1)
    ml_b_f = jnp.linspace(3.0, 6.0, ML_HEADS, dtype=f32) + normal((N_ML, 2, ML_HEADS), 0.1)
    lam_im_init = math.pi * jnp.arange(S5_STATE, dtype=f32)
    return {
        'x': normal((BATCH, SEQ, D)),
        'c': normal((BATCH, D)),
        'ctx': normal((BATCH, CTX_LEN, D)),
        'c_ctx': normal((D,)),
        'mod_w': normal((DEPTH, D, N_MOD * D), D ** -0.5),
        'mod_b': normal((DEPTH, N_MOD * D), 0.01),
        'norm_g': gain((DEPTH, 4, D)),
        'ffn_w_in': normal((DEPTH, D, 2 * F), D ** -0.5),
        'ffn_w_out': normal((DEPTH, F, D), F ** -0.5),
        'gla_w_in': normal((N_GLA, D, GLA_IN), D ** -0.5),
        'gla_w_gate': normal((N_GLA, 2, GLA_RANK, GLA_QK), GLA_RANK ** -0.5),
        'gla_b_gate': normal((N_GLA, 2, GLA_QK), 0.1),
        'gla_norm_g': gain((N_GLA, GLA_DV)),
        'gla_w_out': normal((N_GLA, GLA_VD, D), GLA_VD ** -0.5),
        'hy_w_in': normal((N_HY, D, 3 * D), D ** -0.5),
        'hy_conv_w': normal((N_HY, HY_SHORT, 3 * D), HY_SHORT ** -0.5),
        'hy_conv_b': normal((N_HY, 3 * D), 0.01),
        'hy_f_w1': normal((N_HY, HY_EMB, HY_FILTER_DIM), HY_EMB ** -0.5),
        'hy_f_b1': normal((N_HY, HY_FILTER_DIM), 0.1),
        'hy_f_w2': normal((N_HY, HY_FILTER_DIM, HY_FILTER_DIM), HY_FILTER_DIM ** -0.5),
        'hy_f_b2': normal((N_HY, HY_FILTER_DIM), 0.1),
        'hy_f_w3': normal((N_HY, HY_FILTER_DIM, 2 * D), HY_FILTER_DIM ** -0.5),
        'hy_f_freq': gain((N_HY, HY_FILTER_DIM)),
        'hy_f_bias': normal((N_HY, D), 0.1),
        'hy_w_out': normal((N_HY, D, D), D ** -0.5),
        'ml_w_in': normal((N_ML, D, 2 * ML_INNER), D ** -0.5),
        'ml_conv_w': normal((N_ML, ML_CONV, ML_INNER), ML_CONV ** -0.5),
        'ml_conv_b': normal((N_ML, ML_INNER), 0.01),
        'ml_w_q': normal((N_ML, ML_NBLOCKS, ML_BLOCK, ML_BLOCK), ML_BLOCK ** -0.5),
        'ml_w_k': normal((N_ML, ML_NBLOCKS, ML_BLOCK, ML_BLOCK), ML_BLOCK ** -0.5),
        'ml_w_v': normal((N_ML, ML_NBLOCKS, ML_BLOCK, ML_BLOCK), ML_BLOCK ** -0.5),
        'ml_w_gates': normal((N_ML, 2, 3 * ML_INNER, 2 * ML_HEADS), (3 * ML_INNER) ** -0.5),
        'ml_b_gates': jnp.concatenate([ml_b_i, ml_b_f], axis=-1),
        'ml_norm_g': gain((N_ML, ML_INNER)),
        'ml_skip': gain((N_ML, ML_INNER)),
        'ml_w_out': normal((N_ML, ML_INNER, D), ML_INNER ** -0.5),
        's5_lam_re': -0.5 + normal((N_S5, 2, S5_GROUPS, S5_STATE), 0.01),
        's5_lam_im': lam_im_init + normal((N_S5, 2, S5_GROUPS, S5_STATE), 0.01),
        's5_log_dt': jax.random.uniform(next(keys), (N_S5, 2, S5_GROUPS), f32,
                                        minval=math.log(S5_DT_MIN), maxval=math.log(S5_DT_MAX)),
        's5_b_re': normal((N_S5, S5_GROUPS, S5_STATE, S5_GROUP), (2 * S5_GROUP) ** -0.5),
        's5_b_im': normal((N_S5, S5_GROUPS, S5_STATE, S5_GROUP), (2 * S5_GROUP) ** -0.5),
        's5_c_re': normal((N_S5, S5_GROUPS, S5_GROUP, S5_STATE), (2 * S5_STATE) ** -0.5),
        's5_c_im': normal((N_S5, S5_GROUPS, S5_GROUP, S5_STATE), (2 * S5_STATE) ** -0.5),
        's5_d': normal((N_S5, D)),
        's5_w_glu': normal((N_S5, D, 2 * D), D ** -0.5),
    }

def first_block(x, c, ctx, c_ctx, mod_w, mod_b, norm_g, ffn_w_in, ffn_w_out,
              gla_w_in, gla_w_gate, gla_b_gate, gla_norm_g, gla_w_out,
              hy_w_in, hy_conv_w, hy_conv_b, hy_f_w1, hy_f_b1, hy_f_w2, hy_f_b2, hy_f_w3, hy_f_freq, hy_f_bias,
              hy_w_out,
              ml_w_in, ml_conv_w, ml_conv_b, ml_w_q, ml_w_k, ml_w_v, ml_w_gates, ml_b_gates, ml_norm_g, ml_skip,
              ml_w_out,
              s5_lam_re, s5_lam_im, s5_log_dt, s5_b_re, s5_b_im, s5_c_re, s5_c_im, s5_d, s5_w_glu):
    bsz = x.shape[0]
    rows = x.shape[1] // GRID_W
    lat, cx = x, ctx
    silu_c = jax.nn.silu(c.astype(jnp.float32))
    silu_cc = jax.nn.silu(c_ctx.astype(jnp.float32))
    for i in range(DEPTH):
        kind, j = i % N_MIXERS, i // N_MIXERS
        last = i == DEPTH - 1
        mod_l = (silu_c @ mod_w[i] + mod_b[i]).reshape(bsz, N_MOD, 1, D_MODEL)
        mod_c = (silu_cc @ mod_w[i] + mod_b[i]).reshape(N_MOD, 1, D_MODEL)
        h_lat = modulate(rms_norm(lat, norm_g[i, 0]), mod_l[:, 0], mod_l[:, 1])
        h_ctx = modulate(rms_norm(cx, norm_g[i, 0]), mod_c[0], mod_c[1])
        if kind == 0:
            y_lat, y_ctx = gla_mixer(h_lat, h_ctx, gla_w_in[j], gla_w_gate[j], gla_b_gate[j], gla_norm_g[j],
                                     gla_w_out[j])
        elif kind == 1:
            y_lat, y_ctx = hyena_mixer(h_lat, h_ctx, hy_w_in[j], hy_conv_w[j], hy_conv_b[j], hy_f_w1[j],
                                       hy_f_b1[j], hy_f_w2[j], hy_f_b2[j], hy_f_w3[j], hy_f_freq[j],
                                       hy_f_bias[j], hy_w_out[j])
        elif kind == 2:
            y_lat, y_ctx = mlstm_mixer(to_col_major(h_lat, rows), h_ctx, ml_w_in[j], ml_conv_w[j], ml_conv_b[j],
                                       ml_w_q[j], ml_w_k[j], ml_w_v[j], ml_w_gates[j], ml_b_gates[j],
                                       ml_norm_g[j], ml_skip[j], ml_w_out[j])
            y_lat = from_col_major(y_lat, rows)
        else:
            y_lat, y_ctx = s5_mixer(to_col_major(h_lat, rows), h_ctx, s5_lam_re[j], s5_lam_im[j], s5_log_dt[j],
                                    s5_b_re[j], s5_b_im[j], s5_c_re[j], s5_c_im[j], s5_d[j], s5_w_glu[j])
            y_lat = from_col_major(y_lat, rows)
        lat = lat + (mod_l[:, 2] * rms_norm(y_lat, norm_g[i, 1])).astype(lat.dtype)
        h = modulate(rms_norm(lat, norm_g[i, 2]), mod_l[:, 3], mod_l[:, 4])
        lat = lat + (mod_l[:, 5] * rms_norm(swiglu(h, ffn_w_in[i], ffn_w_out[i]), norm_g[i, 3])).astype(lat.dtype)
        if not last:
            cx = cx + (mod_c[2] * rms_norm(y_ctx, norm_g[i, 1])).astype(cx.dtype)
            hc = modulate(rms_norm(cx, norm_g[i, 2]), mod_c[3], mod_c[4])
            cx = cx + (mod_c[5] * rms_norm(swiglu(hc, ffn_w_in[i], ffn_w_out[i]), norm_g[i, 3])).astype(cx.dtype)
    return lat


DEPTH_2 = 2

HEAD_DIM = 64
ROPE_THETA = 10000.0
RMS_EPS = 1e-6
QBLK = 128
NEG_INF = -1e30

NA_HEADS = 8
NA_ROWS = 8
NA_COLS = 16
NA_WIDTH = NA_HEADS * HEAD_DIM

MLA_HEADS = 8
MLA_Q_RANK = 256
MLA_KV_RANK = 128
MLA_NOPE = 64
MLA_ROPE = 32
MLA_V = 64

DIL_PAIRS = ((128, 1), (512, 4), (2048, 16))
DIL_GROUPS = len(DIL_PAIRS)
DIL_HEADS = D_MODEL // HEAD_DIM

D_FF = 4 * D_MODEL
N_EVEN = (DEPTH_2 + 1) // 2
N_ODD = DEPTH_2 // 2

EVEN_IN = 3 * NA_WIDTH + MLA_Q_RANK + MLA_KV_RANK + MLA_ROPE
EVEN_MIX = NA_WIDTH + MLA_HEADS * MLA_V
ODD_IN = DIL_GROUPS * 3 * DIL_HEADS * HEAD_DIM
ODD_MIX = DIL_HEADS * HEAD_DIM


def rms_norm_2(x, g):
    xf = x.astype(jnp.float32)
    y = xf * lax.rsqrt(jnp.mean(xf * xf, axis=-1, keepdims=True) + RMS_EPS)
    return (y * g.astype(jnp.float32)).astype(x.dtype)

def rope_tables(seq_len, dim):
    inv = 1.0 / (ROPE_THETA ** (jnp.arange(0, dim, 2, dtype=jnp.float32) / dim))
    ang = jnp.arange(seq_len, dtype=jnp.float32)[:, None] * inv[None, :]
    return jnp.cos(ang), jnp.sin(ang)

def apply_rope(x, cos, sin):
    half = x.shape[-1] // 2
    shp = (1, cos.shape[0]) + (1,) * (x.ndim - 3) + (cos.shape[1],)
    c = cos.reshape(shp).astype(x.dtype)
    s = sin.reshape(shp).astype(x.dtype)
    x1, x2 = x[..., :half], x[..., half:]
    return jnp.concatenate([x1 * c - x2 * s, x2 * c + x1 * s], axis=-1)

def neighbourhood_attention(q, k, v, rpb):
    b, s, h, dh = q.shape
    rows = s // GRID_W
    wr = min(NA_ROWS, rows)
    wc = NA_COLS
    qg = q.reshape(b, rows, GRID_W, h, dh)
    kg = k.reshape(b, rows, GRID_W, h, dh)
    vg = v.reshape(b, rows, GRID_W, h, dh)
    cols = jnp.arange(GRID_W)
    col_start = jnp.clip(cols - wc // 2, 0, GRID_W - wc)
    col_idx = col_start[:, None] + jnp.arange(wc)[None, :]
    col_rel = col_idx - cols[:, None] + (NA_COLS - 1)
    scale = dh ** -0.5

    def row_fn(r):
        r_start = jnp.clip(r - wr // 2, 0, rows - wr)
        row_rel = r_start + jnp.arange(wr) - r + (NA_ROWS - 1)
        q_row = lax.dynamic_index_in_dim(qg, r, axis=1, keepdims=False)
        k_rows = lax.dynamic_slice_in_dim(kg, r_start, wr, axis=1)
        v_rows = lax.dynamic_slice_in_dim(vg, r_start, wr, axis=1)
        k_win = k_rows[:, :, col_idx]
        v_win = v_rows[:, :, col_idx]
        sc = jnp.einsum('bchd,bicjhd->bhcij', q_row, k_win,
                        preferred_element_type=jnp.float32) * scale
        bias = rpb[:, row_rel[:, None, None], col_rel[None, :, :]]
        sc = sc + bias.transpose(0, 2, 1, 3).astype(jnp.float32)[None]
        p = jax.nn.softmax(sc.reshape(b, h, GRID_W, wr * wc), axis=-1).reshape(sc.shape)
        return jnp.einsum('bhcij,bicjhd->bchd', p.astype(v.dtype), v_win)

    out = lax.map(row_fn, jnp.arange(rows))
    return out.transpose(1, 0, 2, 3, 4).reshape(b, s, h * dh)

def dense_attention(q, k, v, scale):
    b, s, h, dq = q.shape
    nblk = s // QBLK
    qb = q.reshape(b, nblk, QBLK, h, dq).transpose(1, 0, 2, 3, 4)

    def blk(qi):
        sc = jnp.einsum('bqhd,bkhd->bhqk', qi, k, preferred_element_type=jnp.float32) * scale
        p = jax.nn.softmax(sc, axis=-1)
        return jnp.einsum('bhqk,bkhd->bqhd', p.astype(v.dtype), v)

    out = lax.map(blk, qb)
    return out.transpose(1, 0, 2, 3, 4).reshape(b, s, h * v.shape[-1])

def dilated_attention(q, k, v):
    b, s, g, h, dh = q.shape
    nblk = s // QBLK
    scale = dh ** -0.5
    offsets = [jnp.arange(-(w // 2), w // 2 + 1, d) for (w, d) in DIL_PAIRS]
    ks = [k[:, :, gi] for gi in range(g)]
    vs = [v[:, :, gi] for gi in range(g)]

    def blk(bi):
        start = bi * QBLK
        qpos = start + jnp.arange(QBLK)
        q_blk = lax.dynamic_slice_in_dim(q, start, QBLK, axis=1)
        outs, lses = [], []
        for gi in range(g):
            kpos = qpos[:, None] + offsets[gi][None, :]
            valid = (kpos >= 0) & (kpos < s)
            kidx = jnp.clip(kpos, 0, s - 1)
            k_sel = ks[gi][:, kidx]
            v_sel = vs[gi][:, kidx]
            sc = jnp.einsum('bqhd,bqjhd->bhqj', q_blk[:, :, gi], k_sel,
                            preferred_element_type=jnp.float32) * scale
            sc = jnp.where(valid[None, None], sc, NEG_INF)
            m = jnp.max(sc, axis=-1, keepdims=True)
            e = jnp.exp(sc - m)
            z = jnp.sum(e, axis=-1, keepdims=True)
            o = jnp.einsum('bhqj,bqjhd->bqhd', (e / z).astype(v.dtype), v_sel)
            outs.append(o.astype(jnp.float32))
            lses.append((m + jnp.log(z))[..., 0])
        lse = jnp.stack(lses, axis=0)
        wgt = jax.nn.softmax(lse, axis=0).transpose(0, 1, 3, 2)[..., None]
        out = jnp.sum(wgt * jnp.stack(outs, axis=0), axis=0)
        return out.astype(v.dtype)

    out = lax.map(blk, jnp.arange(nblk))
    return out.transpose(1, 0, 2, 3, 4).reshape(b, s, h * dh)

def even_mixer(xn, w_in, rpb, q_norm, w_uq, kv_norm, w_ukv, w_o, cos_r, sin_r):
    b, s, _ = xn.shape
    hcat = xn @ w_in
    o0 = 3 * NA_WIDTH
    o1 = o0 + MLA_Q_RANK
    o2 = o1 + MLA_KV_RANK
    a_qkv = hcat[..., :o0].reshape(b, s, 3, NA_HEADS, HEAD_DIM)
    out_a = neighbourhood_attention(a_qkv[:, :, 0], a_qkv[:, :, 1], a_qkv[:, :, 2], rpb)
    c_q = rms_norm_2(hcat[..., o0:o1], q_norm)
    c_kv = rms_norm_2(hcat[..., o1:o2], kv_norm)
    k_pe = apply_rope(hcat[..., o2:][:, :, None, :], cos_r, sin_r)
    q = (c_q @ w_uq).reshape(b, s, MLA_HEADS, MLA_NOPE + MLA_ROPE)
    q = jnp.concatenate([q[..., :MLA_NOPE], apply_rope(q[..., MLA_NOPE:], cos_r, sin_r)], axis=-1)
    kv = (c_kv @ w_ukv).reshape(b, s, MLA_HEADS, MLA_NOPE + MLA_V)
    k = jnp.concatenate([kv[..., :MLA_NOPE],
                         jnp.broadcast_to(k_pe, (b, s, MLA_HEADS, MLA_ROPE))], axis=-1)
    v = kv[..., MLA_NOPE:]
    out_b = dense_attention(q, k, v, (MLA_NOPE + MLA_ROPE) ** -0.5)
    return jnp.concatenate([out_a, out_b], axis=-1) @ w_o

def odd_mixer(xn, w_in, w_o, cos_f, sin_f):
    b, s, _ = xn.shape
    hcat = (xn @ w_in).reshape(b, s, DIL_GROUPS, 3, DIL_HEADS, HEAD_DIM)
    q = apply_rope(hcat[:, :, :, 0], cos_f, sin_f)
    k = apply_rope(hcat[:, :, :, 1], cos_f, sin_f)
    v = hcat[:, :, :, 2]
    return dilated_attention(q, k, v) @ w_o

def sq_relu_mlp(xn, w1, w2):
    return jnp.square(jax.nn.relu(xn @ w1)) @ w2

def second_inputs(seed: int = 0) -> dict:
    key = jax.random.key(seed)
    ks = jax.random.split(key, 16)
    f32 = jnp.float32

    def nrm(k, shape, scale):
        return jax.random.normal(k, shape, f32) * scale

    return {
        "x": nrm(ks[0], (BATCH, SEQ, D_MODEL), 1.0),
        "norm_mix": 1.0 + nrm(ks[1], (DEPTH_2, D_MODEL), 0.1),
        "norm_mlp": 1.0 + nrm(ks[2], (DEPTH_2, D_MODEL), 0.1),
        "norm_final": 1.0 + nrm(ks[3], (D_MODEL,), 0.1),
        "ev_w_in": nrm(ks[4], (N_EVEN, D_MODEL, EVEN_IN), D_MODEL ** -0.5),
        "ev_rpb": nrm(ks[5], (N_EVEN, NA_HEADS, 2 * NA_ROWS - 1, 2 * NA_COLS - 1), 0.5),
        "ev_q_norm": 1.0 + nrm(ks[6], (N_EVEN, MLA_Q_RANK), 0.1),
        "ev_w_uq": nrm(ks[7], (N_EVEN, MLA_Q_RANK, MLA_HEADS * (MLA_NOPE + MLA_ROPE)), MLA_Q_RANK ** -0.5),
        "ev_kv_norm": 1.0 + nrm(ks[8], (N_EVEN, MLA_KV_RANK), 0.1),
        "ev_w_ukv": nrm(ks[9], (N_EVEN, MLA_KV_RANK, MLA_HEADS * (MLA_NOPE + MLA_V)), MLA_KV_RANK ** -0.5),
        "ev_w_o": nrm(ks[10], (N_EVEN, EVEN_MIX, D_MODEL), EVEN_MIX ** -0.5),
        "od_w_in": nrm(ks[11], (N_ODD, D_MODEL, ODD_IN), D_MODEL ** -0.5),
        "od_w_o": nrm(ks[12], (N_ODD, ODD_MIX, D_MODEL), ODD_MIX ** -0.5),
        "mlp_w1": nrm(ks[13], (DEPTH_2, D_MODEL, D_FF), D_MODEL ** -0.5),
        "mlp_w2": nrm(ks[14], (DEPTH_2, D_FF, D_MODEL), D_FF ** -0.5),
    }

def second_block(x, norm_mix, norm_mlp, norm_final, ev_w_in, ev_rpb, ev_q_norm, ev_w_uq,
              ev_kv_norm, ev_w_ukv, ev_w_o, od_w_in, od_w_o, mlp_w1, mlp_w2):
    s = x.shape[1]
    cos_r, sin_r = rope_tables(s, MLA_ROPE)
    cos_f, sin_f = rope_tables(s, HEAD_DIM)
    for layer in range(DEPTH_2):
        xn = rms_norm_2(x, norm_mix[layer])
        if layer % 2 == 0:
            e = layer // 2
            x = x + even_mixer(xn, ev_w_in[e], ev_rpb[e], ev_q_norm[e], ev_w_uq[e],
                               ev_kv_norm[e], ev_w_ukv[e], ev_w_o[e], cos_r, sin_r)
        else:
            o = layer // 2
            x = x + odd_mixer(xn, od_w_in[o], od_w_o[o], cos_f, sin_f)
        x = x + sq_relu_mlp(rms_norm_2(x, norm_mlp[layer]), mlp_w1[layer], mlp_w2[layer])
    return rms_norm_2(x, norm_final)


def setup_inputs(seed=0):
    out = dict(first_inputs(seed))
    for name, value in second_inputs(seed + 1).items():
        if name != "x":
            out[name + "_2"] = value
    return out


def reference(
    x, c, ctx, c_ctx, mod_w, mod_b, norm_g, ffn_w_in, ffn_w_out, gla_w_in, gla_w_gate,
    gla_b_gate, gla_norm_g, gla_w_out, hy_w_in, hy_conv_w, hy_conv_b, hy_f_w1, hy_f_b1, hy_f_w2,
    hy_f_b2, hy_f_w3, hy_f_freq, hy_f_bias, hy_w_out, ml_w_in, ml_conv_w, ml_conv_b, ml_w_q,
    ml_w_k, ml_w_v, ml_w_gates, ml_b_gates, ml_norm_g, ml_skip, ml_w_out, s5_lam_re, s5_lam_im,
    s5_log_dt, s5_b_re, s5_b_im, s5_c_re, s5_c_im, s5_d, s5_w_glu, norm_mix_2, norm_mlp_2,
    norm_final_2, ev_w_in_2, ev_rpb_2, ev_q_norm_2, ev_w_uq_2, ev_kv_norm_2, ev_w_ukv_2,
    ev_w_o_2, od_w_in_2, od_w_o_2, mlp_w1_2, mlp_w2_2,
):
    x = first_block(
        x, c, ctx, c_ctx, mod_w, mod_b, norm_g, ffn_w_in, ffn_w_out, gla_w_in, gla_w_gate,
        gla_b_gate, gla_norm_g, gla_w_out, hy_w_in, hy_conv_w, hy_conv_b, hy_f_w1, hy_f_b1,
        hy_f_w2, hy_f_b2, hy_f_w3, hy_f_freq, hy_f_bias, hy_w_out, ml_w_in, ml_conv_w,
        ml_conv_b, ml_w_q, ml_w_k, ml_w_v, ml_w_gates, ml_b_gates, ml_norm_g, ml_skip, ml_w_out,
        s5_lam_re, s5_lam_im, s5_log_dt, s5_b_re, s5_b_im, s5_c_re, s5_c_im, s5_d, s5_w_glu,
    )
    return second_block(
        x, norm_mix_2, norm_mlp_2, norm_final_2, ev_w_in_2, ev_rpb_2, ev_q_norm_2, ev_w_uq_2,
        ev_kv_norm_2, ev_w_ukv_2, ev_w_o_2, od_w_in_2, od_w_o_2, mlp_w1_2, mlp_w2_2,
    )


_drawn_inputs = setup_inputs


def setup_inputs(seed=0):
    import zlib

    import numpy as np

    out = dict(_drawn_inputs(seed))
    spreads = {}
    factors = {'gla_norm_g': 5.087, 'ev_q_norm_2': 7.09, 'ev_kv_norm_2': 3.753}
    for name, (base, spread) in spreads.items():
        noise = np.random.default_rng([zlib.crc32(name.encode()), seed]).standard_normal(out[name].shape)
        drawn = base * np.exp(spread * noise) if base else spread * noise
        out[name] = jnp.asarray(drawn.astype(out[name].dtype))
    for name, factor in factors.items():
        out[name] = (out[name] * factor).astype(out[name].dtype)
    return out
```

```python
from contextlib import ExitStack

import numpy as np

import concourse.bass as bass
from concourse import mybir

ACT = mybir.ActivationFunctionType
ALU = mybir.AluOpType
F32 = mybir.dt.float32
BF16 = mybir.dt.bfloat16
U32 = mybir.dt.uint32
AX = mybir.AxisListType.X

P = 128
SEQ = 256
NT = SEQ // P
D = 1024
KD = D // P
EPS = 1e-6
GRID = 64

GH, GDK, GDV, RANK, CHUNK = 4, 128, 256, 16, 64
GLA_QK, GLA_V = GH * GDK, GH * GDV
GATE_NORM = 16.0
FF = 2816
FFC = FF // P
FF_RING = 6
FF_LOOPS = 3

HD = 64
NA_H, MLA_H, OD_H = 8, 8, 16
NOPE, ROPE, QR, KVR = 64, 32, 256, 128
MQ = NOPE + ROPE
DFF = 4 * D
MLP_RING = 4
MLP_LOOPS = DFF // 256 // MLP_RING
OD_PAIRS = OD_H // 2
RPB = NA_H * 15 * 31
NEG = -1e30

C_ID, C_GM, C_NM, C_MR, C_OM, C_OR = 0, 128, 384, 896, 1024, 2048
C_ALL = 2304
VA_C, VA_CC, VA_NG, VA_MB, VA_QN, VA_KN, VA_BG, VA_N = 0, 8, 16, 48, 96, 98, 99, 107
VB_MIX, VB_MLP, VB_N = 0, 16, 32
POOL = 18432


def constants():
    c = np.zeros((P, C_ALL), np.float32)
    c[:, C_ID:C_ID + P] = np.eye(P)
    j, i = np.meshgrid(np.arange(P), np.arange(P), indexing="ij")
    same = j // CHUNK == i // CHUNK
    c[:, C_GM:C_GM + P] = same & (j <= i)
    c[:, C_GM + P:C_GM + 2 * P] = same & (j >= i)
    tok = np.arange(SEQ)
    start = np.clip(tok % GRID - 8, 0, GRID - 16)
    kc = tok % GRID
    na = np.where((kc[None] >= start[:, None]) & (kc[None] < start[:, None] + 16), 0.0, NEG)
    c[:, C_NM:C_MR] = na.reshape(NT, P, SEQ).transpose(1, 0, 2).reshape(P, -1)

    def rope(pos, dim):
        inv = np.float32(1.0) / (np.float32(10000.0) ** (np.arange(0, dim, 2, dtype=np.float32) / np.float32(dim)))
        ang = pos.astype(np.float32)[:, None] * inv[None]
        co, si = np.cos(ang), np.sin(ang)
        t = np.stack([np.concatenate([co, co], 1), np.concatenate([-si, si], 1)], 1)
        return t.reshape(NT, P, 2 * dim).transpose(1, 0, 2).reshape(P, -1)

    c[:, C_MR:C_OM] = rope(tok, ROPE)
    s, m, a = np.meshgrid(np.arange(4), np.arange(4), np.arange(16), indexing="ij")
    perm = (16 * a + 4 * m + s).reshape(-1)
    dist = perm[None] - perm[:, None]
    wide = np.where(np.abs(dist) <= 64, 0.0, NEG)
    by4 = np.where(dist % 4 == 0, 0.0, NEG)
    by16 = np.where(dist % 16 == 0, 0.0, NEG)
    om = np.zeros((P, NT, 512), np.float32)
    for t in range(NT):
        rows = slice(t * P, t * P + P)
        om[:, t] = np.concatenate([wide[rows], by4[rows, rows], by16[rows, rows]], 1)
    c[:, C_OM:C_OR] = om.reshape(P, -1)
    c[:, C_OR:] = rope(perm, HD)
    return c


def program(nc, a, out):
    with ExitStack() as ctx:
        def sb(name, shape, dt=F32):
            return ctx.enter_context(nc.sbuf_tensor(name, shape, dt))

        def sem(name):
            return ctx.enter_context(nc.semaphore(name))

        bank = [ctx.enter_context(nc.psum_tensor(f"bank{i}", [P, 512], F32)) for i in range(8)]
        pool = sb("weight_pool", [P, POOL])
        work = sb("work", [P, 21504])
        hTs = sb("hT", [P, 4096])
        res = sb("residual", [P, NT, D])
        xn = sb("normed", [P, NT, D])
        consts = sb("consts", [P, C_ALL])
        vecA = sb("vecA", [P, P])
        vecB = sb("vecB", [P, VB_N])
        mods = sb("mods", [P, 48, 2])
        eff = sb("eff", [P, 5, KD])
        silc = sb("silc", [P, KD, 2])
        wglr = sb("wglr", [P, KD, 2 * RANK])
        gnrow = sb("gnrow", [P, GDV])
        stat = sb("stat", [P, 192])
        zero = sb("zero", [P, 512], BF16)
        decay = sb("decay", [P, 2 * GH * 8])
        bend = sb("bend", [P, 2 * GH * 8])
        rsum = sb("rsum", [P, 48])
        rinv = sb("rinv", [P, 48])

        skew = nc.dram_tensor("bias_copies", (GRID, RPB), F32).ap()
        ident = consts[:, C_ID:C_ID + P]
        eps = stat[:, 90:91]

        def view(t, at, *dims):
            n = 1
            for d in dims:
                n *= d
            v = t[:, at:at + n]
            if len(dims) == 2:
                return v.rearrange("p (a b) -> p a b", b=dims[1])
            if len(dims) == 3:
                return v.rearrange("p (a b c) -> p a b c", b=dims[1], c=dims[2])
            if len(dims) == 4:
                return v.rearrange("p (a b c d) -> p a b c d", b=dims[1], c=dims[2], d=dims[3])
            return v

        def dilated(v):
            return v.rearrange("p (a m s) -> p s m a", m=4, s=4)

        def by_sma(v):
            return v.rearrange("p (s m a) -> p s m a", m=4, s=4)

        hT_all = view(hTs, 0, KD, 512)
        G1 = view(work, 0, 2, GH, 512)
        G2 = view(work, 4096, 2, GH, 512)
        qd = view(work, 8192, 2, GH, SEQ)
        kd = view(work, 10240, 2, GH, SEQ)
        wgate = work[0:2 * RANK, 10240:10240 + 2 * GLA_QK]
        glrT = work[0:2 * RANK, 10240 + 2 * GLA_QK:10240 + 2 * GLA_QK + 512]
        kT = view(work, 12288, GH, 512)
        sT = view(work, 12288, 2, 2, 4, P)
        qT = view(work, 14336, GH, SEQ)
        vG = view(work, 15360, 4, GLA_V)
        rG = view(work, 19456, NT, D)
        keT = view(hTs, 0, 2, GH, 4, P)
        reset = view(work, 19456, 2048)
        states = view(work, 4096, 2, 2, GH, GDV)
        og = view(work, 0, NT, D)
        oT = view(hTs, 2048, KD, SEQ)
        ogT = view(work, 2048, KD, SEQ)
        rows = view(work, 8192, 2, D)
        hT = view(hTs, 0, KD, SEQ)
        act_a = view(work, 6144, 2, 512)
        act_b = view(work, 7168, 2, 512)
        nabias = view(work, 0, NA_H, NT, SEQ)
        qkN = view(work, 4096, 8, SEQ)
        vN = view(work, 6144, NT, NA_H * HD)
        vM = view(work, 7168, NT, MLA_H * HD)
        qM = view(work, 8192, MLA_H, SEQ)
        kM = view(work, 10240, MLA_H, SEQ)
        qtm = view(work, 12288, NT, MLA_H, MQ)
        ctm = view(work, 13824, NT, 416)
        cT = view(work, 14656, 3, SEQ)
        prob = view(work, 15424, 2, 512)
        score = view(work, 16448, 2, 512)
        probT = view(work, 17472, 2, 512)
        om = view(work, 18496, NT, D)
        rt = view(work, 20544, 2, 256)
        kpe = view(hTs, 2048, NT, MQ)
        qkT = view(work, 0, 2, 3, 512)
        vO = view(work, 3072, 2, 3, NT, P)
        qr = view(work, 4608, 2, NT, 256)
        ro = view(work, 5632, 2, 256)
        raw = view(work, 6144, 2, 256)
        frow = view(work, 10240, D)

        na_mask = view(consts, C_NM, NT, SEQ)
        mrope = view(consts, C_MR, NT, 2, ROPE)
        omask = view(consts, C_OM, NT, 512)
        orope = view(consts, C_OR, NT, 2, HD)
        gmask = consts[:, C_GM:C_GM + 2 * P].bitcast(U32).rearrange("p (z i) -> p z i", z=2)

        names = """vecs_loaded consts_loaded x_loaded ctx_loaded small_loaded gate_w_loaded table_copied bias_loaded final_loaded stored
            pool_zeroed zero_ready dve_init vec_ps vec_cols silu_done mod_used mod_cols eff_ready
            std_ready xn_ready xT_ps hT_act hT_dve
            glr_ps glr_ready gate_ps gate_in gate_ln gate_sum exp_b decay_ready d_ready exp_d kd_ready ke_ready
            proj_ps proj_out silu_r gr_ready keT_ps keT_act keT_dve sT_ps sT_ready upd_ps state_ready inter_ps o_ps o_std og_ready
            ogT_ps ogT_act ogT_dve rows_ps rows_ready y_ps y_ss y_sum y_std res_ready
            ff_ps ff_act ff_mid ff_used
            c_ps c_std c_ready cT_ps cT_act cT_dve kpe_ready qk_ps qk_act qk_dve vn_ps vn_act vn_dve
            mk_ps mk_out mv_ps mv_out mq_ps mq_rot mqT_ps mqT_out bias_ready
            s_ps max_ready prob_ready pT_ps pT_ready pv_ps o_out
            od_ps od_raw od_v rot_ready qkT_ps qkT_out out_ready
            w_used out_used act_chain dve_chain pool_chain""".split()
        s = {n: sem(n) for n in names}

        class Load:
            pass

        loads, landed = [], {}

        def plan(key, at, parts, free, ring=None):
            e = Load()
            size = sum(int(np.prod(sh)) for _, sh, _ in parts)
            assert at + size <= POOL, key
            e.at, e.size, e.parts, e.free = at, size, parts, free
            name = ring or f"w_{key}"
            if name not in landed:
                landed[name] = [sem(name), 0]
            landed[name][1] += 16 * len(parts)
            e.sem, e.value = landed[name][0], landed[name][1]
            e.after = {}
            for b in loads:
                if b.at < at + size and at < b.at + b.size:
                    e.after[b.free[0]] = max(b.free[1], e.after.get(b.free[0], 0))
            loads.append(e)
            return e

        def pv(e, i=0):
            off, sh, _ = e.parts[i]
            return view(pool, e.at + off, *sh)

        mod_v = a["mod_w"][0].rearrange("(k p) (s c) -> p k s c", p=P, c=512)
        gin = a["gla_w_in"][0].rearrange("(k p) n -> p k n", p=P)
        gout = a["gla_w_out"][0].rearrange("(k p) n -> p k n", p=P)
        fin = a["ffn_w_in"][0].rearrange("(k p) (g f c) -> p k g f c", p=P, g=2, c=P)
        fout = a["ffn_w_out"][0].rearrange("(f p) n -> p f n", p=P)
        evin = a["ev_w_in_2"][0].rearrange("(k p) n -> p k n", p=P)
        uq = a["ev_w_uq_2"][0].rearrange("(k p) n -> p k n", p=P)
        ukv = a["ev_w_ukv_2"][0].rearrange("(k p) n -> p k n", p=P)
        evo = a["ev_w_o_2"][0].rearrange("(k p) n -> p k n", p=P)
        odin = a["od_w_in_2"][0].rearrange("(k p) (g j m c) -> p k g j m c", p=P, g=3, j=3, c=P)
        odo = a["od_w_o_2"][0].rearrange("(k p) n -> p k n", p=P)
        w1v = a["mlp_w1_2"].rearrange("l (k p) (s c) -> l p k s c", p=P, c=256)
        w2v = a["mlp_w2_2"].rearrange("l (s f p) n -> l p s f n", p=P, f=2)

        W4 = [0, 4096, 8192, 12288]
        L = {}
        n = 0
        for i in range(4):
            L["mod", i] = plan(f"mod{i}", W4[i], [(0, (KD, 512), mod_v[:, :, i, :])], ("mod_used", i + 1), ring=f"w_ring{i}")
        seq = [("k", 2, 512, 256), ("q", 2, 0, 256), ("v", 2, 1024, 512), ("r", 2, 2048, 512)]
        ofs = 16384
        for key, cnt, col, w in seq:
            for i in range(cnt):
                at = {"k": (16384, 0), "q": (2048, 4096), "v": (8192, 12288), "r": (0, 4096)}[key][i]
                L[key, i] = plan(f"gla_{key}{i}", at, [(0, (KD, w), gin[:, :, col + i * w:col + i * w + w])],
                                 ("proj_ps", {"k": 2, "q": 6, "v": 12, "r": 18}[key] + {"k": 2, "q": 2, "v": 4, "r": 2}[key] * i))
        for i in range(4, 12):
            L["mod", i] = plan(f"mod{i}", W4[(i + 2) % 4], [(0, (KD, 512), mod_v[:, :, i, :])], ("mod_used", i + 1),
                               ring=f"w_ring{(i + 2) % 4}")
        for i in range(2):
            L["go", i] = plan(f"gla_out{i}", [8192, 12288][i], [(0, (4, D), gout[:, 4 * i:4 * i + 4, :])], ("out_used", i + 1))
        FB = 3072
        L["ffn"] = []
        for f in range(FFC):
            L["ffn"].append(plan(f"ffn{f % FF_RING}", FB * (f % FF_RING),
                                 [(0, (KD, P), fin[:, :, 0, f, :]), (1024, (KD, P), fin[:, :, 1, f, :]),
                                  (2048, (D,), fout[:, f, :])], ("w_used", f + 1), ring=f"w_ffn{f % FF_RING}"))
        L["c"] = plan("ev_c", 0, [(0, (KD, 416), evin[:, :, 1536:1952])], ("c_ps", 2))
        for i in range(4):
            L["qk", i] = plan(f"ev_qk{i}", 3328 + 2048 * i, [(0, (KD, 256), evin[:, :, 256 * i:256 * i + 256])], ("qk_ps", 2 * i + 2))
        L["va"] = plan("ev_v", 11520, [(0, (KD, 512), evin[:, :, 1024:1536])], ("vn_ps", 2))
        L["ukv"] = plan("ev_ukv", 15616, [(0, (1, 1024), ukv)], ("mv_ps", 2))
        L["uq"] = plan("ev_uq", 16640, [(0, (2, 768), uq)], ("mq_ps", 4))
        for i in range(2):
            L["eo", i] = plan(f"ev_out{i}", [0, 4096][i], [(0, (4, D), evo[:, 4 * i:4 * i + 4, :])], ("out_used", i + 3))

        def plan_mlp(l):
            L["mlp", l] = []
            for st in range(MLP_RING * MLP_LOOPS):
                L["mlp", l].append(plan(f"mlp{l}_{st}", 4096 * (st % MLP_RING),
                                        [(0, (KD, 256), w1v[l][:, :, st, :]), (2048, (2, D), w2v[l][:, st, :, :])],
                                        ("w_used", FFC + 16 * l + st + 1),
                                        ring=f"w_mlp{st % MLP_RING}"))

        plan_mlp(0)
        OB = 9216
        L["od"] = [plan(f"od{m % 2}", OB * (m % 2),
                        [(3072 * g + 1024 * j, (KD, P), odin[:, :, g, j, m, :]) for g in range(3) for j in range(3)],
                        ("od_ps", 6 * m + 6), ring=f"w_od{m % 2}") for m in range(OD_PAIRS)]
        for i in range(2):
            L["oo", i] = plan(f"od_out{i}", [0, 4096][i], [(0, (4, D), odo[:, 4 * i:4 * i + 4, :])], ("out_used", i + 5))
        plan_mlp(1)

        class Chain:
            def __init__(self, eng, count):
                self.eng, self.count, self.base, self.k = eng, count, 0, 0

            def __call__(self, ins):
                ins.then_inc(self.count, 1)
                self.k += 1
                self.eng.wait_ge(self.count, self.base + self.k)

            def enter(self, i, per):
                self.saved, self.per = self.base + self.k, per
                self.base, self.k = self.saved + i * per, 0

            def leave(self, times):
                assert self.k == self.per, self.k
                self.base, self.k = self.saved + times * self.per, 0

        OUT_BANK = ((0, 1), (2, 7))

        def y_done(n):
            return (s["y_ps"], n // 2 + 1) if n % 2 else (s["out_used"], n + 2)

        def chunk_of(z, j):
            return j if z == 0 else (3 - j if j < 4 else 11 - j)

        block = ctx.enter_context(nc.Block())
        NS = 96
        U_OD = NA_H + MLA_H

        @block.sync
        def _(sp):
            def fetch(e):
                for name, value in e.after.items():
                    sp.wait_ge(s[name], value)
                for off, sh, src in e.parts:
                    sp.dma_start(view(pool, e.at + off, *sh), src).then_inc(e.sem, 16)

            def fetch_ring(bundles, ring, parts_of, per=1):
                for e in bundles[:ring]:
                    fetch(e)
                rounds = len(bundles) // ring
                with sp.Fori(0, rounds - 1) as i:
                    for j in range(ring):
                        e = bundles[j]
                        sp.wait_ge(s[e.free[0]], i * (ring * per) + e.free[1])
                        for (off, sh, _), src in zip(e.parts, parts_of(i * ring + (ring + j))):
                            sp.dma_start(view(pool, e.at + off, *sh), src).then_inc(e.sem, 16)
                for e in bundles[rounds * ring:]:
                    fetch(e)

            sp.dma_start(consts[:, :], a["consts"]).then_inc(s["consts_loaded"], 16)
            for i in range(4):
                fetch(L["mod", i])
            for key, cnt, _, _ in seq:
                for i in range(cnt):
                    fetch(L[key, i])
            for i in range(4, 12):
                fetch(L["mod", i])
            for i in range(2):
                fetch(L["go", i])
            fetch_ring(L["ffn"], FF_RING, lambda f: (fin[:, :, 0, f, :], fin[:, :, 1, f, :], fout[:, f, :]))
            for key in ["c", ("qk", 0), ("qk", 1), ("qk", 2), ("qk", 3), "va", "ukv", "uq", ("eo", 0), ("eo", 1)]:
                fetch(L[key])
            fetch_ring(L["mlp", 0], MLP_RING, lambda st: (w1v[0][:, :, st, :], w2v[0][:, st, :, :]))
            fetch_ring(L["od"], 2, lambda m: [odin[:, :, g, j, m, :] for g in range(3) for j in range(3)], per=6)
            fetch(L["oo", 0])
            fetch(L["oo", 1])
            fetch_ring(L["mlp", 1], MLP_RING, lambda st: (w1v[1][:, :, st, :], w2v[1][:, st, :, :]))
            for t in range(NT):
                sp.wait_ge(s["out_ready"], t + 1)
                sp.dma_start(out[0, t * P:t * P + P, :], xn[:, t, :]).then_inc(s["stored"], 16)
            sp.wait_ge(s["stored"], 16 * NT)

        @block.gpsimd
        def _(g):
            g.dma_start(skew, a["ev_rpb_2"].rearrange("o h r c -> o (h r c)").to_broadcast([GRID, RPB])).then_inc(s["table_copied"], 16)
            g.memset(vecA[:, :], 0.0).then_inc(s["pool_zeroed"], 1)
            g.memset(work[0:2 * RANK, 10240:10240 + 2 * GLA_QK], 0.0).then_inc(s["pool_zeroed"], 1)
            g.memset(zero[:, :], 0.0).then_inc(s["zero_ready"], 1)
            g.wait_ge(s["small_loaded"], 32)
            g.wait_ge(s["silu_r"], 4)
            for t in range(NT):
                for h in range(GH):
                    v = rG[:, t, GDV * h:GDV * h + GDV]
                    g.tensor_tensor(v, v, gnrow[:, :], ALU.mult).then_inc(s["gr_ready"], 1)
            g.wait_ge(s["table_copied"], 16)
            g.wait_ge(s["out_used"], 2)
            for t in range(NT):
                for hf in range(2):
                    r = 2 * t + hf
                    for rk in range(4):
                        src = bass.AP(skew.tensor, (rk - r + 7) * 31 + 15, [[RPB - 1, GRID], [15 * 31, NA_H], [1, GRID]])
                        g.dma_start(nabias[GRID * hf:GRID * hf + GRID, :, t, GRID * rk:GRID * rk + GRID], src)\
                         .then_inc(s["bias_loaded"], 16)
            g.wait_ge(s["bias_loaded"], 16 * 16)
            g.wait_ge(s["consts_loaded"], 16)
            for h in range(NA_H):
                g.tensor_tensor(nabias[:, h], nabias[:, h], na_mask, ALU.add).then_inc(s["bias_ready"], 1)
            g.wait_ge(s["o_out"], 4)
            g.dma_start(frow, a["norm_final_2"].partition_broadcast(P)).then_inc(s["final_loaded"], 16)

        @block.scalar
        def _(act):
            chain = Chain(act, s["act_chain"])

            act.wait_ge(s["pool_zeroed"], 2)
            for at, src in [(VA_C, a["c"]), (VA_CC, a["c_ctx"].rearrange("(o n) -> o n", o=1)), (VA_NG, a["norm_g"][0]),
                            (VA_MB, a["mod_b"]), (VA_QN, a["ev_q_norm_2"]), (VA_KN, a["ev_kv_norm_2"]),
                            (VA_BG, a["gla_b_gate"][0])]:
                o, n = src.shape
                act.dma_start(hTs[at:at + o * n // P, 0:P], src.rearrange("o (r p) -> (o r) p", p=P)).then_inc(s["vecs_loaded"], 16)
            for at, src in [(VB_MIX, a["norm_mix_2"]), (VB_MLP, a["norm_mlp_2"])]:
                act.dma_start(hTs[at:at + 16, P:2 * P], src.rearrange("o (r p) -> (o r) p", p=P)).then_inc(s["vecs_loaded"], 16)
            act.dma_start(xn[:, :, :], a["ctx"][0].rearrange("(t p) d -> p t d", p=P)).then_inc(s["ctx_loaded"], 16)
            act.dma_start(res[:, :, :], a["x"][0].rearrange("(t p) d -> p t d", p=P)).then_inc(s["x_loaded"], 16)
            act.dma_start(wglr[:, :, :], gin[:, :, 3072:3104]).then_inc(s["small_loaded"], 16)
            act.dma_start(gnrow[:, :], a["gla_norm_g"][0].partition_broadcast(P)).then_inc(s["small_loaded"], 16)
            for z in range(2):
                act.dma_start(work[z * RANK:(z + 1) * RANK, 10240 + z * GLA_QK:10240 + (z + 1) * GLA_QK],
                              a["gla_w_gate"][0, z]).then_inc(s["gate_w_loaded"], 16)

            act.wait_ge(s["vec_cols"], 1)
            for j in range(2):
                act.activation(silc[:, :, j], vecA[:, 8 * j:8 * j + 8], ACT.Silu).then_inc(s["silu_done"], 1)
            act.wait_ge(s["dve_init"], 1)

            def norm_stats(n, src, ready, count):
                act.wait_ge(ready, count)
                junk = work[:, 0:D] if n < 2 else work[:, 20480:20480 + D]
                for t in range(NT):
                    chain(act.activation(junk, src[:, t, :], ACT.Square, accum_out=stat[:, NS + 6 * n + t:NS + 6 * n + t + 1]))
                act.activation(stat[:, NS + 6 * n + 2:NS + 6 * n + 4], stat[:, NS + 6 * n:NS + 6 * n + 2], ACT.Sqrt, bias=eps, scale=1.0 / D).then_inc(s["std_ready"], 1)

            def norm_evac(n, dst, gain, shift, order=by_sma, ordered=by_sma):
                for b in (0, 2):
                    act.wait_ge(s["xT_ps"], 4 * n + b + 1)
                    for k in (2 * b, 2 * b + 1):
                        src = bank[b][:, 256 * (k - 2 * b):256 * (k - 2 * b) + 256]
                        ins = act.activation(by_sma(dst(k)), order(src), ACT.Identity, scale=gain(k),
                                             bias=shift(k) if shift else 0.0)
                    ins.then_inc(s["hT_act"], 1)

            norm_stats(0, xn, s["ctx_loaded"], 16)
            norm_stats(1, res, s["x_loaded"], 16)
            act.wait_ge(s["eff_ready"], 2)
            norm_evac(0, lambda k: hT_all[:, k, 0:256], lambda k: eff[:, 0, k:k + 1], lambda k: mods[:, k, 1:2])
            norm_evac(1, lambda k: hT_all[:, k, 256:512], lambda k: eff[:, 1, k:k + 1], lambda k: mods[:, k, 0:1])

            for zh in range(8):
                z, h = zh // GH, zh % GH
                act.wait_ge(s["gate_ps"], zh + 1)
                act.activation(G1[:, z, h, :], bank[1 + zh % 4][:, :], ACT.Identity, bias=vecA[:, VA_BG + zh:VA_BG + zh + 1])\
                   .then_inc(s["gate_in"], 1)
            act.wait_ge(s["gate_in"], 8)
            for z in range(2):
                chain(act.activation(G2[:, z], G1[:, z], ACT.Abs))
                chain(act.activation(G2[:, z], G2[:, z], ACT.Exp, scale=-1.0))
                act.activation(G2[:, z], G2[:, z], ACT.Ln, bias=1.0).then_inc(s["gate_ln"], 1)
            for z in range(2):
                act.wait_ge(s["gate_sum"], z + 1)
                act.activation(qd[:, z], G2[:, z, :, 256:512], ACT.Exp, scale=1.0 / GATE_NORM)\
                   .then_inc(s["exp_b"], 1)
                act.activation(kd[:, z], G2[:, z, :, 256:512], ACT.Exp, scale=-1.0 / GATE_NORM).then_inc(s["exp_b"], 1)
                act.activation(decay[:, 32 * z:32 * z + 32], bend[:, 32 * z:32 * z + 32], ACT.Exp, scale=1.0 / GATE_NORM)\
                   .then_inc(s["decay_ready"], 1)
                act.wait_ge(s["d_ready"], z + 1)
                act.activation(G1[:, z], G1[:, z], ACT.Exp, scale=1.0 / GATE_NORM).then_inc(s["exp_d"], 1)
            act.wait_ge(s["gate_sum"], 2)
            for j in range(4):
                act.wait_ge(s["proj_ps"], 17 + j)
                act.activation(rG[:, j % 2, 512 * (j // 2):512 * (j // 2) + 512], bank[5 + (16 + j) % 3][:, :], ACT.Silu)\
                   .then_inc(s["silu_r"], 1)
            for zh in range(1, 8, 2):
                act.wait_ge(s["keT_ps"], zh + 1)
                act.activation(keT[:, zh // GH, zh % GH], bank[zh % 4][:, :].rearrange("p (t d) -> p t d", t=4), ACT.Copy)\
                   .then_inc(s["keT_act"], 1)
            act.wait_ge(s["o_ps"], 1)
            for t in range(NT):
                for h in range(GH):
                    chain(act.activation(work[:, 20480 - 5 * 1024:20480 - 5 * 1024 + GDV],
                                         bank[2 * t + h // 2][:, GDV * (h % 2):GDV * (h % 2) + GDV], ACT.Square,
                                         accum_out=stat[:, 16 + 4 * t + h:17 + 4 * t + h]))
            act.activation(stat[:, 24:32], stat[:, 16:24], ACT.Sqrt, bias=eps, scale=1.0 / GDV).then_inc(s["o_std"], 1)

            def turn_evac(n, dst, order):
                for b in (0, 2):
                    act.wait_ge(s["ogT_ps"], 4 * n + b + 1)
                    for k in (2 * b, 2 * b + 1):
                        ins = act.activation(order(dst[:, k, :]), by_sma(bank[4 + b][:, 256 * (k - 2 * b):256 * (k - 2 * b) + 256]), ACT.Copy)
                    ins.then_inc(s["ogT_act"], 1)

            turn_evac(0, ogT, by_sma)

            def y_stats(n):
                act.wait_ge(*y_done(n))
                for b in range(4):
                    act.activation(xn[:, b // 2, 512 * (b % 2):512 * (b % 2) + 512], bank[b][:, :], ACT.Square, accum_out=stat[:, 32 + b:33 + b])\
                       .then_inc(s["y_ss"], 1)
                act.wait_ge(s["y_sum"], n + 1)
                act.activation(stat[:, 38:40], stat[:, 36:38], ACT.Sqrt, bias=eps, scale=1.0 / D).then_inc(s["y_std"], 1)

            y_stats(0)
            norm_stats(2, res, s["res_ready"], 2)
            act.wait_ge(s["eff_ready"], 5)
            norm_evac(2, lambda k: hT[:, k, :], lambda k: eff[:, 2, k:k + 1], lambda k: mods[:, 3 * KD + k, 0:1])

            def ffn_silu(f, j):
                act.wait_ge(s["ff_ps"], f + 1)
                if not isinstance(f, int) or f >= 2:
                    act.wait_ge(s["ff_mid"], f - 1)
                act.activation(act_a[:, j % 2, 0:256], bank[4 + j % 2][:, 0:256], ACT.Silu).then_inc(s["ff_act"], 1)

            for f in range(FF_RING):
                ffn_silu(f, f)
            with act.Fori(0, FF_LOOPS - 1) as i:
                for j in range(FF_RING):
                    ffn_silu(i * FF_RING + (FF_RING + j), j)
            for f in range(FF_LOOPS * FF_RING, FFC):
                ffn_silu(f, f)
            y_stats(1)

            norm_stats(3, res, s["res_ready"], 4)
            norm_evac(3, lambda k: hT[:, k, :], lambda k: vecB[:, VB_MIX + k:VB_MIX + k + 1], None)
            for t in range(NT):
                act.wait_ge(s["c_ps"], t + 1)
                chain(act.activation(score[:, 0, 0:256], bank[4 + t][:, 0:QR], ACT.Square, accum_out=stat[:, 40 + t:41 + t]))
                chain(act.activation(score[:, 0, 0:128], bank[4 + t][:, QR:QR + KVR], ACT.Square, accum_out=stat[:, 42 + t:43 + t]))
            act.activation(stat[:, 44:46], stat[:, 40:42], ACT.Sqrt, bias=eps, scale=1.0 / QR).then_inc(s["c_std"], 1)
            act.activation(stat[:, 46:48], stat[:, 42:44], ACT.Sqrt, bias=eps, scale=1.0 / KVR).then_inc(s["c_std"], 1)
            for c in range(1, 8, 2):
                act.wait_ge(s["qk_ps"], c + 1)
                act.activation(qkN[:, c, :], bank[7][:, 0:256], ACT.Copy).then_inc(s["qk_act"], 1)
            act.wait_ge(s["vn_ps"], 2)
            act.activation(vN[:, 1, :], bank[7][:, :], ACT.Copy).then_inc(s["vn_act"], 1)
            act.wait_ge(s["cT_ps"], 1)
            for k in range(2):
                act.activation(cT[:, k, :], bank[4][:, 256 * k:256 * k + 256], ACT.Copy,
                               scale=vecA[:, VA_QN + k:VA_QN + k + 1]).then_inc(s["cT_act"], 1)
            for h in range(MLA_H):
                act.wait_ge(s["mk_ps"], h // 2 + 1)
                act.activation(kM[0:NOPE, h, :], bank[4 + h // 2][0:NOPE, 256 * (h % 2):256 * (h % 2) + 256], ACT.Copy)\
                   .then_inc(s["mk_out"], 1)
            for t in range(NT):
                act.wait_ge(s["mv_ps"], t + 1)
                act.activation(vM[:, t, :], bank[4 + t][:, :], ACT.Copy).then_inc(s["mv_out"], 1)

            def exp_unit(u, j, halves, scale, col):
                act.wait_ge(s["max_ready"], u + 1)
                if not isinstance(u, int) or u >= 2:
                    act.wait_ge(s["pT_ps"], u - 1)
                w = 512 // halves
                for h in range(halves):
                    src = score[:, j % 2, h * w:h * w + w] if scale == 1.0 else bank[3 + j % 2][:, h * w:h * w + w]
                    ins = act.activation(prob[:, j % 2, h * w:h * w + w], src, ACT.Exp, scale=scale,
                                         bias=stat[:, 48 + 2 * (j % 4) + h:49 + 2 * (j % 4) + h], accum_out=col(h))
                ins.then_inc(s["prob_ready"], 1)

            def turned_unit(u, j):
                act.wait_ge(s["pT_ps"], u + 1)
                if not isinstance(u, int) or u >= 2:
                    act.wait_ge(s["pv_ps"], u - 1)
                act.activation(probT[:, j % 2, :], bank[5 + j % 2][:, :], ACT.Copy).then_inc(s["pT_ready"], 1)

            for u in range(U_OD + 1):
                if u < U_OD:
                    exp_unit(u, u, 2, 1.0 if u < NA_H else MQ ** -0.5, lambda h: rsum[:, 16 * h + u:16 * h + u + 1])
                if u >= 1:
                    turned_unit(u - 1, u - 1)
            turn_evac(1, oT, by_sma)
            norm_stats(4, res, s["res_ready"], 6)
            norm_evac(4, lambda k: hT[:, k, :], lambda k: vecB[:, VB_MLP + k:VB_MLP + k + 1], None)

            def mlp(l):
                with act.Fori(0, MLP_LOOPS) as i:
                    for j in range(MLP_RING):
                        st = i * MLP_RING + (FFC + 16 * l + j)
                        act.wait_ge(s["ff_ps"], st + 1)
                        act.wait_ge(s["ff_mid"], st - 1)
                        act.activation(act_a[:, j % 2, :], bank[4 + j % 2][:, :], ACT.Relu).then_inc(s["ff_act"], 1)

            mlp(0)

            norm_stats(5, res, s["res_ready"], 8)
            norm_evac(5, lambda k: hT[:, k, :], lambda k: vecB[:, VB_MIX + 8 + k:VB_MIX + 9 + k], None, order=dilated)

            def od_values(m, par, g, t):
                act.wait_ge(s["od_ps"], 6 * m + (2 * g + t + 1))
                if g == 0 and t == 0:
                    act.wait_ge(s["pv_ps"], 4 * m + (U_OD - 4))
                if not isinstance(m, int) or m or g:
                    act.wait_ge(s["rot_ready"], 6 * m + (2 * g + t - 1))
                act.activation(raw[:, t, :], bank[t][:, 0:256], ACT.Copy).then_inc(s["od_raw"], 1)
                act.activation(vO[:, par, g, t, :], bank[t][:, 256:384], ACT.Copy).then_inc(s["od_v"], 1)

            def od_turned(m, par, g):
                act.wait_ge(s["qkT_ps"], 3 * m + (g + 1))
                act.activation(qkT[:, par, g, :], bank[2][:, :], ACT.Copy).then_inc(s["qkT_out"], 1)

            def od_col(par, j):
                return lambda h: rsum[:, 32 + 4 * par + 2 * (j % 2) + j // 2:33 + 4 * par + 2 * (j % 2) + j // 2]

            def od_pair(m, n, pm, pn):
                u = None if n is None else 4 * n + U_OD
                if m is not None:
                    od_values(m, pm, 0, 0)
                    od_values(m, pm, 0, 1)
                if n is not None:
                    od_turned(n, pn, 2)
                if m is not None:
                    od_values(m, pm, 1, 0)
                    od_values(m, pm, 1, 1)
                if n is not None:
                    exp_unit(u + 0, 0, 1, 1.0, od_col(pn, 0))
                    exp_unit(u + 1, 1, 1, 1.0, od_col(pn, 1))
                if m is not None:
                    od_turned(m, pm, 0)
                    od_values(m, pm, 2, 0)
                if n is not None:
                    turned_unit(u + 0, 0)
                    turned_unit(u + 1, 1)
                    exp_unit(u + 2, 2, 1, 1.0, od_col(pn, 2))
                    exp_unit(u + 3, 3, 1, 1.0, od_col(pn, 3))
                if m is not None:
                    od_values(m, pm, 2, 1)
                if n is not None:
                    turned_unit(u + 2, 2)
                    turned_unit(u + 3, 3)
                if m is not None:
                    od_turned(m, pm, 1)

            od_pair(0, None, 0, None)
            with act.Fori(0, OD_PAIRS // 2 - 1) as i:
                od_pair(2 * i + 1, 2 * i, 1, 0)
                od_pair(2 * i + 2, 2 * i + 1, 0, 1)
            od_pair(OD_PAIRS - 1, OD_PAIRS - 2, 1, 0)
            od_pair(None, OD_PAIRS - 1, None, 1)
            turn_evac(2, oT, dilated)
            norm_stats(6, res, s["res_ready"], 10)
            norm_evac(6, lambda k: hT[:, k, :], lambda k: vecB[:, VB_MLP + 8 + k:VB_MLP + 9 + k], None)
            mlp(1)
            norm_stats(7, res, s["res_ready"], 12)

        @block.vector
        def _(dve):
            chain = Chain(dve, s["dve_chain"])
            dve.memset(stat[:, 90:91], EPS).then_inc(s["dve_init"], 1)
            dve.wait_ge(s["vec_ps"], 1)
            dve.wait_ge(s["pool_zeroed"], 1)
            dve.tensor_copy(vecA[:, 0:VA_N], bank[4][:, 0:VA_N]).then_inc(s["vec_cols"], 1)
            dve.wait_ge(s["vec_ps"], 2)
            dve.tensor_copy(vecB[:, :], bank[5][:, 0:VB_N]).then_inc(s["vec_cols"], 1)
            dve.wait_ge(s["vec_cols"], 2)

            def norm_scale(n, src, dst):
                dve.wait_ge(s["std_ready"], n + 1)
                if n > 1:
                    dve.wait_ge(s["xT_ps"], 4 * n)
                chain(dve.reciprocal(stat[:, NS + 6 * n + 4:NS + 6 * n + 6], stat[:, NS + 6 * n + 2:NS + 6 * n + 4]))
                for t in range(NT):
                    dve.tensor_scalar(dst[:, t, :], src[:, t, :], stat[:, NS + 6 * n + 4 + t:NS + 6 * n + 5 + t], None, ALU.mult)\
                       .then_inc(s["xn_ready"], 1)

            def norm_evac(n, dst, gain, shift, order=by_sma):
                for b in (1, 3):
                    dve.wait_ge(s["xT_ps"], 4 * n + b + 1)
                    for k in (2 * b, 2 * b + 1):
                        src = bank[b][:, 256 * (k - 2 * b):256 * (k - 2 * b) + 256]
                        if shift:
                            ins = dve.tensor_scalar(dst(k), src, gain(k), shift(k), ALU.mult, ALU.add)
                        else:
                            ins = dve.tensor_scalar(by_sma(dst(k)), order(src), gain(k), None, ALU.mult)
                    ins.then_inc(s["hT_dve"], 1)

            norm_scale(0, xn, xn)
            norm_scale(1, res, rG)

            def mod_evac(b, lo, hi):
                v = bank[b][:, 2 * lo:2 * hi].rearrange("p (m j) -> p m j", j=2)
                bias = vecA[:, VA_MB + lo:VA_MB + hi].unsqueeze(2).to_broadcast([P, hi - lo, 2])
                ins = dve.tensor_tensor(mods[:, lo:hi, :], v, bias, ALU.add)
                ins.then_inc(s["mod_cols"], 1)

            def eff_scale(i, m, j, g):
                dve.scalar_tensor_tensor(out=eff[:, i, :], in0=mods[:, KD * m:KD * m + KD, j], scalar=1.0,
                                         in1=vecA[:, VA_NG + KD * g:VA_NG + KD * g + KD], op0=ALU.add, op1=ALU.mult)\
                   .then_inc(s["eff_ready"], 1)

            dve.wait_ge(s["mod_used"], 4)
            mod_evac(7, 0, 16)
            dve.wait_ge(s["mod_cols"], 1)
            eff_scale(0, 1, 1, 0)
            eff_scale(1, 1, 0, 0)
            dve.wait_ge(s["eff_ready"], 2)
            norm_evac(0, lambda k: hT_all[:, k, 0:256], lambda k: eff[:, 0, k:k + 1], lambda k: mods[:, k, 1:2])
            norm_evac(1, lambda k: hT_all[:, k, 256:512], lambda k: eff[:, 1, k:k + 1], lambda k: mods[:, k, 0:1])
            dve.wait_ge(s["glr_ps"], 1)
            dve.tensor_copy(glrT, bank[0][0:2 * RANK, :]).then_inc(s["glr_ready"], 1)

            def proj(j):
                dve.wait_ge(s["proj_ps"], j + 1)
                b = bank[5 + j % 3]
                if j < 4:
                    ins = dve.tensor_copy(kT[:, j, :], b[:, :])
                elif j < 8:
                    ins = dve.tensor_scalar(qT[:, j - 4, :], b[:, 0:256], GDK ** -0.5, None, ALU.mult)
                else:
                    half, tile = (j - 8) // 4, (j - 8) % 4
                    ins = dve.tensor_copy(vG[:, tile, 512 * half:512 * half + 512], b[:, :])
                ins.then_inc(s["proj_out"], 1)

            def chunks(v):
                return v.rearrange("p h (c i) -> p (h c) i", i=CHUNK)

            def gates(z):
                dve.wait_ge(s["gate_ln"], z + 1)
                chain(dve.tensor_scalar(G1[:, z], G1[:, z], 0.0, None, ALU.min))
                chain(dve.tensor_tensor(G1[:, z], G1[:, z], G2[:, z], ALU.subtract))
                gin_, gout_ = (G[:, z].rearrange("p h t -> p (h t)") for G in (G1, G2))
                if z:
                    gin_, gout_ = gin_[:, ::-1], gout_[:, ::-1]
                chain(dve.tensor_tensor_scan(gout_, reset, gin_, 0.0, ALU.mult, ALU.add))
                last = 0 if z else CHUNK - 1
                dve.tensor_copy(bend[:, 32 * z:32 * z + 32], chunks(G2[:, z])[:, :, last]).then_inc(s["gate_sum"], 1)
                dve.wait_ge(s["gate_sum"], z + 1)
                dve.tensor_tensor(chunks(G1[:, z]), bend[:, 32 * z:32 * z + 32].unsqueeze(2).to_broadcast([P, 32, CHUNK]),
                                  chunks(G2[:, z]), ALU.subtract).then_inc(s["d_ready"], 1)

            def decayed(z):
                dve.wait_ge(s["exp_b"], 2 * z + 2)
                dve.wait_ge(s["proj_out"], 8)
                dve.tensor_tensor(qd[:, z], qd[:, z], qT, ALU.mult).then_inc(s["kd_ready"], 1)
                dve.tensor_tensor(kd[:, z], kd[:, z], kT[:, :, 256:512], ALU.mult).then_inc(s["kd_ready"], 1)
                dve.wait_ge(s["exp_d"], z + 1)
                dve.tensor_tensor(G1[:, z], G1[:, z], kT, ALU.mult).then_inc(s["ke_ready"], 1)

            for j in range(3):
                proj(j)
            dve.wait_ge(s["xT_ps"], 8)
            chain(dve.memset(reset, 1.0))
            chain(dve.memset(reset[:, ::CHUNK], 0.0))
            gates(0)
            proj(3)
            proj(4)
            gates(1)
            for j in range(5, 10):
                proj(j)
            decayed(0)
            for j in range(10, 12):
                proj(j)
            decayed(1)
            dve.wait_ge(s["ke_ready"], 2)
            dve.wait_ge(s["kd_ready"], 4)
            chain(dve.memset(work[:, 12288:14336], 0.0))
            for j in range(12, 16):
                proj(j)
            dve.wait_ge(s["mod_used"], 12)
            mod_evac(0, 16, 48)
            dve.wait_ge(s["mod_cols"], 2)
            eff_scale(2, 4, 0, 2)
            for i, m, g in ((3, 2, 1), (4, 5, 3)):
                dve.tensor_tensor(eff[:, i, :], mods[:, KD * m:KD * m + KD, 0], vecA[:, VA_NG + KD * g:VA_NG + KD * g + KD],
                                  ALU.mult).then_inc(s["eff_ready"], 1)
            for z in range(2):
                for u in range(2):
                    dve.wait_ge(s["sT_ps"], 2 * z + u + 1)
                    mask = consts[:, C_GM + P * z:C_GM + P * z + P].bitcast(U32).unsqueeze(1).to_broadcast([P, 4, P])
                    dve.copy_predicated(sT[:, z, u], mask, bank[4 + 2 * z + u][:, :].rearrange("p (a i) -> p a i", a=4))\
                       .then_inc(s["sT_ready"], 1)
                for zh in (4 * z, 4 * z + 2):
                    dve.wait_ge(s["keT_ps"], zh + 1)
                    dve.tensor_copy(keT[:, zh // GH, zh % GH], bank[zh % 4][:, :].rearrange("p (t d) -> p t d", t=4))\
                       .then_inc(s["keT_dve"], 1)
            for j in range(7):
                for z in range(2):
                    dve.wait_ge(s["upd_ps"], 2 * j + z + 1)
                    if j == 0 and z == 0:
                        dve.wait_ge(s["decay_ready"], 2)
                    if j >= 5:
                        dve.wait_ge(s["inter_ps"], 2 * (j - 5) + z + 1)
                    if j and z == 0:
                        dve.wait_ge(s["state_ready"], 2 * j)
                    for h in range(GH):
                        upd = bank[4 + 2 * z + h // 2][:, GDV * (h % 2):GDV * (h % 2) + GDV]
                        new = states[:, (j + 1) % 2, z, h, :]
                        if j == 0:
                            ins = dve.tensor_copy(new, upd)
                        else:
                            col = 32 * z + 8 * h + chunk_of(z, j)
                            ins = dve.scalar_tensor_tensor(out=new, in0=states[:, j % 2, z, h, :], scalar=decay[:, col:col + 1],
                                                           in1=upd, op0=ALU.mult, op1=ALU.add)
                    ins.then_inc(s["state_ready"], 1)
            for b in range(4):
                dve.wait_ge(s["rows_ps"], b + 1)
                dve.tensor_copy(rows[:, b // 2, 512 * (b % 2):512 * (b % 2) + 512], bank[4 + b][:, :]).then_inc(s["rows_ready"], 1)
            dve.wait_ge(s["o_std"], 1)
            chain(dve.reciprocal(stat[:, 8:16], stat[:, 24:32]))
            dve.wait_ge(s["gr_ready"], 8)
            for t in range(NT):
                for h in range(GH):
                    ins = dve.scalar_tensor_tensor(out=og[:, t, GDV * h:GDV * h + GDV],
                                                   in0=bank[2 * t + h // 2][:, GDV * (h % 2):GDV * (h % 2) + GDV],
                                                   scalar=stat[:, 8 + 4 * t + h:9 + 4 * t + h],
                                                   in1=rG[:, t, GDV * h:GDV * h + GDV], op0=ALU.mult, op1=ALU.mult)
                ins.then_inc(s["og_ready"], 1)

            def turn_evac(n, dst, order):
                for b in (1, 3):
                    dve.wait_ge(s["ogT_ps"], 4 * n + b + 1)
                    for k in (2 * b, 2 * b + 1):
                        ins = dve.tensor_copy(order(dst[:, k, :]), by_sma(bank[4 + b][:, 256 * (k - 2 * b):256 * (k - 2 * b) + 256]))
                    ins.then_inc(s["ogT_dve"], 1)

            turn_evac(0, ogT, by_sma)

            def gated_update(n):
                dve.wait_ge(s["y_ss"], 4 * n + 4)
                v = stat[:, 32:36].rearrange("p (t h) -> p t h", h=2)
                dve.tensor_tensor(stat[:, 36:38], v[:, :, 0], v[:, :, 1], ALU.add).then_inc(s["y_sum"], 1)
                dve.wait_ge(s["y_std"], n + 1)
                chain(dve.reciprocal(stat[:, 86:88], stat[:, 38:40]))
                if n == 0:
                    dve.wait_ge(s["rows_ready"], 4)
                for b in range(4):
                    t, h = b // 2, b % 2
                    w = dve.scalar_tensor_tensor(out=xn[:, t, 512 * h:512 * h + 512], in0=bank[b][:, :],
                                                 scalar=stat[:, 86 + t:87 + t], in1=rows[:, n, 512 * h:512 * h + 512],
                                                 op0=ALU.mult, op1=ALU.mult)
                    w.then_inc(s["dve_chain"], 1)
                    chain.k += 1
                dve.wait_ge(s["dve_chain"], chain.base + chain.k)
                for t in range(NT):
                    dve.tensor_tensor(res[:, t, :], res[:, t, :], xn[:, t, :], ALU.add).then_inc(s["res_ready"], 1)

            gated_update(0)
            norm_scale(2, res, xn)
            norm_evac(2, lambda k: hT[:, k, :], lambda k: eff[:, 2, k:k + 1], lambda k: mods[:, 3 * KD + k, 0:1])

            def ffn_mul(f, j):
                dve.wait_ge(s["ff_act"], f + 1)
                if not isinstance(f, int) or f >= 2:
                    dve.wait_ge(s["ff_used"], f - 1)
                dve.tensor_tensor(act_b[:, j % 2, 0:256], act_a[:, j % 2, 0:256], bank[4 + j % 2][:, 256:512], ALU.mult)\
                   .then_inc(s["ff_mid"], 1)

            for f in range(FF_RING):
                ffn_mul(f, f)
            with dve.Fori(0, FF_LOOPS - 1) as i:
                for j in range(FF_RING):
                    ffn_mul(i * FF_RING + (FF_RING + j), j)
            for f in range(FF_LOOPS * FF_RING, FFC):
                ffn_mul(f, f)
            gated_update(1)

            norm_scale(3, res, xn)
            norm_evac(3, lambda k: hT[:, k, :], lambda k: vecB[:, VB_MIX + k:VB_MIX + k + 1], None)
            chain(dve.memset(kpe[:, :, 0:NOPE], 0.0))

            def rotate(dst, src, table, heads, w, tmp, last):
                n = heads * w
                a0, b0 = tmp[:, 0, 0:n].rearrange("p (h d) -> p h d", d=w), tmp[:, 1, 0:n]
                cos = table[:, 0, :].unsqueeze(1).to_broadcast([P, heads, w])
                sin = table[:, 1, :].rearrange("p (c d) -> p c d", c=2)
                dve.tensor_tensor(a0, src, cos, ALU.mult).then_inc(s["dve_chain"], 1)
                sw = src.rearrange("p h (c d) -> p h c d", c=2)[:, :, ::-1, :]
                dve.tensor_tensor(b0.rearrange("p (h c d) -> p h c d", c=2, d=w // 2), sw,
                                  sin.unsqueeze(1).to_broadcast([P, heads, 2, w // 2]), ALU.mult).then_inc(s["dve_chain"], 1)
                chain.k += 2
                dve.wait_ge(s["dve_chain"], chain.base + chain.k)
                last(dve.tensor_tensor(dst, a0, b0.rearrange("p (h d) -> p h d", d=w), ALU.add))

            dve.wait_ge(s["c_std"], 2)
            chain(dve.reciprocal(stat[:, 60:64], stat[:, 44:48]))
            for t in range(NT):
                dve.tensor_scalar(ctm[:, t, 0:QR], bank[4 + t][:, 0:QR], stat[:, 60 + t:61 + t], None, ALU.mult)\
                   .then_inc(s["c_ready"], 1)
                dve.tensor_scalar(ctm[:, t, QR:QR + KVR], bank[4 + t][:, QR:QR + KVR], stat[:, 62 + t:63 + t], None, ALU.mult)\
                   .then_inc(s["c_ready"], 1)
                rotate(kpe[:, t:t + 1, NOPE:MQ], bank[4 + t][:, QR + KVR:416].unsqueeze(1), mrope[:, t], 1, ROPE, rt,
                       lambda ins: ins.then_inc(s["kpe_ready"], 1))
                dve.wait_ge(s["kpe_ready"], t + 1)
            for c in range(0, 8, 2):
                dve.wait_ge(s["qk_ps"], c + 1)
                dve.tensor_copy(qkN[:, c, :], bank[6][:, 0:256]).then_inc(s["qk_dve"], 1)
            dve.wait_ge(s["vn_ps"], 1)
            dve.tensor_copy(vN[:, 0, :], bank[6][:, :]).then_inc(s["vn_dve"], 1)
            dve.wait_ge(s["cT_ps"], 2)
            dve.tensor_scalar(cT[:, 2, :], bank[5][:, 0:256], vecA[:, VA_KN:VA_KN + 1], None, ALU.mult).then_inc(s["cT_dve"], 1)
            dve.tensor_copy(kM[NOPE:MQ, :, :], bank[5][NOPE:MQ, 256:512].unsqueeze(1).to_broadcast([ROPE, MLA_H, SEQ]))\
               .then_inc(s["cT_dve"], 1)
            for t in range(NT):
                for hf in range(2):
                    b = 2 * t + hf
                    dve.wait_ge(s["mq_ps"], b + 1)
                    src = bank[b][:, 0:384].rearrange("p (h d) -> p h d", d=MQ)
                    dst = qtm[:, t, 4 * hf:4 * hf + 4, :]
                    dve.tensor_copy(dst[:, :, 0:NOPE], src[:, :, 0:NOPE]).then_inc(s["mq_rot"], 1)
                    rotate(dst[:, :, NOPE:MQ], src[:, :, NOPE:MQ], mrope[:, t], 4, ROPE, rt, lambda ins: ins.then_inc(s["mq_rot"], 1))
                    dve.wait_ge(s["mq_rot"], 2 * b + 2)
            for i in range(4):
                dve.wait_ge(s["mqT_ps"], i + 1)
                dve.tensor_copy(qM[0:MQ, 2 * i:2 * i + 2, :], bank[i][0:MQ, :].rearrange("p (h t) -> p h t", h=2))\
                   .then_inc(s["mqT_out"], 1)

            def neg_max(u, j, src, halves, scale, addend):
                dve.wait_ge(s["s_ps"], u + 1)
                v = bank[3 + j % 2][:, :].rearrange("p (a k) -> p a k", a=halves)
                dst = stat[:, 48 + 2 * (j % 4):48 + 2 * (j % 4) + halves]
                if addend is not None:
                    if not isinstance(u, int) or u >= 2:
                        dve.wait_ge(s["prob_ready"], u - 1)
                    sc = score[:, j % 2, :].rearrange("p (a k) -> p a k", a=halves)
                    chain(dve.scalar_tensor_tensor(out=sc, in0=v, scalar=scale, in1=addend, op0=ALU.mult, op1=ALU.add))
                    dve.tensor_reduce(dst, sc, AX, ALU.max, negate=True).then_inc(s["max_ready"], 1)
                else:
                    chain(dve.tensor_reduce(dst, v, AX, ALU.max, negate=True))
                    dve.tensor_scalar(dst, dst, scale, None, ALU.mult).then_inc(s["max_ready"], 1)

            dve.wait_ge(s["bias_ready"], NA_H)
            for u in range(U_OD):
                if u < NA_H:
                    neg_max(u, u, None, 2, HD ** -0.5, nabias[:, u])
                else:
                    neg_max(u, u, None, 2, MQ ** -0.5, None)
                if u == NA_H + 2 or u == U_OD - 1:
                    k = 0 if u < U_OD - 1 else 1
                    dve.wait_ge(s["pv_ps"], NA_H * (k + 1))
                    r = rsum[:, 0:32].rearrange("p (t h) -> p t h", t=2)[:, :, 8 * k:8 * k + 8]
                    ri = rinv[:, 16 * k:16 * k + 16].rearrange("p (t h) -> p t h", t=2)
                    chain(dve.reciprocal(ri, r))
                    for t in range(NT):
                        dve.tensor_tensor(om[:, t, 512 * k:512 * k + 512].rearrange("p (h d) -> p h d", d=HD),
                                          bank[OUT_BANK[k][t]][:, :].rearrange("p (h d) -> p h d", d=HD),
                                          ri[:, t, :].unsqueeze(2).to_broadcast([P, 8, HD]), ALU.mult).then_inc(s["o_out"], 1)
            turn_evac(1, oT, by_sma)

            def update(n):
                dve.wait_ge(*y_done(n))
                for t in range(NT):
                    for h in range(2):
                        v = res[:, t, 512 * h:512 * h + 512]
                        ins = dve.tensor_tensor(v, v, bank[2 * t + h][:, :], ALU.add)
                    ins.then_inc(s["res_ready"], 1)
                dve.wait_ge(s["res_ready"], 2 * n + 2)

            update(2)
            norm_scale(4, res, xn)
            norm_evac(4, lambda k: hT[:, k, :], lambda k: vecB[:, VB_MLP + k:VB_MLP + k + 1], None)

            def mlp(l):
                with dve.Fori(0, MLP_LOOPS) as i:
                    for j in range(MLP_RING):
                        st = i * MLP_RING + (FFC + 16 * l + j)
                        dve.wait_ge(s["ff_act"], st + 1)
                        dve.wait_ge(s["ff_used"], st - 1)
                        dve.tensor_tensor(act_b[:, j % 2, :], act_a[:, j % 2, :], act_a[:, j % 2, :], ALU.mult)\
                           .then_inc(s["ff_mid"], 1)

            mlp(0)
            update(3)
            norm_scale(5, res, xn)
            norm_evac(5, lambda k: hT[:, k, :], lambda k: vecB[:, VB_MIX + 8 + k:VB_MIX + 9 + k], None, order=dilated)

            def od_rotate(m, par, g, t):
                dve.wait_ge(s["od_raw"], 6 * m + (2 * g + t + 1))
                if not isinstance(m, int) or 3 * m + g >= 2:
                    dve.wait_ge(s["qkT_ps"], 3 * m + (g - 1))
                rotate(qr[:, (3 * par + g) % 2, t, :].rearrange("p (h d) -> p h d", d=HD),
                       raw[:, t, :].rearrange("p (h d) -> p h d", d=HD), orope[:, t], 4, HD, ro,
                       lambda ins: ins.then_inc(s["rot_ready"], 1))
                dve.wait_ge(s["rot_ready"], 6 * m + (2 * g + t + 1))

            def od_max(u, j):
                neg_max(u, j, None, 1, HD ** -0.5, omask[:, j % 2, :].unsqueeze(1))

            om5 = om.rearrange("p t (n h d) -> p t n h d", h=2, d=HD)

            def od_out(n, par):
                dve.wait_ge(s["pv_ps"], 4 * n + (U_OD + 4))
                chain(dve.reciprocal(rinv[:, 32 + 4 * par:36 + 4 * par], rsum[:, 32 + 4 * par:36 + 4 * par]))
                for t in range(NT):
                    ins = dve.tensor_tensor(om5[:, t, n, :, :], bank[7][:, P * t:P * t + P].rearrange("p (h d) -> p h d", d=HD),
                                            rinv[:, 32 + 4 * par + 2 * t:34 + 4 * par + 2 * t].unsqueeze(2).to_broadcast([P, 2, HD]),
                                            ALU.mult)
                ins.then_inc(s["o_out"], 1)

            def od_pair(m, n, pm, pn):
                u = None if n is None else 4 * n + U_OD
                if m is not None:
                    for g, t in ((0, 0), (0, 1), (1, 0), (1, 1)):
                        od_rotate(m, pm, g, t)
                if n is not None:
                    od_max(u + 0, 0)
                    od_max(u + 1, 1)
                if m is not None:
                    od_rotate(m, pm, 2, 0)
                if n is not None:
                    od_max(u + 2, 2)
                    od_max(u + 3, 3)
                if m is not None:
                    od_rotate(m, pm, 2, 1)
                if n is not None:
                    od_out(n, pn)

            od_pair(0, None, 0, None)
            with dve.Fori(0, OD_PAIRS // 2 - 1) as i:
                chain.enter(i, 2 * (6 * 2 + 4 + 1))
                od_pair(2 * i + 1, 2 * i, 1, 0)
                od_pair(2 * i + 2, 2 * i + 1, 0, 1)
            chain.leave(OD_PAIRS // 2 - 1)
            od_pair(OD_PAIRS - 1, OD_PAIRS - 2, 1, 0)
            od_pair(None, OD_PAIRS - 1, None, 1)
            turn_evac(2, oT, dilated)
            update(4)
            norm_scale(6, res, xn)
            norm_evac(6, lambda k: hT[:, k, :], lambda k: vecB[:, VB_MLP + 8 + k:VB_MLP + 9 + k], None)
            mlp(1)
            update(5)
            dve.wait_ge(s["final_loaded"], 16)
            norm_scale(7, res, xn)
            for t in range(NT):
                dve.wait_ge(s["xn_ready"], 15 + t)
                dve.tensor_tensor(xn[:, t, :], xn[:, t, :], frow, ALU.mult).then_inc(s["out_ready"], 1)

        @block.tensor
        def _(pe):
            mm = pe.matmul

            def landed_wait(e):
                pe.wait_ge(e.sem, e.value)

            pe.wait_ge(s["vecs_loaded"], 16 * 9)
            pe.wait_ge(s["consts_loaded"], 16)
            pe.transpose(bank[4][:, 0:VA_N], hTs[0:VA_N, 0:P], ident[0:VA_N, 0:VA_N]).then_inc(s["vec_ps"], 1)
            pe.transpose(bank[5][:, 0:VB_N], hTs[0:VB_N, P:2 * P], ident[0:VB_N, 0:VB_N]).then_inc(s["vec_ps"], 1)

            def mod_slot(i, b):
                e = L["mod", i]
                landed_wait(e)
                w = pv(e)
                for c in range(4):
                    for k in range(KD):
                        ins = mm(bank[b][:, 2 * (4 * i + c):2 * (4 * i + c) + 2], w[:, k, P * c:P * c + P], silc[:, k, :],
                                 start=(k == 0), stop=(k == KD - 1))
                return ins

            pe.wait_ge(s["silu_done"], 2)
            for i in range(4):
                mod_slot(i, 7).then_inc(s["mod_used"], 1)

            def turn_tokens(n, src):
                for t in range(NT):
                    pe.wait_ge(s["xn_ready"], 2 * n + t + 1)
                    if t == 0 and n == 1:
                        pe.wait_ge(s["hT_act"], 2)
                        pe.wait_ge(s["hT_dve"], 2)
                    for b in range(4):
                        for k in (2 * b, 2 * b + 1):
                            ins = pe.transpose(bank[b][:, 256 * (k - 2 * b) + P * t:256 * (k - 2 * b) + P * t + P],
                                               src[:, t, P * k:P * k + P], ident)
                        if t == NT - 1:
                            ins.then_inc(s["xT_ps"], 1)

            def hT_wait(n):
                pe.wait_ge(s["hT_act"], 2 * n + 2)
                pe.wait_ge(s["hT_dve"], 2 * n + 2)

            turn_tokens(0, xn)
            turn_tokens(1, rG)
            hT_wait(1)
            pe.wait_ge(s["small_loaded"], 32)
            for k in range(KD):
                ins = mm(bank[0][0:2 * RANK, :], wglr[:, k, :], hT_all[:, k, :], start=(k == 0), stop=(k == KD - 1))
            ins.then_inc(s["glr_ps"], 1)
            pe.wait_ge(s["glr_ready"], 1)
            pe.wait_ge(s["gate_w_loaded"], 32)
            for zh in range(8):
                if zh >= 4:
                    pe.wait_ge(s["gate_in"], zh - 3)
                mm(bank[1 + zh % 4][:, :], wgate[:, P * zh:P * zh + P], glrT, start=True, stop=True).then_inc(s["gate_ps"], 1)

            for j in range(20):
                if j >= 3 and j < 19:
                    pe.wait_ge(s["proj_out"], j - 2)
                if j == 19:
                    pe.wait_ge(s["silu_r"], 1)
                b = bank[5 + j % 3]
                if j < 8:
                    e = L["k" if j < 4 else "q", (j % 4) // 2]
                    if j % 2 == 0:
                        landed_wait(e)
                    toks = slice(0, 512) if j < 4 else slice(256, 512)
                    for k in range(KD):
                        ins = mm(b[:, 0:toks.stop - toks.start], pv(e)[:, k, P * (j % 2):P * (j % 2) + P], hT_all[:, k, toks],
                                 start=(k == 0), stop=(k == KD - 1))
                    ins.then_inc(s["proj_ps"], 1)
                else:
                    per = 4 if j < 16 else 2
                    jj = j - (8 if j < 16 else 16)
                    e = L["v" if j < 16 else "r", jj // per]
                    if jj % per == 0:
                        landed_wait(e)
                    tok = P * (jj % per) + (0 if j < 16 else 256)
                    for k in range(KD):
                        ins = mm(b[:, :], hT_all[:, k, tok:tok + P], pv(e)[:, k, :], start=(k == 0), stop=(k == KD - 1))
                    ins.then_inc(s["proj_ps"], 1)
            for i in range(4, 12):
                mod_slot(i, 0).then_inc(s["mod_used"], 1)
            pe.wait_ge(s["silu_r"], 4)

            pe.wait_ge(s["kd_ready"], 4)
            pe.wait_ge(s["ke_ready"], 2)
            pe.wait_ge(s["mod_cols"], 2)
            pe.wait_ge(s["proj_out"], 16)
            for z in range(2):
                for u in range(2):
                    for h in range(2):
                        for t in range(NT):
                            ins = mm(bank[4 + 2 * z + u][:, P * (2 * h + t):P * (2 * h + t) + P],
                                     kd[:, z, 2 * u + h, P * t:P * t + P], qd[:, z, 2 * u + h, P * t:P * t + P],
                                     start=True, stop=True)
                    ins.then_inc(s["sT_ps"], 1)
                for h in range(GH):
                    zh = GH * z + h
                    if zh >= 4:
                        pe.wait_ge(s["keT_act"] if zh % 2 else s["keT_dve"], (zh - 4) // 2 + 1)
                    for t in range(4):
                        ins = pe.transpose(bank[zh % 4][:, P * t:P * t + P], G1[:, z, h, P * t:P * t + P], ident)
                    ins.then_inc(s["keT_ps"], 1)
            pe.wait_ge(s["sT_ready"], 4)
            pe.wait_ge(s["keT_act"], 4)
            pe.wait_ge(s["keT_dve"], 4)

            def state_update(j, z):
                if j:
                    pe.wait_ge(s["state_ready"], 2 * (j - 1) + z + 1)
                ch = chunk_of(z, j)
                lo = CHUNK * (ch % 2)
                for h in range(GH):
                    ins = mm(bank[4 + 2 * z + h // 2][:, GDV * (h % 2):GDV * (h % 2) + GDV], keT[lo:lo + CHUNK, z, h, ch // 2, :],
                             vG[lo:lo + CHUNK, ch // 2, GDV * h:GDV * h + GDV], start=True, stop=True)
                ins.then_inc(s["upd_ps"], 1)

            def from_state(j, z):
                pe.wait_ge(s["state_ready"], 2 * j + z + 1)
                cl = j - 3 if z == 0 else 6 - j
                lo = CHUNK * (cl % 2)
                for h in range(GH):
                    ins = mm(bank[2 * (cl // 2) + h // 2][lo:lo + CHUNK, GDV * (h % 2):GDV * (h % 2) + GDV],
                             qd[:, z, h, CHUNK * cl:CHUNK * cl + CHUNK], states[:, (j + 1) % 2, z, h, :],
                             start=False, stop=False, skip_group_check=True)
                ins.then_inc(s["inter_ps"], 1)

            state_update(0, 0)
            state_update(0, 1)
            for t in range(NT):
                for u in range(2):
                    for h in range(2):
                        for z in range(2):
                            mm(bank[2 * t + u][:, GDV * h:GDV * h + GDV], sT[:, z, u, 2 * h + t, :],
                               vG[:, 2 + t, GDV * (2 * u + h):GDV * (2 * u + h) + GDV], start=(h == 0 and z == 0), stop=False,
                               skip_group_check=True)
            for j in range(1, 7):
                for z in range(2):
                    state_update(j, z)
                if j > 3:
                    for z in range(2):
                        from_state(j - 1, z)
            for z in range(2):
                from_state(6, z)
            pe.wait_ge(s["zero_ready"], 1)
            for b in range(4):
                ins = mm(bank[b][:, 0:512], zero[:, 0:P], zero[:, :], start=False, stop=True, skip_group_check=True)
            ins.then_inc(s["o_ps"], 1)
            pe.wait_ge(s["state_ready"], 14)
            pe.wait_ge(s["eff_ready"], 5)
            for b in range(4):
                for k in range(4):
                    kk = 4 * (b % 2) + k
                    ins = mm(bank[4 + b][:, P * k:P * k + P], eff[:, 3 + b // 2, kk:kk + 1].to_broadcast([P, P]), ident,
                             start=True, stop=True)
                ins.then_inc(s["rows_ps"], 1)

            def turn_mixed(n, src):
                for b in range(4):
                    for k in (2 * b, 2 * b + 1):
                        for t in range(NT):
                            ins = pe.transpose(bank[4 + b][:, 256 * (k - 2 * b) + P * t:256 * (k - 2 * b) + P * t + P],
                                               src[:, t, P * k:P * k + P], ident)
                    ins.then_inc(s["ogT_ps"], 1)

            def out_product(n, keys, srcT):
                pe.wait_ge(s["ogT_act"], 2 * n + 2)
                pe.wait_ge(s["ogT_dve"], 2 * n + 2)
                for i, key in enumerate(keys):
                    e = L[key]
                    landed_wait(e)
                    for kk in range(4):
                        k = 4 * i + kk
                        for b in range(4):
                            ins = mm(bank[b][:, :], srcT[:, k, P * (b // 2):P * (b // 2) + P], pv(e)[:, kk, 512 * (b % 2):512 * (b % 2) + 512],
                                     start=(k == 0), stop=(k == KD - 1))
                    ins.then_inc(s["out_used"], 1)

            pe.wait_ge(s["rows_ready"], 4)
            pe.wait_ge(s["og_ready"], 2)
            turn_mixed(0, og)
            out_product(0, [("go", 0), ("go", 1)], ogT)
            turn_tokens(2, xn)
            hT_wait(2)

            def zero_banks():
                for b in range(4):
                    mm(bank[b][:, :], zero[:, 0:P], zero[:, :], start=True, stop=False, skip_group_check=True)

            def close_banks():
                for b in range(4):
                    ins = mm(bank[b][:, :], zero[:, 0:P], zero[:, :], start=False, stop=True, skip_group_check=True)
                ins.then_inc(s["y_ps"], 1)

            zero_banks()

            def ffn_up(f, j, landed_at):
                e = L["ffn"][j]
                pe.wait_ge(e.sem, landed_at)
                if not isinstance(f, int) or f >= 2:
                    pe.wait_ge(s["ff_mid"], f - 1)
                for hf in range(2):
                    for k in range(KD):
                        ins = mm(bank[4 + j % 2][:, 256 * hf:256 * hf + 256], pv(e, hf)[:, k, :], hT[:, k, :],
                                 start=(k == 0), stop=(k == KD - 1))
                ins.then_inc(s["ff_ps"], 1)

            def ffn_down(f, j):
                pe.wait_ge(s["ff_mid"], f + 1)
                e = L["ffn"][j]
                for b in range(4):
                    ins = mm(bank[b][:, :], act_b[:, j % 2, P * (b // 2):P * (b // 2) + P], pv(e, 2)[:, 512 * (b % 2):512 * (b % 2) + 512],
                             start=False, stop=False, skip_group_check=True)
                    if b == 2:
                        ins.then_inc(s["ff_used"], 1)
                ins.then_inc(s["w_used"], 1)

            def ffn_round(f0, n, landed_at):
                for j in range(n):
                    ffn_up(f0 + j, j, landed_at)
                    if j:
                        ffn_down(f0 + (j - 1), j - 1)
                ffn_down(f0 + (n - 1), n - 1)

            step_f = 16 * 3
            ffn_round(0, FF_RING, step_f)
            with pe.Fori(0, FF_LOOPS - 1) as i:
                ffn_round(i * FF_RING + FF_RING, FF_RING, i * step_f + 2 * step_f)
            ffn_round(FF_LOOPS * FF_RING, FFC - FF_LOOPS * FF_RING, (FF_LOOPS + 1) * step_f)
            close_banks()

            turn_tokens(3, xn)
            hT_wait(3)
            e = L["c"]
            landed_wait(e)
            for t in range(NT):
                for k in range(KD):
                    ins = mm(bank[4 + t][:, 0:416], hT[:, k, P * t:P * t + P], pv(e)[:, k, :], start=(k == 0), stop=(k == KD - 1))
                ins.then_inc(s["c_ps"], 1)
            for c in range(8):
                e = L["qk", c // 2]
                if c % 2 == 0:
                    landed_wait(e)
                if c >= 2:
                    pe.wait_ge(s["qk_act"] if c % 2 else s["qk_dve"], c // 2)
                for k in range(KD):
                    ins = mm(bank[6 + c % 2][:, 0:256], pv(e)[:, k, P * (c % 2):P * (c % 2) + P], hT[:, k, :],
                             start=(k == 0), stop=(k == KD - 1))
                ins.then_inc(s["qk_ps"], 1)
            landed_wait(L["va"])
            pe.wait_ge(s["qk_act"], 4)
            pe.wait_ge(s["qk_dve"], 4)
            for t in range(NT):
                for k in range(KD):
                    ins = mm(bank[6 + t][:, :], hT[:, k, P * t:P * t + P], pv(L["va"])[:, k, :], start=(k == 0), stop=(k == KD - 1))
                ins.then_inc(s["vn_ps"], 1)
            pe.wait_ge(s["c_ready"], 4)
            pe.wait_ge(s["kpe_ready"], 2)
            for k in range(3):
                for t in range(NT):
                    ins = pe.transpose(bank[4 + k // 2][:, 256 * (k % 2) + P * t:256 * (k % 2) + P * t + P], ctm[:, t, P * k:P * k + P], ident)
                if k == 1:
                    ins.then_inc(s["cT_ps"], 1)
            for t in range(NT):
                ins = pe.transpose(bank[5][0:MQ, 256 + P * t:256 + P * t + P], kpe[:, t, :], ident)
            ins.then_inc(s["cT_ps"], 1)
            pe.wait_ge(s["cT_act"], 2)
            pe.wait_ge(s["cT_dve"], 2)
            pe.wait_ge(s["vn_act"], 1)
            pe.wait_ge(s["vn_dve"], 1)
            landed_wait(L["ukv"])
            wk = pv(L["ukv"])[:, 0, :].rearrange("p (h c) -> p h c", c=NOPE + HD)
            for h in range(MLA_H):
                ins = mm(bank[4 + h // 2][0:NOPE, 256 * (h % 2):256 * (h % 2) + 256], wk[:, h, 0:NOPE], cT[:, 2, :], start=True, stop=True)
                if h % 2:
                    ins.then_inc(s["mk_ps"], 1)
            landed_wait(L["uq"])
            for t in range(NT):
                for hf in range(2):
                    for k in range(2):
                        ins = mm(bank[2 * t + hf][:, 0:384], cT[:, k, P * t:P * t + P], pv(L["uq"])[:, k, 384 * hf:384 * hf + 384],
                                 start=(k == 0), stop=(k == 1))
                    ins.then_inc(s["mq_ps"], 1)
            pe.wait_ge(s["mk_out"], MLA_H)
            for t in range(NT):
                mm(bank[4 + t][:, :], cT[:, 2, P * t:P * t + P], wk[:, :, NOPE:], start=True, stop=True).then_inc(s["mv_ps"], 1)
            pe.wait_ge(s["mq_rot"], 8)
            for i in range(4):
                for h in (2 * i, 2 * i + 1):
                    for t in range(NT):
                        ins = pe.transpose(bank[i][0:MQ, 256 * (h - 2 * i) + P * t:256 * (h - 2 * i) + P * t + P], qtm[:, t, h, :], ident)
                ins.then_inc(s["mqT_ps"], 1)
            pe.wait_ge(s["mqT_out"], 4)
            pe.wait_ge(s["mv_out"], 2)
            pe.wait_ge(s["cT_dve"], 2)

            def ev_scores(u):
                if u >= 2:
                    pe.wait_ge(s["prob_ready"], u - 1)
                for t in range(NT):
                    if u < NA_H:
                        lo = HD * (u % 2)
                        q, k = qkN[lo:lo + HD, u // 2, P * t:P * t + P], qkN[lo:lo + HD, 4 + u // 2, :]
                    else:
                        q, k = qM[0:MQ, u - NA_H, P * t:P * t + P], kM[0:MQ, u - NA_H, :]
                    ins = mm(bank[3 + u % 2][:, 256 * t:256 * t + 256], q, k, start=True, stop=True)
                ins.then_inc(s["s_ps"], 1)

            def turn_probs(u, j, count):
                pe.wait_ge(s["prob_ready"], count)
                if not isinstance(u, int) or u >= 2:
                    pe.wait_ge(s["pT_ready"], u - 1)
                for b in range(4):
                    ins = pe.transpose(bank[5 + j % 2][:, P * b:P * b + P], prob[:, j % 2, P * b:P * b + P], ident)
                ins.then_inc(s["pT_ps"], 1)

            def ev_values(u):
                pe.wait_ge(s["pT_ready"], u + 1)
                k, h = u // 8, u % 8
                v = vN if k == 0 else vM
                for t in range(NT):
                    for c in range(2):
                        ins = mm(bank[OUT_BANK[k][t]][:, HD * h:HD * h + HD], probT[:, u % 2, P * (2 * t + c):P * (2 * t + c) + P],
                                 v[:, c, HD * h:HD * h + HD], start=(c == 0), stop=(c == 1))
                ins.then_inc(s["pv_ps"], 1)

            for u in range(U_OD + 2):
                if u < U_OD:
                    ev_scores(u)
                if 1 <= u <= U_OD:
                    turn_probs(u - 1, u - 1, u)
                if u >= 2:
                    ev_values(u - 2)
            pe.wait_ge(s["o_out"], 4)
            pe.wait_ge(s["pT_ready"], U_OD)
            turn_mixed(1, om)
            out_product(1, [("eo", 0), ("eo", 1)], oT)

            def mlp(l):
                per = 16 * 2
                first = L["mlp", l]

                def up(st, j, i):
                    e = first[j]
                    pe.wait_ge(e.sem, i * per + e.value)
                    pe.wait_ge(s["ff_mid"], st - 1)
                    for f in range(2):
                        for k in range(KD):
                            ins = mm(bank[4 + j % 2][:, 256 * f:256 * f + 256], pv(e)[:, k, P * f:P * f + P], hT[:, k, :],
                                     start=(k == 0), stop=(k == KD - 1))
                    ins.then_inc(s["ff_ps"], 1)

                def down(st, j):
                    e = first[j]
                    pe.wait_ge(s["ff_mid"], st + 1)
                    for f in range(2):
                        for b in range(4):
                            ins = mm(bank[b][:, :], act_b[:, j % 2, 256 * f + P * (b // 2):256 * f + P * (b // 2) + P],
                                     pv(e, 1)[:, f, 512 * (b % 2):512 * (b % 2) + 512], start=False, stop=False, skip_group_check=True)
                            if f == 1 and b == 2:
                                ins.then_inc(s["ff_used"], 1)
                    ins.then_inc(s["w_used"], 1)

                zero_banks()
                with pe.Fori(0, MLP_LOOPS) as i:
                    st = i * MLP_RING + (FFC + 16 * l)
                    for j in range(MLP_RING):
                        up(st + j, j, i)
                        if j:
                            down(st + (j - 1), j - 1)
                    down(st + (MLP_RING - 1), MLP_RING - 1)
                close_banks()

            turn_tokens(4, xn)
            hT_wait(4)
            mlp(0)

            turn_tokens(5, xn)
            hT_wait(5)

            def od_proj(m, par, g, t, landed_at):
                e = L["od"][par]
                if g == 0 and t == 0:
                    pe.wait_ge(e.sem, landed_at)
                if not isinstance(m, int) or m or g:
                    pe.wait_ge(s["od_v"], 6 * m + (2 * g + t - 1))
                w = pool[:, e.at + 3072 * g:e.at + 3072 * g + 3072].rearrange("p (j k c) -> p k j c", j=3, k=KD)
                for k in range(KD):
                    ins = mm(bank[t][:, 0:384], hT[:, k, P * t:P * t + P], w[:, k], start=(k == 0), stop=(k == KD - 1))
                ins.then_inc(s["od_ps"], 1)

            def od_turn(m, par, g):
                pe.wait_ge(s["rot_ready"], 6 * m + (2 * g + 2))
                if not isinstance(m, int) or m or g:
                    pe.wait_ge(s["qkT_out"], 3 * m + g)
                for j in range(2):
                    for t in range(NT):
                        ins = pe.transpose(bank[2][:, 256 * j + P * t:256 * j + P * t + P],
                                           qr[:, (3 * par + g) % 2, t, P * j:P * j + P], ident)
                ins.then_inc(s["qkT_ps"], 1)

            def od_scores(u, par, j):
                pe.wait_ge(s["prob_ready"], u - 1)
                h, t = j // 2, j % 2
                lo = HD * h
                for g, (at, k0, n) in enumerate([(0, 256, 256), (256, 256 + P * t, P), (384, 256 + P * t, P)]):
                    ins = mm(bank[3 + j % 2][:, at:at + n], qkT[lo:lo + HD, par, g, P * t:P * t + P], qkT[lo:lo + HD, par, g, k0:k0 + n],
                             start=True, stop=True)
                ins.then_inc(s["s_ps"], 1)

            def od_attend(u, par, j, n):
                pe.wait_ge(s["pT_ready"], u + 1)
                if j == 0:
                    pe.wait_ge(s["o_out"], n + 4)
                h, t = j // 2, j % 2
                for b, (g, tile) in enumerate([(0, 0), (0, 1), (1, t), (2, t)]):
                    ins = mm(bank[7][:, P * t + HD * h:P * t + HD * h + HD], probT[:, j % 2, P * b:P * b + P],
                             vO[:, par, g, tile, HD * h:HD * h + HD], start=(b == 0), stop=(b == 3))
                ins.then_inc(s["pv_ps"], 1)

            def od_pair(m, n, pm, pn, landed_at):
                u = None if n is None else 4 * n + U_OD
                if m is not None:
                    od_proj(m, pm, 0, 0, landed_at)
                    od_proj(m, pm, 0, 1, landed_at)
                if n is not None:
                    od_turn(n, pn, 2)
                if m is not None:
                    od_proj(m, pm, 1, 0, landed_at)
                    od_proj(m, pm, 1, 1, landed_at)
                if n is not None:
                    pe.wait_ge(s["qkT_out"], 3 * n + 3)
                    od_scores(u + 0, pn, 0)
                    od_scores(u + 1, pn, 1)
                if m is not None:
                    od_turn(m, pm, 0)
                    od_proj(m, pm, 2, 0, landed_at)
                if n is not None:
                    turn_probs(u + 0, 0, u + 1)
                    turn_probs(u + 1, 1, u + 2)
                    od_scores(u + 2, pn, 2)
                    od_scores(u + 3, pn, 3)
                if m is not None:
                    od_proj(m, pm, 2, 1, landed_at)
                if n is not None:
                    od_attend(u + 0, pn, 0, n)
                    od_attend(u + 1, pn, 1, n)
                    turn_probs(u + 2, 2, u + 3)
                    turn_probs(u + 3, 3, u + 4)
                if m is not None:
                    od_turn(m, pm, 1)
                if n is not None:
                    od_attend(u + 2, pn, 2, n)
                    od_attend(u + 3, pn, 3, n)

            per = 16 * 9
            od_pair(0, None, 0, None, per)
            with pe.Fori(0, OD_PAIRS // 2 - 1) as i:
                od_pair(2 * i + 1, 2 * i, 1, 0, i * per + per)
                od_pair(2 * i + 2, 2 * i + 1, 0, 1, i * per + 2 * per)
            od_pair(OD_PAIRS - 1, OD_PAIRS - 2, 1, 0, OD_PAIRS // 2 * per)
            od_pair(None, OD_PAIRS - 1, None, 1, None)
            pe.wait_ge(s["o_out"], 4 + OD_PAIRS)
            turn_mixed(2, om)
            out_product(2, [("oo", 0), ("oo", 1)], oT)
            turn_tokens(6, xn)
            hT_wait(6)
            mlp(1)


_INS = ['x', 'c', 'ctx', 'c_ctx', 'mod_w', 'mod_b', 'norm_g', 'ffn_w_in', 'ffn_w_out', 'gla_w_in', 'gla_w_gate',
        'gla_b_gate', 'gla_norm_g', 'gla_w_out', 'norm_mix_2', 'norm_mlp_2', 'norm_final_2', 'ev_w_in_2', 'ev_rpb_2',
        'ev_q_norm_2', 'ev_w_uq_2', 'ev_kv_norm_2', 'ev_w_ukv_2', 'ev_w_o_2', 'od_w_in_2', 'od_w_o_2', 'mlp_w1_2',
        'mlp_w2_2']


def kernel(**inputs):
    import numpy as _np
    import concourse.bacc as _bacc
    from concourse import mybir as _mybir
    from concourse.bass_utils import run_bass_kernel_spmd as _run

    nc = _bacc.Bacc("TRN2", target_bir_lowering=False, num_devices=1)
    arrays, args = {}, {}
    for name in _INS:
        v = _np.ascontiguousarray(inputs[name])
        arrays[f"in_{name}_dram"] = v
        args[name] = nc.dram_tensor(f"in_{name}_dram", v.shape, _mybir.dt.from_np(v.dtype), kind="ExternalInput").ap()
    table = constants()
    arrays["in_consts_dram"] = table
    args["consts"] = nc.dram_tensor("in_consts_dram", table.shape, F32, kind="ExternalInput").ap()
    out = nc.dram_tensor("out_0_dram", (1, SEQ, D), F32, kind="ExternalOutput").ap()
    program(nc, args, out)
    r = _run(nc, [arrays], core_ids=[0])
    return r.results[0]["out_0_dram"]
```

```python
from contextlib import ExitStack

import numpy as np

import concourse.bass as bass
from concourse import mybir

ACT = mybir.ActivationFunctionType
ALU = mybir.AluOpType
F32 = mybir.dt.float32
F32R = mybir.dt.float32r
BF16 = mybir.dt.bfloat16
U32 = mybir.dt.uint32
AX = mybir.AxisListType.X

P = 128
SEQ = 256
NT = SEQ // P
D = 1024
KD = D // P
EPS = 1e-6
GRID = 64

GH, GDK, GDV, RANK, CHUNK = 4, 128, 256, 16, 64
GLA_QK, GLA_V = GH * GDK, GH * GDV
GATE_NORM = 16.0
FF = 2816
FFC = FF // P
FF_RING = 6
FF_LOOPS = 3

HD = 64
NA_H, MLA_H, OD_H = 8, 8, 16
NOPE, ROPE, QR, KVR = 64, 32, 256, 128
MQ = NOPE + ROPE
DFF = 4 * D
MLP_RING = 4
MLP_LOOPS = DFF // 256 // MLP_RING
OD_PAIRS = OD_H // 2
RPB = NA_H * 15 * 31
NEG = -1e30

C_ID, C_GM, C_NM, C_MR, C_OM, C_OR = 0, 128, 384, 896, 1024, 2048
C_ALL = 2304
VA_C, VA_CC, VA_NG, VA_MB, VA_QN, VA_KN, VA_BG, VA_N = 0, 8, 16, 48, 96, 98, 99, 107
VB_MIX, VB_MLP, VB_N = 0, 16, 32
POOL = 18432


def constants():
    c = np.zeros((P, C_ALL), np.float32)
    c[:, C_ID:C_ID + P] = np.eye(P)
    j, i = np.meshgrid(np.arange(P), np.arange(P), indexing="ij")
    same = j // CHUNK == i // CHUNK
    c[:, C_GM:C_GM + P] = same & (j <= i)
    c[:, C_GM + P:C_GM + 2 * P] = same & (j >= i)
    tok = np.arange(SEQ)
    start = np.clip(tok % GRID - 8, 0, GRID - 16)
    kc = tok % GRID
    na = np.where((kc[None] >= start[:, None]) & (kc[None] < start[:, None] + 16), 0.0, NEG)
    c[:, C_NM:C_MR] = na.reshape(NT, P, SEQ).transpose(1, 0, 2).reshape(P, -1)

    def rope(pos, dim):
        inv = np.float32(1.0) / (np.float32(10000.0) ** (np.arange(0, dim, 2, dtype=np.float32) / np.float32(dim)))
        ang = pos.astype(np.float32)[:, None] * inv[None]
        co, si = np.cos(ang), np.sin(ang)
        t = np.stack([np.concatenate([co, co], 1), np.concatenate([-si, si], 1)], 1)
        return t.reshape(NT, P, 2 * dim).transpose(1, 0, 2).reshape(P, -1)

    c[:, C_MR:C_OM] = rope(tok, ROPE)
    s, m, a = np.meshgrid(np.arange(4), np.arange(4), np.arange(16), indexing="ij")
    perm = (16 * a + 4 * m + s).reshape(-1)
    dist = perm[None] - perm[:, None]
    wide = np.where(np.abs(dist) <= 64, 0.0, NEG)
    by4 = np.where(dist % 4 == 0, 0.0, NEG)
    by16 = np.where(dist % 16 == 0, 0.0, NEG)
    om = np.zeros((P, NT, 512), np.float32)
    for t in range(NT):
        rows = slice(t * P, t * P + P)
        om[:, t] = np.concatenate([wide[rows], by4[rows, rows], by16[rows, rows]], 1)
    c[:, C_OM:C_OR] = om.reshape(P, -1)
    c[:, C_OR:] = rope(perm, HD)
    return c


def program(nc, a, out):
    with ExitStack() as ctx:
        def sb(name, shape, dt=F32):
            return ctx.enter_context(nc.sbuf_tensor(name, shape, dt))

        def sem(name):
            return ctx.enter_context(nc.semaphore(name))

        bank = [ctx.enter_context(nc.psum_tensor(f"bank{i}", [P, 512], F32)) for i in range(8)]
        areas = {}

        def area(name, words):
            areas[name] = -(-nc.sbuf_base // 32) * 32
            return sb(name, [P, words])

        def over(name, where, at, words):
            return nc.alloc_sbuf_tensor_at(name, [P, words], F32R, offset=areas[where] + 4 * at)

        pool = area("weight_pool", POOL)
        work = area("work", 21504)
        hTs = area("hT", 4096)
        res = sb("residual", [P, NT, D])
        xn = sb("normed", [P, NT, D])
        consts = sb("consts", [P, C_ALL])
        vecA = sb("vecA", [P, P])
        vecB = sb("vecB", [P, VB_N])
        mods = sb("mods", [P, 48, 2])
        eff = sb("eff", [P, 5, KD])
        silc = sb("silc", [P, KD, 2])
        wglr = sb("wglr", [P, KD, 2 * RANK])
        gnrow = sb("gnrow", [P, GDV])
        stat = sb("stat", [P, 192])
        zero = sb("zero", [P, 512], BF16)
        decay = sb("decay", [P, 2 * GH * 8])
        bend = sb("bend", [P, 2 * GH * 8])
        rsum = sb("rsum", [P, 48])
        rinv = sb("rinv", [P, 48])

        skew = nc.dram_tensor("bias_copies", (GRID, RPB), F32).ap()
        ident = consts[:, C_ID:C_ID + P]
        eps = stat[:, 90:91]

        def view(t, at, *dims):
            n = 1
            for d in dims:
                n *= d
            v = t[:, at:at + n]
            if len(dims) == 2:
                return v.rearrange("p (a b) -> p a b", b=dims[1])
            if len(dims) == 3:
                return v.rearrange("p (a b c) -> p a b c", b=dims[1], c=dims[2])
            if len(dims) == 4:
                return v.rearrange("p (a b c d) -> p a b c d", b=dims[1], c=dims[2], d=dims[3])
            return v

        def dilated(v):
            return v.rearrange("p (a m s) -> p s m a", m=4, s=4)

        def by_sma(v):
            return v.rearrange("p (s m a) -> p s m a", m=4, s=4)

        hT_all = view(hTs, 0, KD, 512)
        G1 = view(work, 0, 2, GH, 512)
        G2 = view(work, 4096, 2, GH, 512)
        qd = view(work, 8192, 2, GH, SEQ)
        kd = view(work, 10240, 2, GH, SEQ)
        wgate = work[0:2 * RANK, 10240:10240 + 2 * GLA_QK]
        glrT = work[0:2 * RANK, 10240 + 2 * GLA_QK:10240 + 2 * GLA_QK + 512]
        kT = view(work, 12288, GH, 512)
        sT = view(work, 12288, 2, 2, 4, P)
        qT = view(work, 14336, GH, SEQ)
        vG = view(work, 15360, 4, GLA_V)
        rG = view(work, 19456, NT, D)
        keT = view(hTs, 0, 2, GH, 4, P)
        reset = view(work, 19456, 2048)
        states = view(work, 4096, 2, 2, GH, GDV)
        og = view(work, 0, NT, D)
        oT = view(hTs, 2048, KD, SEQ)
        ogT = view(work, 2048, KD, SEQ)
        rows = view(work, 6144, 2, D)
        hT = view(hTs, 0, KD, SEQ)
        normT = view(work, 16384, KD, SEQ)
        act_a = view(work, 16384, 2, 512)
        act_s = view(work, 19456, 2, 512)
        hT2 = [view(over(f"hT_{w}", "hT", 2048 * i, 2048), 0, KD, SEQ) for i, w in enumerate(("high", "low"))]
        mid2 = [view(over(f"hidden_{w}", "work", 17408 + 1024 * i, 1024), 0, 2, 512) for i, w in enumerate(("high", "low"))]
        ffU = [[over(f"ffn_up{j}_{w}", "work", at + 2048 * i, 2048) for i, w in enumerate(("high", "low"))]
               for j, at in enumerate((10240, 0))]
        ffD = [[over(f"ffn_down{j}_{w}", "work", at + 4096 + 1024 * i, 1024) for i, w in enumerate(("high", "low"))]
               for j, at in enumerate((10240, 0))]
        mlU = [[over(f"mlp_up{j}_{w}", "work", 8192 * j + 2048 * i, 2048) for i, w in enumerate(("high", "low"))] for j in range(2)]
        mlD = [[over(f"mlp_down{j}_{w}", "work", 8192 * j + 4096 + 2048 * i, 2048) for i, w in enumerate(("high", "low"))]
               for j in range(2)]
        odW = [[over(f"od_w{j}_{w}", where, at + 3072 * i, 3072) for i, w in enumerate(("high", "low"))]
               for j, (where, at) in enumerate((("weight_pool", 9216), ("work", 6656)))]
        nabias = view(work, 0, NA_H, NT, SEQ)
        qkN = view(work, 4096, 8, SEQ)
        vN = view(work, 6144, NT, NA_H * HD)
        vM = view(work, 7168, NT, MLA_H * HD)
        qM = view(work, 8192, MLA_H, SEQ)
        kM = view(work, 10240, MLA_H, SEQ)
        qtm = view(work, 12288, NT, MLA_H, MQ)
        ctm = view(work, 13824, NT, 416)
        cT = view(work, 14656, 3, SEQ)
        prob = view(work, 15424, 2, 512)
        score = view(work, 16448, 2, 512)
        probT = view(work, 17472, 2, 512)
        om = view(work, 18496, NT, D)
        rt = view(work, 20544, 2, 256)
        kpe = view(hTs, 2048, NT, MQ)
        qkT = view(work, 0, 2, 3, 512)
        vO = view(work, 3072, 2, 3, NT, P)
        qr = view(work, 4608, 2, NT, 256)
        ro = view(work, 5632, 2, 256)
        raw = view(work, 6144, 2, 256)
        frow = consts[:, C_OM:C_OM + D]

        na_mask = view(consts, C_NM, NT, SEQ)
        mrope = view(consts, C_MR, NT, 2, ROPE)
        omask = view(consts, C_OM, NT, 512)
        orope = view(consts, C_OR, NT, 2, HD)
        gmask = consts[:, C_GM:C_GM + 2 * P].bitcast(U32).rearrange("p (z i) -> p z i", z=2)

        names = """vecs_loaded consts_loaded x_loaded ctx_loaded small_loaded gate_w_loaded table_copied bias_loaded final_loaded stored
            pool_zeroed zero_ready dve_init vec_ps vec_cols silu_done mod_used mod_cols eff_ready
            std_ready xn_ready xT_ps hT_act hT_dve
            glr_ps glr_ready gate_ps gate_in gate_ln gate_sum exp_b decay_ready d_ready exp_d kd_ready ke_ready
            proj_ps proj_out silu_r gr_ready keT_ps keT_act keT_dve sT_ps sT_ready upd_ps state_ready inter_ps o_ps o_std og_ready
            ogT_ps ogT_act ogT_dve rows_ps rows_ready y_ps y_ss y_sum y_std res_ready
            hiU_ready loU_ready hiD_ready loD_ready od_hi od_lo hT_hi hT_lo
            ff_ps ff_act ff_mid
            c_ps c_std c_ready cT_ps cT_act cT_dve kpe_ready qk_ps qk_act qk_dve vn_ps vn_act vn_dve
            mk_ps mk_out mv_ps mv_out mq_ps mq_rot mqT_ps mqT_out bias_ready
            s_ps max_ready prob_ready pT_ps pT_ready pv_ps o_out
            od_ps od_raw od_v rot_ready qkT_ps qkT_out out_ready
            w_used out_used act_chain dve_chain pool_chain""".split()
        s = {n: sem(n) for n in names}

        class Load:
            pass

        loads, landed = [], {}

        def plan(key, at, parts, free, ring=None):
            e = Load()
            size = sum(int(np.prod(sh)) for _, sh, _ in parts)
            assert at + size <= POOL, key
            e.at, e.size, e.parts, e.free = at, size, parts, free
            name = ring or f"w_{key}"
            if name not in landed:
                landed[name] = [sem(name), 0]
            landed[name][1] += 16 * len(parts)
            e.sem, e.value = landed[name][0], landed[name][1]
            e.after = {}
            for b in loads:
                if b.at < at + size and at < b.at + b.size:
                    e.after[b.free[0]] = max(b.free[1], e.after.get(b.free[0], 0))
            loads.append(e)
            return e

        def pv(e, i=0):
            off, sh, _ = e.parts[i]
            return view(pool, e.at + off, *sh)

        mod_v = a["mod_w"][0].rearrange("(k p) (s c) -> p k s c", p=P, c=512)
        gin = a["gla_w_in"][0].rearrange("(k p) n -> p k n", p=P)
        gout = a["gla_w_out"][0].rearrange("(k p) n -> p k n", p=P)
        fin = a["ffn_w_in"][0].rearrange("(k p) (g f c) -> p k g f c", p=P, g=2, c=P)
        fout = a["ffn_w_out"][0].rearrange("(f p) n -> p f n", p=P)
        evin = a["ev_w_in_2"][0].rearrange("(k p) n -> p k n", p=P)
        uq = a["ev_w_uq_2"][0].rearrange("(k p) n -> p k n", p=P)
        ukv = a["ev_w_ukv_2"][0].rearrange("(k p) n -> p k n", p=P)
        evo = a["ev_w_o_2"][0].rearrange("(k p) n -> p k n", p=P)
        odin = a["od_w_in_2"][0].rearrange("(k p) (g j m c) -> p k g j m c", p=P, g=3, j=3, c=P)
        odo = a["od_w_o_2"][0].rearrange("(k p) n -> p k n", p=P)
        w1v = a["mlp_w1_2"].rearrange("l (k p) (s c) -> l p k s c", p=P, c=256)
        w2v = a["mlp_w2_2"].rearrange("l (s f p) n -> l p s f n", p=P, f=2)

        W4 = [0, 4096, 8192, 12288]
        L = {}
        n = 0
        for i in range(4):
            L["mod", i] = plan(f"mod{i}", W4[i], [(0, (KD, 512), mod_v[:, :, i, :])], ("mod_used", i + 1), ring=f"w_ring{i}")
        seq = [("k", 2, 512, 256), ("q", 2, 0, 256), ("v", 2, 1024, 512), ("r", 2, 2048, 512)]
        ofs = 16384
        for key, cnt, col, w in seq:
            for i in range(cnt):
                at = {"k": (16384, 0), "q": (2048, 4096), "v": (8192, 12288), "r": (0, 4096)}[key][i]
                L[key, i] = plan(f"gla_{key}{i}", at, [(0, (KD, w), gin[:, :, col + i * w:col + i * w + w])],
                                 ("proj_ps", {"k": 2, "q": 6, "v": 12, "r": 18}[key] + {"k": 2, "q": 2, "v": 4, "r": 2}[key] * i))
        for i in range(4, 12):
            L["mod", i] = plan(f"mod{i}", W4[(i + 2) % 4], [(0, (KD, 512), mod_v[:, :, i, :])], ("mod_used", i + 1),
                               ring=f"w_ring{(i + 2) % 4}")
        for i in range(2):
            L["go", i] = plan(f"gla_out{i}", [8192, 12288][i], [(0, (4, D), gout[:, 4 * i:4 * i + 4, :])], ("out_used", i + 1))
        FB = 3072
        L["ffn"] = []
        for f in range(FFC):
            L["ffn"].append(plan(f"ffn{f % FF_RING}", FB * (f % FF_RING),
                                 [(0, (KD, P), fin[:, :, 0, f, :]), (1024, (KD, P), fin[:, :, 1, f, :]),
                                  (2048, (D,), fout[:, f, :])], ("loD_ready", f + 1), ring=f"w_ffn{f % FF_RING}"))
        L["c"] = plan("ev_c", 12288, [(0, (KD, 416), evin[:, :, 1536:1952])], ("c_ps", 2))
        for i in range(4):
            L["qk", i] = plan(f"ev_qk{i}", (15616, 0, 2048, 4096)[i], [(0, (KD, 256), evin[:, :, 256 * i:256 * i + 256])], ("qk_ps", 2 * i + 2))
        L["va"] = plan("ev_v", 6144, [(0, (KD, 512), evin[:, :, 1024:1536])], ("vn_ps", 2))
        L["ukv"] = plan("ev_ukv", 10240, [(0, (1, 1024), ukv)], ("mv_ps", 2))
        L["uq"] = plan("ev_uq", 11264, [(0, (2, 768), uq)], ("mq_ps", 4))
        for i in range(2):
            L["eo", i] = plan(f"ev_out{i}", [8192, 12288][i], [(0, (4, D), evo[:, 4 * i:4 * i + 4, :])], ("out_used", i + 3))

        def plan_mlp(l):
            L["mlp", l] = []
            for st in range(MLP_RING * MLP_LOOPS):
                L["mlp", l].append(plan(f"mlp{l}_{st}", 4096 * ((st + 2 * l) % MLP_RING),
                                        [(0, (KD, 256), w1v[l][:, :, st, :]), (2048, (2, D), w2v[l][:, st, :, :])],
                                        ("loD_ready", FFC + 16 * l + st + 1),
                                        ring=f"w_mlp{st % MLP_RING}"))

        plan_mlp(0)
        L["od"] = [plan(f"od{g}", 3072 * g, [(1024 * j, (KD, P), odin[:, :, g, j, m, :]) for j in range(3)],
                        ("od_lo", 3 * m + g + 1), ring=f"w_od{g}") for m in range(OD_PAIRS) for g in range(3)]
        plan("od_split", 9216, [(0, (6144,), None)], ("od_ps", 6 * OD_PAIRS))
        for i in range(2):
            L["oo", i] = plan(f"od_out{i}", [0, 4096][i], [(0, (4, D), odo[:, 4 * i:4 * i + 4, :])], ("out_used", i + 5))
        plan_mlp(1)

        class Chain:
            def __init__(self, eng, count):
                self.eng, self.count, self.base, self.k = eng, count, 0, 0

            def __call__(self, ins):
                ins.then_inc(self.count, 1)
                self.k += 1
                self.eng.wait_ge(self.count, self.base + self.k)

            def enter(self, i, per):
                self.saved, self.per = self.base + self.k, per
                self.base, self.k = self.saved + i * per, 0

            def leave(self, times):
                assert self.k == self.per, self.k
                self.base, self.k = self.saved + times * self.per, 0

        OUT_BANK = ((0, 1), (2, 7))

        def y_done(n):
            return (s["y_ps"], n // 2 + 1) if n % 2 else (s["out_used"], n + 2)

        def chunk_of(z, j):
            return j if z == 0 else (3 - j if j < 4 else 11 - j)

        block = ctx.enter_context(nc.Block())
        NS = 96
        U_OD = NA_H + MLA_H

        @block.sync
        def _(sp):
            def fetch(e):
                for name, value in e.after.items():
                    sp.wait_ge(s[name], value)
                for off, sh, src in e.parts:
                    sp.dma_start(view(pool, e.at + off, *sh), src).then_inc(e.sem, 16)

            def fetch_ring(bundles, ring, parts_of):
                for e in bundles[:ring]:
                    fetch(e)
                rounds = len(bundles) // ring
                with sp.Fori(0, rounds - 1) as i:
                    for j in range(ring):
                        e = bundles[j]
                        sp.wait_ge(s[e.free[0]], i * ring + e.free[1])
                        for (off, sh, _), src in zip(e.parts, parts_of(i + 1, j)):
                            sp.dma_start(view(pool, e.at + off, *sh), src).then_inc(e.sem, 16)
                for e in bundles[rounds * ring:]:
                    fetch(e)

            sp.dma_start(consts[:, :], a["consts"]).then_inc(s["consts_loaded"], 16)
            for i in range(4):
                fetch(L["mod", i])
            for key, cnt, _, _ in seq:
                for i in range(cnt):
                    fetch(L[key, i])
            for i in range(4, 12):
                fetch(L["mod", i])
            for i in range(2):
                fetch(L["go", i])
            fetch_ring(L["ffn"], FF_RING, lambda r, j: (fin[:, :, 0, r * FF_RING + j, :], fin[:, :, 1, r * FF_RING + j, :],
                                                     fout[:, r * FF_RING + j, :]))
            for key in ["c", ("qk", 0), ("qk", 1), ("qk", 2), ("qk", 3), "va", "ukv", "uq", ("eo", 0), ("eo", 1)]:
                fetch(L[key])
            fetch_ring(L["mlp", 0], MLP_RING, lambda r, j: (w1v[0][:, :, r * MLP_RING + j, :], w2v[0][:, r * MLP_RING + j, :, :]))
            fetch_ring(L["od"], 3, lambda m, g: [odin[:, :, g, j, m, :] for j in range(3)])
            fetch(L["oo", 0])
            fetch(L["oo", 1])
            fetch_ring(L["mlp", 1], MLP_RING, lambda r, j: (w1v[1][:, :, r * MLP_RING + j, :], w2v[1][:, r * MLP_RING + j, :, :]))
            for t in range(NT):
                sp.wait_ge(s["out_ready"], t + 1)
                sp.dma_start(out[0, t * P:t * P + P, :], xn[:, t, :]).then_inc(s["stored"], 16)
            sp.wait_ge(s["stored"], 16 * NT)

        @block.gpsimd
        def _(g):
            g.dma_start(skew, a["ev_rpb_2"].rearrange("o h r c -> o (h r c)").to_broadcast([GRID, RPB])).then_inc(s["table_copied"], 16)
            g.memset(vecA[:, :], 0.0).then_inc(s["pool_zeroed"], 1)
            g.memset(work[0:2 * RANK, 10240:10240 + 2 * GLA_QK], 0.0).then_inc(s["pool_zeroed"], 1)
            g.memset(zero[:, :], 0.0).then_inc(s["zero_ready"], 1)
            g.wait_ge(s["small_loaded"], 32)
            g.wait_ge(s["silu_r"], 4)
            for t in range(NT):
                for h in range(GH):
                    v = rG[:, t, GDV * h:GDV * h + GDV]
                    g.tensor_tensor(v, v, gnrow[:, :], ALU.mult).then_inc(s["gr_ready"], 1)
            g.wait_ge(s["table_copied"], 16)
            g.wait_ge(s["y_ps"], 1)
            for t in range(NT):
                for hf in range(2):
                    r = 2 * t + hf
                    for rk in range(4):
                        src = bass.AP(skew.tensor, (rk - r + 7) * 31 + 15, [[RPB - 1, GRID], [15 * 31, NA_H], [1, GRID]])
                        g.dma_start(nabias[GRID * hf:GRID * hf + GRID, :, t, GRID * rk:GRID * rk + GRID], src)\
                         .then_inc(s["bias_loaded"], 16)
            g.wait_ge(s["bias_loaded"], 16 * 16)
            g.wait_ge(s["consts_loaded"], 16)
            for h in range(NA_H):
                g.tensor_tensor(nabias[:, h], nabias[:, h], na_mask, ALU.add).then_inc(s["bias_ready"], 1)
            g.wait_ge(s["o_out"], 4 + OD_PAIRS)
            g.dma_start(frow, a["norm_final_2"].partition_broadcast(P)).then_inc(s["final_loaded"], 16)

        @block.scalar
        def _(act):
            chain = Chain(act, s["act_chain"])

            act.wait_ge(s["pool_zeroed"], 2)
            for at, src in [(VA_C, a["c"]), (VA_CC, a["c_ctx"].rearrange("(o n) -> o n", o=1)), (VA_NG, a["norm_g"][0]),
                            (VA_MB, a["mod_b"]), (VA_QN, a["ev_q_norm_2"]), (VA_KN, a["ev_kv_norm_2"]),
                            (VA_BG, a["gla_b_gate"][0])]:
                o, n = src.shape
                act.dma_start(hTs[at:at + o * n // P, 0:P], src.rearrange("o (r p) -> (o r) p", p=P)).then_inc(s["vecs_loaded"], 16)
            for at, src in [(VB_MIX, a["norm_mix_2"]), (VB_MLP, a["norm_mlp_2"])]:
                act.dma_start(hTs[at:at + 16, P:2 * P], src.rearrange("o (r p) -> (o r) p", p=P)).then_inc(s["vecs_loaded"], 16)
            act.dma_start(xn[:, :, :], a["ctx"][0].rearrange("(t p) d -> p t d", p=P)).then_inc(s["ctx_loaded"], 16)
            act.dma_start(res[:, :, :], a["x"][0].rearrange("(t p) d -> p t d", p=P)).then_inc(s["x_loaded"], 16)
            act.dma_start(wglr[:, :, :], gin[:, :, 3072:3104]).then_inc(s["small_loaded"], 16)
            act.dma_start(gnrow[:, :], a["gla_norm_g"][0].partition_broadcast(P)).then_inc(s["small_loaded"], 16)
            for z in range(2):
                act.dma_start(work[z * RANK:(z + 1) * RANK, 10240 + z * GLA_QK:10240 + (z + 1) * GLA_QK],
                              a["gla_w_gate"][0, z]).then_inc(s["gate_w_loaded"], 16)

            act.wait_ge(s["vec_cols"], 1)
            for j in range(2):
                act.activation(silc[:, :, j], vecA[:, 8 * j:8 * j + 8], ACT.Silu).then_inc(s["silu_done"], 1)
            act.wait_ge(s["dve_init"], 1)

            def norm_stats(n, src, ready, count):
                act.wait_ge(ready, count)
                junk = work[:, 0:D] if n < 2 else work[:, 20480:20480 + D]
                for t in range(NT):
                    chain(act.activation(junk, src[:, t, :], ACT.Square, accum_out=stat[:, NS + 6 * n + t:NS + 6 * n + t + 1]))
                act.activation(stat[:, NS + 6 * n + 2:NS + 6 * n + 4], stat[:, NS + 6 * n:NS + 6 * n + 2], ACT.Sqrt, bias=eps, scale=1.0 / D).then_inc(s["std_ready"], 1)

            def norm_evac(n, dst, gain, shift, order=by_sma, split=False):
                for b in (0, 2):
                    act.wait_ge(s["xT_ps"], 4 * n + b + 1)
                    for k in (2 * b, 2 * b + 1):
                        src = bank[b][:, 256 * (k - 2 * b):256 * (k - 2 * b) + 256]
                        ins = act.activation(by_sma(dst(k)), order(src), ACT.Identity, scale=gain(k),
                                             bias=shift(k) if shift else 0.0)
                    ins.then_inc(s["hT_act"], 1)
                    if split:
                        for k in (2 * b, 2 * b + 1):
                            src = bank[b][:, 256 * (k - 2 * b):256 * (k - 2 * b) + 256]
                            ins = act.activation(by_sma(hT2[0][:, k, :]), order(src), ACT.Identity, scale=gain(k),
                                                 bias=shift(k) if shift else 0.0)
                        ins.then_inc(s["hT_hi"], 1)

            def high(dst, e, off, landed_at, done):
                act.wait_ge(e.sem, landed_at)
                act.activation(dst[:, :], pool[:, e.at + off:e.at + off + dst.shape[1]], ACT.Copy).then_inc(s[done], 1)

            norm_stats(0, xn, s["ctx_loaded"], 16)
            norm_stats(1, res, s["x_loaded"], 16)
            act.wait_ge(s["eff_ready"], 2)
            norm_evac(0, lambda k: hT_all[:, k, 0:256], lambda k: eff[:, 0, k:k + 1], lambda k: mods[:, k, 1:2])
            norm_evac(1, lambda k: hT_all[:, k, 256:512], lambda k: eff[:, 1, k:k + 1], lambda k: mods[:, k, 0:1])

            for zh in range(8):
                z, h = zh // GH, zh % GH
                act.wait_ge(s["gate_ps"], zh + 1)
                act.activation(G1[:, z, h, :], bank[1 + zh % 4][:, :], ACT.Identity, bias=vecA[:, VA_BG + zh:VA_BG + zh + 1])\
                   .then_inc(s["gate_in"], 1)
            act.wait_ge(s["gate_in"], 8)
            for z in range(2):
                chain(act.activation(G2[:, z], G1[:, z], ACT.Abs))
                chain(act.activation(G2[:, z], G2[:, z], ACT.Exp, scale=-1.0))
                act.activation(G2[:, z], G2[:, z], ACT.Ln, bias=1.0).then_inc(s["gate_ln"], 1)
            for z in range(2):
                act.wait_ge(s["gate_sum"], z + 1)
                act.activation(qd[:, z], G2[:, z, :, 256:512], ACT.Exp, scale=1.0 / GATE_NORM)\
                   .then_inc(s["exp_b"], 1)
                act.activation(kd[:, z], G2[:, z, :, 256:512], ACT.Exp, scale=-1.0 / GATE_NORM).then_inc(s["exp_b"], 1)
                act.activation(decay[:, 32 * z:32 * z + 32], bend[:, 32 * z:32 * z + 32], ACT.Exp, scale=1.0 / GATE_NORM)\
                   .then_inc(s["decay_ready"], 1)
                act.wait_ge(s["d_ready"], z + 1)
                act.activation(G1[:, z], G1[:, z], ACT.Exp, scale=1.0 / GATE_NORM).then_inc(s["exp_d"], 1)
            act.wait_ge(s["gate_sum"], 2)
            for j in range(4):
                act.wait_ge(s["proj_ps"], 17 + j)
                act.activation(rG[:, j % 2, 512 * (j // 2):512 * (j // 2) + 512], bank[5 + (16 + j) % 3][:, :], ACT.Silu)\
                   .then_inc(s["silu_r"], 1)
            for zh in range(1, 8, 2):
                act.wait_ge(s["keT_ps"], zh + 1)
                act.activation(keT[:, zh // GH, zh % GH], bank[zh % 4][:, :].rearrange("p (t d) -> p t d", t=4), ACT.Copy)\
                   .then_inc(s["keT_act"], 1)
            act.wait_ge(s["o_ps"], 1)
            for t in range(NT):
                for h in range(GH):
                    chain(act.activation(work[:, 20480 - 5 * 1024:20480 - 5 * 1024 + GDV],
                                         bank[2 * t + h // 2][:, GDV * (h % 2):GDV * (h % 2) + GDV], ACT.Square,
                                         accum_out=stat[:, 16 + 4 * t + h:17 + 4 * t + h]))
            act.activation(stat[:, 24:32], stat[:, 16:24], ACT.Sqrt, bias=eps, scale=1.0 / GDV).then_inc(s["o_std"], 1)

            def turn_evac(n, dst, order):
                for b in (0, 2):
                    act.wait_ge(s["ogT_ps"], 4 * n + b + 1)
                    for k in (2 * b, 2 * b + 1):
                        ins = act.activation(order(dst[:, k, :]), by_sma(bank[4 + b][:, 256 * (k - 2 * b):256 * (k - 2 * b) + 256]), ACT.Copy)
                    ins.then_inc(s["ogT_act"], 1)

            turn_evac(0, ogT, by_sma)
            ffn = L["ffn"]
            act.wait_ge(s["og_ready"], 2)
            high(ffU[0][0], ffn[0], 0, ffn[0].value, "hiU_ready")
            high(ffD[0][0], ffn[0], 2048, ffn[0].value, "hiD_ready")

            def y_stats(n):
                act.wait_ge(*y_done(n))
                for b in range(4):
                    act.activation(xn[:, b // 2, 512 * (b % 2):512 * (b % 2) + 512], bank[b][:, :], ACT.Square, accum_out=stat[:, 32 + b:33 + b])\
                       .then_inc(s["y_ss"], 1)
                act.wait_ge(s["y_sum"], n + 1)
                act.activation(stat[:, 38:40], stat[:, 36:38], ACT.Sqrt, bias=eps, scale=1.0 / D).then_inc(s["y_std"], 1)

            y_stats(0)
            norm_stats(2, res, s["res_ready"], 2)
            act.wait_ge(s["eff_ready"], 5)
            norm_evac(2, lambda k: normT[:, k, :], lambda k: eff[:, 2, k:k + 1], lambda k: mods[:, 3 * KD + k, 0:1], split=True)

            act.wait_ge(s["out_used"], 2)
            high(ffU[1][0], ffn[1], 0, ffn[1].value, "hiU_ready")

            def ffn_step(f, j, n_up, n_down, landed_at):
                act.wait_ge(s["ff_ps"], f + 1)
                if not isinstance(f, int) or f >= 2:
                    act.wait_ge(s["ff_mid"], f - 1)
                act.activation(act_a[:, j % 2, 0:256], bank[4 + j % 2][:, 0:256], ACT.Silu).then_inc(s["ff_act"], 1)
                if n_up:
                    e = ffn[(j + 2) % FF_RING]
                    high(ffU[j % 2][0], e, 0, landed_at + STEP_F * ((j + 2) // FF_RING), "hiU_ready")
                if n_down:
                    if not isinstance(f, int) or f >= 1:
                        act.wait_ge(s["w_used"], f)
                    e = ffn[(j + 1) % FF_RING]
                    high(ffD[(j + 1) % 2][0], e, 2048, landed_at + STEP_F * ((j + 1) // FF_RING), "hiD_ready")

            STEP_F = 16 * 3
            for f in range(FF_RING):
                ffn_step(f, f, True, True, STEP_F)
            with act.Fori(0, FF_LOOPS - 1) as i:
                for j in range(FF_RING):
                    ffn_step(i * FF_RING + (FF_RING + j), j, True, True, i * STEP_F + 2 * STEP_F)
            for f in range(FF_LOOPS * FF_RING, FFC):
                ffn_step(f, f % FF_RING, f + 2 < FFC, f + 1 < FFC, (FF_LOOPS + 1) * STEP_F)
            y_stats(1)

            norm_stats(3, res, s["res_ready"], 4)
            norm_evac(3, lambda k: hT[:, k, :], lambda k: vecB[:, VB_MIX + k:VB_MIX + k + 1], None)
            for t in range(NT):
                act.wait_ge(s["c_ps"], t + 1)
                chain(act.activation(score[:, 0, 0:256], bank[4 + t][:, 0:QR], ACT.Square, accum_out=stat[:, 40 + t:41 + t]))
                chain(act.activation(score[:, 0, 0:128], bank[4 + t][:, QR:QR + KVR], ACT.Square, accum_out=stat[:, 42 + t:43 + t]))
            act.activation(stat[:, 44:46], stat[:, 40:42], ACT.Sqrt, bias=eps, scale=1.0 / QR).then_inc(s["c_std"], 1)
            act.activation(stat[:, 46:48], stat[:, 42:44], ACT.Sqrt, bias=eps, scale=1.0 / KVR).then_inc(s["c_std"], 1)
            for c in range(1, 8, 2):
                act.wait_ge(s["qk_ps"], c + 1)
                act.activation(qkN[:, c, :], bank[7][:, 0:256], ACT.Copy).then_inc(s["qk_act"], 1)
            act.wait_ge(s["vn_ps"], 2)
            act.activation(vN[:, 1, :], bank[7][:, :], ACT.Copy).then_inc(s["vn_act"], 1)
            act.wait_ge(s["cT_ps"], 1)
            for k in range(2):
                act.activation(cT[:, k, :], bank[4][:, 256 * k:256 * k + 256], ACT.Copy,
                               scale=vecA[:, VA_QN + k:VA_QN + k + 1]).then_inc(s["cT_act"], 1)
            for h in range(MLA_H):
                act.wait_ge(s["mk_ps"], h // 2 + 1)
                act.activation(kM[0:NOPE, h, :], bank[4 + h // 2][0:NOPE, 256 * (h % 2):256 * (h % 2) + 256], ACT.Copy)\
                   .then_inc(s["mk_out"], 1)
            for t in range(NT):
                act.wait_ge(s["mv_ps"], t + 1)
                act.activation(vM[:, t, :], bank[4 + t][:, :], ACT.Copy).then_inc(s["mv_out"], 1)

            def exp_unit(u, j, halves, scale, col):
                act.wait_ge(s["max_ready"], u + 1)
                if not isinstance(u, int) or u >= 2:
                    act.wait_ge(s["pT_ps"], u - 1)
                w = 512 // halves
                for h in range(halves):
                    src = score[:, j % 2, h * w:h * w + w] if scale == 1.0 else bank[3 + j % 2][:, h * w:h * w + w]
                    ins = act.activation(prob[:, j % 2, h * w:h * w + w], src, ACT.Exp, scale=scale,
                                         bias=stat[:, 48 + 2 * (j % 4) + h:49 + 2 * (j % 4) + h], accum_out=col(h))
                ins.then_inc(s["prob_ready"], 1)

            def turned_unit(u, j):
                act.wait_ge(s["pT_ps"], u + 1)
                if not isinstance(u, int) or u >= 2:
                    act.wait_ge(s["pv_ps"], u - 1)
                act.activation(probT[:, j % 2, :], bank[5 + j % 2][:, :], ACT.Copy).then_inc(s["pT_ready"], 1)

            for u in range(U_OD + 1):
                if u < U_OD:
                    exp_unit(u, u, 2, 1.0 if u < NA_H else MQ ** -0.5, lambda h: rsum[:, 16 * h + u:16 * h + u + 1])
                if u >= 1:
                    turned_unit(u - 1, u - 1)
            turn_evac(1, oT, by_sma)

            def mlp_first(l):
                e = L["mlp", l]
                high(mlU[0][0], e[0], 0, e[0].value, "hiU_ready")
                high(mlD[0][0], e[0], 2048, e[0].value, "hiD_ready")
                high(mlU[1][0], e[1], 0, e[1].value, "hiU_ready")

            act.wait_ge(s["o_out"], 4)
            mlp_first(0)
            norm_stats(4, res, s["res_ready"], 6)
            norm_evac(4, lambda k: normT[:, k, :], lambda k: vecB[:, VB_MLP + k:VB_MLP + k + 1], None, split=True)

            def mlp(l):
                first, per = L["mlp", l], 16 * 2

                def step(r, j, n_up, n_down):
                    st = r * MLP_RING + (FFC + 16 * l + j)
                    act.wait_ge(s["ff_ps"], st + 1)
                    act.wait_ge(s["ff_mid"], st - 1)
                    act.activation(act_a[:, j % 2, :], bank[4 + j % 2][:, :], ACT.Relu).then_inc(s["ff_act"], 1)
                    if n_up:
                        e = first[(j + 2) % MLP_RING]
                        high(mlU[j % 2][0], e, 0, r * per + (e.value + per * ((j + 2) // MLP_RING)), "hiU_ready")
                    if n_down:
                        act.wait_ge(s["w_used"], st)
                        e = first[(j + 1) % MLP_RING]
                        high(mlD[(j + 1) % 2][0], e, 2048, r * per + (e.value + per * ((j + 1) // MLP_RING)), "hiD_ready")

                with act.Fori(0, MLP_LOOPS - 1) as i:
                    for j in range(MLP_RING):
                        step(i, j, True, True)
                for j in range(MLP_RING):
                    step(MLP_LOOPS - 1, j, j + 2 < MLP_RING, j + 1 < MLP_RING)

            mlp(0)

            def od_high(m, par, g, free):
                act.wait_ge(s[free[0]], free[1])
                high(odW[(3 * par + g) % 2][0], L["od"][g], 0, 48 * m + 48, "od_hi")

            od_high(0, 0, 0, ("loD_ready", FFC + 16))
            norm_stats(5, res, s["res_ready"], 8)
            norm_evac(5, lambda k: normT[:, k, :], lambda k: vecB[:, VB_MIX + 8 + k:VB_MIX + 9 + k], None, order=dilated, split=True)

            def od_values(m, par, g, t):
                act.wait_ge(s["od_ps"], 6 * m + (2 * g + t + 1))
                if g == 0 and t == 0:
                    act.wait_ge(s["pv_ps"], 4 * m + (U_OD - 4))
                if not isinstance(m, int) or m or g:
                    act.wait_ge(s["rot_ready"], 6 * m + (2 * g + t - 1))
                act.activation(raw[:, t, :], bank[t][:, 0:256], ACT.Copy).then_inc(s["od_raw"], 1)
                act.activation(vO[:, par, g, t, :], bank[t][:, 256:384], ACT.Copy).then_inc(s["od_v"], 1)

            def od_turned(m, par, g):
                act.wait_ge(s["qkT_ps"], 3 * m + (g + 1))
                act.activation(qkT[:, par, g, :], bank[2][:, :], ACT.Copy).then_inc(s["qkT_out"], 1)

            def od_col(par, j):
                return lambda h: rsum[:, 32 + 4 * par + 2 * (j % 2) + j // 2:33 + 4 * par + 2 * (j % 2) + j // 2]

            def od_pair(m, n, pm, pn):
                u = None if n is None else 4 * n + U_OD
                if m is not None:
                    od_high(m, pm, 1, ("w_used", FFC + 16) if isinstance(m, int) and m == 0 else ("od_ps", 6 * m))
                    od_values(m, pm, 0, 0)
                    od_values(m, pm, 0, 1)
                if n is not None:
                    od_turned(n, pn, 2)
                if m is not None:
                    od_high(m, pm, 2, ("od_ps", 6 * m + 2))
                    od_values(m, pm, 1, 0)
                    od_values(m, pm, 1, 1)
                if n is not None:
                    exp_unit(u + 0, 0, 1, 1.0, od_col(pn, 0))
                    exp_unit(u + 1, 1, 1, 1.0, od_col(pn, 1))
                if m is not None:
                    od_turned(m, pm, 0)
                    if not isinstance(m, int) or m < OD_PAIRS - 1:
                        od_high(m + 1, 1 - pm, 0, ("od_ps", 6 * m + 4))
                    od_values(m, pm, 2, 0)
                if n is not None:
                    turned_unit(u + 0, 0)
                    turned_unit(u + 1, 1)
                    exp_unit(u + 2, 2, 1, 1.0, od_col(pn, 2))
                    exp_unit(u + 3, 3, 1, 1.0, od_col(pn, 3))
                if m is not None:
                    od_values(m, pm, 2, 1)
                if n is not None:
                    turned_unit(u + 2, 2)
                    turned_unit(u + 3, 3)
                if m is not None:
                    od_turned(m, pm, 1)

            od_pair(0, None, 0, None)
            with act.Fori(0, OD_PAIRS // 2 - 1) as i:
                od_pair(2 * i + 1, 2 * i, 1, 0)
                od_pair(2 * i + 2, 2 * i + 1, 0, 1)
            od_pair(OD_PAIRS - 1, OD_PAIRS - 2, 1, 0)
            od_pair(None, OD_PAIRS - 1, None, 1)
            turn_evac(2, oT, dilated)
            mlp_first(1)
            norm_stats(6, res, s["res_ready"], 10)
            norm_evac(6, lambda k: normT[:, k, :], lambda k: vecB[:, VB_MLP + 8 + k:VB_MLP + 9 + k], None, split=True)
            mlp(1)
            norm_stats(7, res, s["res_ready"], 12)

        @block.vector
        def _(dve):
            chain = Chain(dve, s["dve_chain"])
            dve.memset(stat[:, 90:91], EPS).then_inc(s["dve_init"], 1)
            dve.wait_ge(s["vec_ps"], 1)
            dve.wait_ge(s["pool_zeroed"], 1)
            dve.tensor_copy(vecA[:, 0:VA_N], bank[4][:, 0:VA_N]).then_inc(s["vec_cols"], 1)
            dve.wait_ge(s["vec_ps"], 2)
            dve.tensor_copy(vecB[:, :], bank[5][:, 0:VB_N]).then_inc(s["vec_cols"], 1)
            dve.wait_ge(s["vec_cols"], 2)

            def norm_scale(n, src, dst):
                dve.wait_ge(s["std_ready"], n + 1)
                if n > 1:
                    dve.wait_ge(s["xT_ps"], 4 * n)
                chain(dve.reciprocal(stat[:, NS + 6 * n + 4:NS + 6 * n + 6], stat[:, NS + 6 * n + 2:NS + 6 * n + 4]))
                for t in range(NT):
                    dve.tensor_scalar(dst[:, t, :], src[:, t, :], stat[:, NS + 6 * n + 4 + t:NS + 6 * n + 5 + t], None, ALU.mult)\
                       .then_inc(s["xn_ready"], 1)

            def norm_evac(n, dst, gain, shift, order=by_sma, split=False):
                for b in (1, 3):
                    dve.wait_ge(s["xT_ps"], 4 * n + b + 1)
                    for high in ((False, True) if split else (False,)):
                        for k in (2 * b, 2 * b + 1):
                            src, to = bank[b][:, 256 * (k - 2 * b):256 * (k - 2 * b) + 256], hT2[0][:, k, :] if high else dst(k)
                            if shift:
                                ins = dve.tensor_scalar(to, src, gain(k), shift(k), ALU.mult, ALU.add)
                            else:
                                ins = dve.tensor_scalar(by_sma(to), order(src), gain(k), None, ALU.mult)
                        if not high:
                            ins.then_inc(s["hT_dve"], 1)
                    if split:
                        chain(ins)
                        low(hT2[1][:, 2 * b:2 * b + 2, :], normT[:, 2 * b:2 * b + 2, :], hT2[0][:, 2 * b:2 * b + 2, :], "hT_lo")
                        r = (2, 4, 5, 6).index(n)
                        dve.wait_ge(s["hT_hi"], 2 * r + (b + 1) // 2)
                        low(hT2[1][:, 2 * b - 2:2 * b, :], normT[:, 2 * b - 2:2 * b, :], hT2[0][:, 2 * b - 2:2 * b, :], "hT_lo")

            def low(dst, whole, high, done):
                dve.tensor_tensor(dst, whole, high.bitcast(F32), ALU.subtract).then_inc(s[done], 1)

            def low_weights(pair, e, off, hi, count, done):
                dve.wait_ge(s[hi], count)
                low(pair[1][:, :], pool[:, e.at + off:e.at + off + pair[1].shape[1]], pair[0][:, :], done)

            norm_scale(0, xn, xn)
            norm_scale(1, res, rG)

            def mod_evac(b, lo, hi):
                v = bank[b][:, 2 * lo:2 * hi].rearrange("p (m j) -> p m j", j=2)
                bias = vecA[:, VA_MB + lo:VA_MB + hi].unsqueeze(2).to_broadcast([P, hi - lo, 2])
                ins = dve.tensor_tensor(mods[:, lo:hi, :], v, bias, ALU.add)
                ins.then_inc(s["mod_cols"], 1)

            def eff_scale(i, m, j, g):
                dve.scalar_tensor_tensor(out=eff[:, i, :], in0=mods[:, KD * m:KD * m + KD, j], scalar=1.0,
                                         in1=vecA[:, VA_NG + KD * g:VA_NG + KD * g + KD], op0=ALU.add, op1=ALU.mult)\
                   .then_inc(s["eff_ready"], 1)

            dve.wait_ge(s["mod_used"], 4)
            mod_evac(7, 0, 16)
            dve.wait_ge(s["mod_cols"], 1)
            eff_scale(0, 1, 1, 0)
            eff_scale(1, 1, 0, 0)
            dve.wait_ge(s["eff_ready"], 2)
            norm_evac(0, lambda k: hT_all[:, k, 0:256], lambda k: eff[:, 0, k:k + 1], lambda k: mods[:, k, 1:2])
            norm_evac(1, lambda k: hT_all[:, k, 256:512], lambda k: eff[:, 1, k:k + 1], lambda k: mods[:, k, 0:1])
            dve.wait_ge(s["glr_ps"], 1)
            dve.tensor_copy(glrT, bank[0][0:2 * RANK, :]).then_inc(s["glr_ready"], 1)

            def proj(j):
                dve.wait_ge(s["proj_ps"], j + 1)
                b = bank[5 + j % 3]
                if j < 4:
                    ins = dve.tensor_copy(kT[:, j, :], b[:, :])
                elif j < 8:
                    ins = dve.tensor_scalar(qT[:, j - 4, :], b[:, 0:256], GDK ** -0.5, None, ALU.mult)
                else:
                    half, tile = (j - 8) // 4, (j - 8) % 4
                    ins = dve.tensor_copy(vG[:, tile, 512 * half:512 * half + 512], b[:, :])
                ins.then_inc(s["proj_out"], 1)

            def chunks(v):
                return v.rearrange("p h (c i) -> p (h c) i", i=CHUNK)

            def gates(z):
                dve.wait_ge(s["gate_ln"], z + 1)
                chain(dve.tensor_scalar(G1[:, z], G1[:, z], 0.0, None, ALU.min))
                chain(dve.tensor_tensor(G1[:, z], G1[:, z], G2[:, z], ALU.subtract))
                gin_, gout_ = (G[:, z].rearrange("p h t -> p (h t)") for G in (G1, G2))
                if z:
                    gin_, gout_ = gin_[:, ::-1], gout_[:, ::-1]
                chain(dve.tensor_tensor_scan(gout_, reset, gin_, 0.0, ALU.mult, ALU.add))
                last = 0 if z else CHUNK - 1
                dve.tensor_copy(bend[:, 32 * z:32 * z + 32], chunks(G2[:, z])[:, :, last]).then_inc(s["gate_sum"], 1)
                dve.wait_ge(s["gate_sum"], z + 1)
                dve.tensor_tensor(chunks(G1[:, z]), bend[:, 32 * z:32 * z + 32].unsqueeze(2).to_broadcast([P, 32, CHUNK]),
                                  chunks(G2[:, z]), ALU.subtract).then_inc(s["d_ready"], 1)

            def decayed(z):
                dve.wait_ge(s["exp_b"], 2 * z + 2)
                dve.wait_ge(s["proj_out"], 8)
                dve.tensor_tensor(qd[:, z], qd[:, z], qT, ALU.mult).then_inc(s["kd_ready"], 1)
                dve.tensor_tensor(kd[:, z], kd[:, z], kT[:, :, 256:512], ALU.mult).then_inc(s["kd_ready"], 1)
                dve.wait_ge(s["exp_d"], z + 1)
                dve.tensor_tensor(G1[:, z], G1[:, z], kT, ALU.mult).then_inc(s["ke_ready"], 1)

            for j in range(3):
                proj(j)
            dve.wait_ge(s["xT_ps"], 8)
            chain(dve.memset(reset, 1.0))
            chain(dve.memset(reset[:, ::CHUNK], 0.0))
            gates(0)
            proj(3)
            proj(4)
            gates(1)
            for j in range(5, 10):
                proj(j)
            decayed(0)
            for j in range(10, 12):
                proj(j)
            decayed(1)
            dve.wait_ge(s["ke_ready"], 2)
            dve.wait_ge(s["kd_ready"], 4)
            chain(dve.memset(work[:, 12288:14336], 0.0))
            for j in range(12, 16):
                proj(j)
            dve.wait_ge(s["mod_used"], 12)
            mod_evac(0, 16, 48)
            dve.wait_ge(s["mod_cols"], 2)
            eff_scale(2, 4, 0, 2)
            for i, m, g in ((3, 2, 1), (4, 5, 3)):
                dve.tensor_tensor(eff[:, i, :], mods[:, KD * m:KD * m + KD, 0], vecA[:, VA_NG + KD * g:VA_NG + KD * g + KD],
                                  ALU.mult).then_inc(s["eff_ready"], 1)
            for z in range(2):
                for u in range(2):
                    dve.wait_ge(s["sT_ps"], 2 * z + u + 1)
                    mask = consts[:, C_GM + P * z:C_GM + P * z + P].bitcast(U32).unsqueeze(1).to_broadcast([P, 4, P])
                    dve.copy_predicated(sT[:, z, u], mask, bank[4 + 2 * z + u][:, :].rearrange("p (a i) -> p a i", a=4))\
                       .then_inc(s["sT_ready"], 1)
                for zh in (4 * z, 4 * z + 2):
                    dve.wait_ge(s["keT_ps"], zh + 1)
                    dve.tensor_copy(keT[:, zh // GH, zh % GH], bank[zh % 4][:, :].rearrange("p (t d) -> p t d", t=4))\
                       .then_inc(s["keT_dve"], 1)
            for j in range(7):
                for z in range(2):
                    dve.wait_ge(s["upd_ps"], 2 * j + z + 1)
                    if j == 0 and z == 0:
                        dve.wait_ge(s["decay_ready"], 2)
                    if j >= 5:
                        dve.wait_ge(s["inter_ps"], 2 * (j - 5) + z + 1)
                    if j and z == 0:
                        dve.wait_ge(s["state_ready"], 2 * j)
                    for h in range(GH):
                        upd = bank[4 + 2 * z + h // 2][:, GDV * (h % 2):GDV * (h % 2) + GDV]
                        new = states[:, (j + 1) % 2, z, h, :]
                        if j == 0:
                            ins = dve.tensor_copy(new, upd)
                        else:
                            col = 32 * z + 8 * h + chunk_of(z, j)
                            ins = dve.scalar_tensor_tensor(out=new, in0=states[:, j % 2, z, h, :], scalar=decay[:, col:col + 1],
                                                           in1=upd, op0=ALU.mult, op1=ALU.add)
                    ins.then_inc(s["state_ready"], 1)
            for b in range(4):
                dve.wait_ge(s["rows_ps"], b + 1)
                dve.tensor_copy(rows[:, b // 2, 512 * (b % 2):512 * (b % 2) + 512], bank[4 + b][:, :]).then_inc(s["rows_ready"], 1)
            dve.wait_ge(s["o_std"], 1)
            chain(dve.reciprocal(stat[:, 8:16], stat[:, 24:32]))
            dve.wait_ge(s["gr_ready"], 8)
            for t in range(NT):
                for h in range(GH):
                    ins = dve.scalar_tensor_tensor(out=og[:, t, GDV * h:GDV * h + GDV],
                                                   in0=bank[2 * t + h // 2][:, GDV * (h % 2):GDV * (h % 2) + GDV],
                                                   scalar=stat[:, 8 + 4 * t + h:9 + 4 * t + h],
                                                   in1=rG[:, t, GDV * h:GDV * h + GDV], op0=ALU.mult, op1=ALU.mult)
                ins.then_inc(s["og_ready"], 1)

            def turn_evac(n, dst, order):
                for b in (1, 3):
                    dve.wait_ge(s["ogT_ps"], 4 * n + b + 1)
                    for k in (2 * b, 2 * b + 1):
                        ins = dve.tensor_copy(order(dst[:, k, :]), by_sma(bank[4 + b][:, 256 * (k - 2 * b):256 * (k - 2 * b) + 256]))
                    ins.then_inc(s["ogT_dve"], 1)

            turn_evac(0, ogT, by_sma)
            ffn = L["ffn"]
            low_weights(ffU[0], ffn[0], 0, "hiU_ready", 1, "loU_ready")
            low_weights(ffD[0], ffn[0], 2048, "hiD_ready", 1, "loD_ready")

            def gated_update(n):
                dve.wait_ge(s["y_ss"], 4 * n + 4)
                v = stat[:, 32:36].rearrange("p (t h) -> p t h", h=2)
                dve.tensor_tensor(stat[:, 36:38], v[:, :, 0], v[:, :, 1], ALU.add).then_inc(s["y_sum"], 1)
                dve.wait_ge(s["y_std"], n + 1)
                chain(dve.reciprocal(stat[:, 86:88], stat[:, 38:40]))
                if n == 0:
                    dve.wait_ge(s["rows_ready"], 4)
                for b in range(4):
                    t, h = b // 2, b % 2
                    w = dve.scalar_tensor_tensor(out=xn[:, t, 512 * h:512 * h + 512], in0=bank[b][:, :],
                                                 scalar=stat[:, 86 + t:87 + t], in1=rows[:, n, 512 * h:512 * h + 512],
                                                 op0=ALU.mult, op1=ALU.mult)
                    w.then_inc(s["dve_chain"], 1)
                    chain.k += 1
                dve.wait_ge(s["dve_chain"], chain.base + chain.k)
                for t in range(NT):
                    dve.tensor_tensor(res[:, t, :], res[:, t, :], xn[:, t, :], ALU.add).then_inc(s["res_ready"], 1)

            gated_update(0)
            norm_scale(2, res, xn)
            norm_evac(2, lambda k: normT[:, k, :], lambda k: eff[:, 2, k:k + 1], lambda k: mods[:, 3 * KD + k, 0:1], split=True)

            low_weights(ffU[1], ffn[1], 0, "hiU_ready", 2, "loU_ready")

            def split_hidden(j, n, product):
                whole, hi, lo = act_s[:, j % 2, 0:n], mid2[0][:, j % 2, 0:n], mid2[1][:, j % 2, 0:n]
                chain(dve.tensor_tensor(whole, *product, ALU.mult))
                chain(dve.tensor_copy(hi, whole))
                low(lo, whole, hi, "ff_mid")

            def ffn_step(f, j, n_up, n_down):
                dve.wait_ge(s["ff_act"], f + 1)
                if not isinstance(f, int) or f >= 2:
                    dve.wait_ge(s["w_used"], f - 1)
                split_hidden(j, 256, (act_a[:, j % 2, 0:256], bank[4 + j % 2][:, 256:512]))
                if n_up:
                    low_weights(ffU[j % 2], ffn[(j + 2) % FF_RING], 0, "hiU_ready", f + 3, "loU_ready")
                if n_down:
                    low_weights(ffD[(j + 1) % 2], ffn[(j + 1) % FF_RING], 2048, "hiD_ready", f + 2, "loD_ready")

            for f in range(FF_RING):
                ffn_step(f, f, True, True)
            with dve.Fori(0, FF_LOOPS - 1) as i:
                chain.enter(i, 2 * FF_RING)
                for j in range(FF_RING):
                    ffn_step(i * FF_RING + (FF_RING + j), j, True, True)
            chain.leave(FF_LOOPS - 1)
            for f in range(FF_LOOPS * FF_RING, FFC):
                ffn_step(f, f % FF_RING, f + 2 < FFC, f + 1 < FFC)
            gated_update(1)

            norm_scale(3, res, xn)
            norm_evac(3, lambda k: hT[:, k, :], lambda k: vecB[:, VB_MIX + k:VB_MIX + k + 1], None)
            chain(dve.memset(kpe[:, :, 0:NOPE], 0.0))

            def rotate(dst, src, table, heads, w, tmp, last):
                n = heads * w
                a0, b0 = tmp[:, 0, 0:n].rearrange("p (h d) -> p h d", d=w), tmp[:, 1, 0:n]
                cos = table[:, 0, :].unsqueeze(1).to_broadcast([P, heads, w])
                sin = table[:, 1, :].rearrange("p (c d) -> p c d", c=2)
                dve.tensor_tensor(a0, src, cos, ALU.mult).then_inc(s["dve_chain"], 1)
                sw = src.rearrange("p h (c d) -> p h c d", c=2)[:, :, ::-1, :]
                dve.tensor_tensor(b0.rearrange("p (h c d) -> p h c d", c=2, d=w // 2), sw,
                                  sin.unsqueeze(1).to_broadcast([P, heads, 2, w // 2]), ALU.mult).then_inc(s["dve_chain"], 1)
                chain.k += 2
                dve.wait_ge(s["dve_chain"], chain.base + chain.k)
                last(dve.tensor_tensor(dst, a0, b0.rearrange("p (h d) -> p h d", d=w), ALU.add))

            dve.wait_ge(s["c_std"], 2)
            chain(dve.reciprocal(stat[:, 60:64], stat[:, 44:48]))
            for t in range(NT):
                dve.tensor_scalar(ctm[:, t, 0:QR], bank[4 + t][:, 0:QR], stat[:, 60 + t:61 + t], None, ALU.mult)\
                   .then_inc(s["c_ready"], 1)
                dve.tensor_scalar(ctm[:, t, QR:QR + KVR], bank[4 + t][:, QR:QR + KVR], stat[:, 62 + t:63 + t], None, ALU.mult)\
                   .then_inc(s["c_ready"], 1)
                rotate(kpe[:, t:t + 1, NOPE:MQ], bank[4 + t][:, QR + KVR:416].unsqueeze(1), mrope[:, t], 1, ROPE, rt,
                       lambda ins: ins.then_inc(s["kpe_ready"], 1))
                dve.wait_ge(s["kpe_ready"], t + 1)
            for c in range(0, 8, 2):
                dve.wait_ge(s["qk_ps"], c + 1)
                dve.tensor_copy(qkN[:, c, :], bank[6][:, 0:256]).then_inc(s["qk_dve"], 1)
            dve.wait_ge(s["vn_ps"], 1)
            dve.tensor_copy(vN[:, 0, :], bank[6][:, :]).then_inc(s["vn_dve"], 1)
            dve.wait_ge(s["cT_ps"], 2)
            dve.tensor_scalar(cT[:, 2, :], bank[5][:, 0:256], vecA[:, VA_KN:VA_KN + 1], None, ALU.mult).then_inc(s["cT_dve"], 1)
            dve.tensor_copy(kM[NOPE:MQ, :, :], bank[5][NOPE:MQ, 256:512].unsqueeze(1).to_broadcast([ROPE, MLA_H, SEQ]))\
               .then_inc(s["cT_dve"], 1)
            for t in range(NT):
                for hf in range(2):
                    b = 2 * t + hf
                    dve.wait_ge(s["mq_ps"], b + 1)
                    src = bank[b][:, 0:384].rearrange("p (h d) -> p h d", d=MQ)
                    dst = qtm[:, t, 4 * hf:4 * hf + 4, :]
                    dve.tensor_copy(dst[:, :, 0:NOPE], src[:, :, 0:NOPE]).then_inc(s["mq_rot"], 1)
                    rotate(dst[:, :, NOPE:MQ], src[:, :, NOPE:MQ], mrope[:, t], 4, ROPE, rt, lambda ins: ins.then_inc(s["mq_rot"], 1))
                    dve.wait_ge(s["mq_rot"], 2 * b + 2)
            for i in range(4):
                dve.wait_ge(s["mqT_ps"], i + 1)
                dve.tensor_copy(qM[0:MQ, 2 * i:2 * i + 2, :], bank[i][0:MQ, :].rearrange("p (h t) -> p h t", h=2))\
                   .then_inc(s["mqT_out"], 1)

            def neg_max(u, j, src, halves, scale, addend):
                dve.wait_ge(s["s_ps"], u + 1)
                v = bank[3 + j % 2][:, :].rearrange("p (a k) -> p a k", a=halves)
                dst = stat[:, 48 + 2 * (j % 4):48 + 2 * (j % 4) + halves]
                if addend is not None:
                    if not isinstance(u, int) or u >= 2:
                        dve.wait_ge(s["prob_ready"], u - 1)
                    sc = score[:, j % 2, :].rearrange("p (a k) -> p a k", a=halves)
                    chain(dve.scalar_tensor_tensor(out=sc, in0=v, scalar=scale, in1=addend, op0=ALU.mult, op1=ALU.add))
                    dve.tensor_reduce(dst, sc, AX, ALU.max, negate=True).then_inc(s["max_ready"], 1)
                else:
                    chain(dve.tensor_reduce(dst, v, AX, ALU.max, negate=True))
                    dve.tensor_scalar(dst, dst, scale, None, ALU.mult).then_inc(s["max_ready"], 1)

            dve.wait_ge(s["bias_ready"], NA_H)
            for u in range(U_OD):
                if u < NA_H:
                    neg_max(u, u, None, 2, HD ** -0.5, nabias[:, u])
                else:
                    neg_max(u, u, None, 2, MQ ** -0.5, None)
                if u == NA_H + 2 or u == U_OD - 1:
                    k = 0 if u < U_OD - 1 else 1
                    dve.wait_ge(s["pv_ps"], NA_H * (k + 1))
                    r = rsum[:, 0:32].rearrange("p (t h) -> p t h", t=2)[:, :, 8 * k:8 * k + 8]
                    ri = rinv[:, 16 * k:16 * k + 16].rearrange("p (t h) -> p t h", t=2)
                    chain(dve.reciprocal(ri, r))
                    for t in range(NT):
                        dve.tensor_tensor(om[:, t, 512 * k:512 * k + 512].rearrange("p (h d) -> p h d", d=HD),
                                          bank[OUT_BANK[k][t]][:, :].rearrange("p (h d) -> p h d", d=HD),
                                          ri[:, t, :].unsqueeze(2).to_broadcast([P, 8, HD]), ALU.mult).then_inc(s["o_out"], 1)
            turn_evac(1, oT, by_sma)

            def update(n):
                dve.wait_ge(*y_done(n))
                for t in range(NT):
                    for h in range(2):
                        v = res[:, t, 512 * h:512 * h + 512]
                        ins = dve.tensor_tensor(v, v, bank[2 * t + h][:, :], ALU.add)
                    ins.then_inc(s["res_ready"], 1)
                dve.wait_ge(s["res_ready"], 2 * n + 2)

            def mlp_first(l):
                e, n = L["mlp", l], FFC + 16 * l
                low_weights(mlU[0], e[0], 0, "hiU_ready", n + 1, "loU_ready")
                low_weights(mlD[0], e[0], 2048, "hiD_ready", n + 1, "loD_ready")
                low_weights(mlU[1], e[1], 0, "hiU_ready", n + 2, "loU_ready")

            mlp_first(0)
            update(2)
            norm_scale(4, res, xn)
            norm_evac(4, lambda k: normT[:, k, :], lambda k: vecB[:, VB_MLP + k:VB_MLP + k + 1], None, split=True)

            def mlp(l):
                first = L["mlp", l]

                def step(r, j, n_up, n_down):
                    st = r * MLP_RING + (FFC + 16 * l + j)
                    dve.wait_ge(s["ff_act"], st + 1)
                    dve.wait_ge(s["w_used"], st - 1)
                    split_hidden(j, 512, (act_a[:, j % 2, :], act_a[:, j % 2, :]))
                    if n_up:
                        low_weights(mlU[j % 2], first[(j + 2) % MLP_RING], 0, "hiU_ready", st + 3, "loU_ready")
                    if n_down:
                        low_weights(mlD[(j + 1) % 2], first[(j + 1) % MLP_RING], 2048, "hiD_ready", st + 2, "loD_ready")

                with dve.Fori(0, MLP_LOOPS - 1) as i:
                    chain.enter(i, 2 * MLP_RING)
                    for j in range(MLP_RING):
                        step(i, j, True, True)
                chain.leave(MLP_LOOPS - 1)
                for j in range(MLP_RING):
                    step(MLP_LOOPS - 1, j, j + 2 < MLP_RING, j + 1 < MLP_RING)

            mlp(0)

            def od_low(m, par, g):
                low_weights(odW[(3 * par + g) % 2], L["od"][g], 0, "od_hi", 3 * m + (g + 1), "od_lo")

            od_low(0, 0, 0)
            update(3)
            norm_scale(5, res, xn)
            norm_evac(5, lambda k: normT[:, k, :], lambda k: vecB[:, VB_MIX + 8 + k:VB_MIX + 9 + k], None, order=dilated, split=True)

            def od_rotate(m, par, g, t):
                dve.wait_ge(s["od_raw"], 6 * m + (2 * g + t + 1))
                if not isinstance(m, int) or 3 * m + g >= 2:
                    dve.wait_ge(s["qkT_ps"], 3 * m + (g - 1))
                rotate(qr[:, (3 * par + g) % 2, t, :].rearrange("p (h d) -> p h d", d=HD),
                       raw[:, t, :].rearrange("p (h d) -> p h d", d=HD), orope[:, t], 4, HD, ro,
                       lambda ins: ins.then_inc(s["rot_ready"], 1))
                dve.wait_ge(s["rot_ready"], 6 * m + (2 * g + t + 1))

            def od_max(u, j):
                neg_max(u, j, None, 1, HD ** -0.5, omask[:, j % 2, :].unsqueeze(1))

            om5 = om.rearrange("p t (n h d) -> p t n h d", h=2, d=HD)

            def od_out(n, par):
                dve.wait_ge(s["pv_ps"], 4 * n + (U_OD + 4))
                chain(dve.reciprocal(rinv[:, 32 + 4 * par:36 + 4 * par], rsum[:, 32 + 4 * par:36 + 4 * par]))
                for t in range(NT):
                    ins = dve.tensor_tensor(om5[:, t, n, :, :], bank[7][:, P * t:P * t + P].rearrange("p (h d) -> p h d", d=HD),
                                            rinv[:, 32 + 4 * par + 2 * t:34 + 4 * par + 2 * t].unsqueeze(2).to_broadcast([P, 2, HD]),
                                            ALU.mult)
                ins.then_inc(s["o_out"], 1)

            def od_pair(m, n, pm, pn):
                u = None if n is None else 4 * n + U_OD
                if m is not None:
                    od_low(m, pm, 1)
                    od_rotate(m, pm, 0, 0)
                    od_rotate(m, pm, 0, 1)
                    od_low(m, pm, 2)
                    od_rotate(m, pm, 1, 0)
                    od_rotate(m, pm, 1, 1)
                if n is not None:
                    od_max(u + 0, 0)
                    od_max(u + 1, 1)
                if m is not None:
                    if not isinstance(m, int) or m < OD_PAIRS - 1:
                        od_low(m + 1, 1 - pm, 0)
                    od_rotate(m, pm, 2, 0)
                if n is not None:
                    od_max(u + 2, 2)
                    od_max(u + 3, 3)
                if m is not None:
                    od_rotate(m, pm, 2, 1)
                if n is not None:
                    od_out(n, pn)

            od_pair(0, None, 0, None)
            with dve.Fori(0, OD_PAIRS // 2 - 1) as i:
                chain.enter(i, 2 * (6 * 2 + 4 + 1))
                od_pair(2 * i + 1, 2 * i, 1, 0)
                od_pair(2 * i + 2, 2 * i + 1, 0, 1)
            chain.leave(OD_PAIRS // 2 - 1)
            od_pair(OD_PAIRS - 1, OD_PAIRS - 2, 1, 0)
            od_pair(None, OD_PAIRS - 1, None, 1)
            turn_evac(2, oT, dilated)
            mlp_first(1)
            update(4)
            norm_scale(6, res, xn)
            norm_evac(6, lambda k: normT[:, k, :], lambda k: vecB[:, VB_MLP + 8 + k:VB_MLP + 9 + k], None, split=True)
            mlp(1)
            update(5)
            dve.wait_ge(s["final_loaded"], 16)
            norm_scale(7, res, xn)
            for t in range(NT):
                dve.wait_ge(s["xn_ready"], 15 + t)
                dve.tensor_tensor(xn[:, t, :], xn[:, t, :], frow, ALU.mult).then_inc(s["out_ready"], 1)

        @block.tensor
        def _(pe):
            mm = pe.matmul

            def landed_wait(e):
                pe.wait_ge(e.sem, e.value)

            pe.wait_ge(s["vecs_loaded"], 16 * 9)
            pe.wait_ge(s["consts_loaded"], 16)
            pe.transpose(bank[4][:, 0:VA_N], hTs[0:VA_N, 0:P], ident[0:VA_N, 0:VA_N]).then_inc(s["vec_ps"], 1)
            pe.transpose(bank[5][:, 0:VB_N], hTs[0:VB_N, P:2 * P], ident[0:VB_N, 0:VB_N]).then_inc(s["vec_ps"], 1)

            def mod_slot(i, b):
                e = L["mod", i]
                landed_wait(e)
                w = pv(e)
                for c in range(4):
                    for k in range(KD):
                        ins = mm(bank[b][:, 2 * (4 * i + c):2 * (4 * i + c) + 2], w[:, k, P * c:P * c + P], silc[:, k, :],
                                 start=(k == 0), stop=(k == KD - 1))
                return ins

            pe.wait_ge(s["silu_done"], 2)
            for i in range(4):
                mod_slot(i, 7).then_inc(s["mod_used"], 1)

            def turn_tokens(n, src):
                for t in range(NT):
                    pe.wait_ge(s["xn_ready"], 2 * n + t + 1)
                    if t == 0 and n == 1:
                        pe.wait_ge(s["hT_act"], 2)
                        pe.wait_ge(s["hT_dve"], 2)
                    for b in range(4):
                        for k in (2 * b, 2 * b + 1):
                            ins = pe.transpose(bank[b][:, 256 * (k - 2 * b) + P * t:256 * (k - 2 * b) + P * t + P],
                                               src[:, t, P * k:P * k + P], ident)
                        if t == NT - 1:
                            ins.then_inc(s["xT_ps"], 1)

            def hT_wait(n):
                pe.wait_ge(s["hT_act"], 2 * n + 2)
                pe.wait_ge(s["hT_dve"], 2 * n + 2)

            turn_tokens(0, xn)
            turn_tokens(1, rG)
            hT_wait(1)
            pe.wait_ge(s["small_loaded"], 32)
            for k in range(KD):
                ins = mm(bank[0][0:2 * RANK, :], wglr[:, k, :], hT_all[:, k, :], start=(k == 0), stop=(k == KD - 1))
            ins.then_inc(s["glr_ps"], 1)
            pe.wait_ge(s["glr_ready"], 1)
            pe.wait_ge(s["gate_w_loaded"], 32)
            for zh in range(8):
                if zh >= 4:
                    pe.wait_ge(s["gate_in"], zh - 3)
                mm(bank[1 + zh % 4][:, :], wgate[:, P * zh:P * zh + P], glrT, start=True, stop=True).then_inc(s["gate_ps"], 1)

            for j in range(20):
                if j >= 3 and j < 19:
                    pe.wait_ge(s["proj_out"], j - 2)
                if j == 19:
                    pe.wait_ge(s["silu_r"], 1)
                b = bank[5 + j % 3]
                if j < 8:
                    e = L["k" if j < 4 else "q", (j % 4) // 2]
                    if j % 2 == 0:
                        landed_wait(e)
                    toks = slice(0, 512) if j < 4 else slice(256, 512)
                    for k in range(KD):
                        ins = mm(b[:, 0:toks.stop - toks.start], pv(e)[:, k, P * (j % 2):P * (j % 2) + P], hT_all[:, k, toks],
                                 start=(k == 0), stop=(k == KD - 1))
                    ins.then_inc(s["proj_ps"], 1)
                else:
                    per = 4 if j < 16 else 2
                    jj = j - (8 if j < 16 else 16)
                    e = L["v" if j < 16 else "r", jj // per]
                    if jj % per == 0:
                        landed_wait(e)
                    tok = P * (jj % per) + (0 if j < 16 else 256)
                    for k in range(KD):
                        ins = mm(b[:, :], hT_all[:, k, tok:tok + P], pv(e)[:, k, :], start=(k == 0), stop=(k == KD - 1))
                    ins.then_inc(s["proj_ps"], 1)
            for i in range(4, 12):
                mod_slot(i, 0).then_inc(s["mod_used"], 1)
            pe.wait_ge(s["silu_r"], 4)

            pe.wait_ge(s["kd_ready"], 4)
            pe.wait_ge(s["ke_ready"], 2)
            pe.wait_ge(s["mod_cols"], 2)
            pe.wait_ge(s["proj_out"], 16)
            for z in range(2):
                for u in range(2):
                    for h in range(2):
                        for t in range(NT):
                            ins = mm(bank[4 + 2 * z + u][:, P * (2 * h + t):P * (2 * h + t) + P],
                                     kd[:, z, 2 * u + h, P * t:P * t + P], qd[:, z, 2 * u + h, P * t:P * t + P],
                                     start=True, stop=True)
                    ins.then_inc(s["sT_ps"], 1)
                for h in range(GH):
                    zh = GH * z + h
                    if zh >= 4:
                        pe.wait_ge(s["keT_act"] if zh % 2 else s["keT_dve"], (zh - 4) // 2 + 1)
                    for t in range(4):
                        ins = pe.transpose(bank[zh % 4][:, P * t:P * t + P], G1[:, z, h, P * t:P * t + P], ident)
                    ins.then_inc(s["keT_ps"], 1)
            pe.wait_ge(s["sT_ready"], 4)
            pe.wait_ge(s["keT_act"], 4)
            pe.wait_ge(s["keT_dve"], 4)

            def state_update(j, z):
                if j:
                    pe.wait_ge(s["state_ready"], 2 * (j - 1) + z + 1)
                ch = chunk_of(z, j)
                lo = CHUNK * (ch % 2)
                for h in range(GH):
                    ins = mm(bank[4 + 2 * z + h // 2][:, GDV * (h % 2):GDV * (h % 2) + GDV], keT[lo:lo + CHUNK, z, h, ch // 2, :],
                             vG[lo:lo + CHUNK, ch // 2, GDV * h:GDV * h + GDV], start=True, stop=True)
                ins.then_inc(s["upd_ps"], 1)

            def from_state(j, z):
                pe.wait_ge(s["state_ready"], 2 * j + z + 1)
                cl = j - 3 if z == 0 else 6 - j
                lo = CHUNK * (cl % 2)
                for h in range(GH):
                    ins = mm(bank[2 * (cl // 2) + h // 2][lo:lo + CHUNK, GDV * (h % 2):GDV * (h % 2) + GDV],
                             qd[:, z, h, CHUNK * cl:CHUNK * cl + CHUNK], states[:, (j + 1) % 2, z, h, :],
                             start=False, stop=False, skip_group_check=True)
                ins.then_inc(s["inter_ps"], 1)

            state_update(0, 0)
            state_update(0, 1)
            for t in range(NT):
                for u in range(2):
                    for h in range(2):
                        for z in range(2):
                            mm(bank[2 * t + u][:, GDV * h:GDV * h + GDV], sT[:, z, u, 2 * h + t, :],
                               vG[:, 2 + t, GDV * (2 * u + h):GDV * (2 * u + h) + GDV], start=(h == 0 and z == 0), stop=False,
                               skip_group_check=True)
            for j in range(1, 7):
                for z in range(2):
                    state_update(j, z)
                if j > 3:
                    for z in range(2):
                        from_state(j - 1, z)
            for z in range(2):
                from_state(6, z)
            pe.wait_ge(s["zero_ready"], 1)
            for b in range(4):
                ins = mm(bank[b][:, 0:512], zero[:, 0:P], zero[:, :], start=False, stop=True, skip_group_check=True)
            ins.then_inc(s["o_ps"], 1)
            pe.wait_ge(s["state_ready"], 14)
            pe.wait_ge(s["eff_ready"], 5)
            for b in range(4):
                for k in range(4):
                    kk = 4 * (b % 2) + k
                    ins = mm(bank[4 + b][:, P * k:P * k + P], eff[:, 3 + b // 2, kk:kk + 1].to_broadcast([P, P]), ident,
                             start=True, stop=True)
                ins.then_inc(s["rows_ps"], 1)

            def turn_mixed(n, src):
                for b in range(4):
                    for k in (2 * b, 2 * b + 1):
                        for t in range(NT):
                            ins = pe.transpose(bank[4 + b][:, 256 * (k - 2 * b) + P * t:256 * (k - 2 * b) + P * t + P],
                                               src[:, t, P * k:P * k + P], ident)
                    ins.then_inc(s["ogT_ps"], 1)

            def out_product(n, keys, srcT):
                pe.wait_ge(s["ogT_act"], 2 * n + 2)
                pe.wait_ge(s["ogT_dve"], 2 * n + 2)
                for i, key in enumerate(keys):
                    e = L[key]
                    landed_wait(e)
                    for kk in range(4):
                        k = 4 * i + kk
                        for b in range(4):
                            ins = mm(bank[b][:, :], srcT[:, k, P * (b // 2):P * (b // 2) + P], pv(e)[:, kk, 512 * (b % 2):512 * (b % 2) + 512],
                                     start=(k == 0), stop=(k == KD - 1))
                    ins.then_inc(s["out_used"], 1)

            pe.wait_ge(s["rows_ready"], 4)
            pe.wait_ge(s["og_ready"], 2)
            turn_mixed(0, og)
            out_product(0, [("go", 0), ("go", 1)], ogT)
            turn_tokens(2, xn)
            pe.wait_ge(s["hT_lo"], 4)

            def zero_banks():
                for b in range(4):
                    mm(bank[b][:, :], zero[:, 0:P], zero[:, :], start=True, stop=False, skip_group_check=True)

            def close_banks():
                for b in range(4):
                    ins = mm(bank[b][:, :], zero[:, 0:P], zero[:, :], start=False, stop=True, skip_group_check=True)
                ins.then_inc(s["y_ps"], 1)

            zero_banks()

            def split_mm(out_, left, right, start, stop):
                flag = {"skip_group_check": True} if not (start or stop) else {}
                mm(out_, left[0], right[0], start=start, stop=False, **flag)
                mm(out_, left[0], right[1], start=False, stop=False, **flag)
                return mm(out_, left[1], right[0], start=False, stop=stop, **flag)

            def both(pair, pick):
                return [pick(x) for x in pair]

            def ffn_up(f, j):
                pe.wait_ge(s["loU_ready"], f + 1)
                if not isinstance(f, int) or f >= 2:
                    pe.wait_ge(s["ff_mid"], f - 1)
                for g in range(2):
                    for k in range(KD):
                        ins = split_mm(bank[4 + j % 2][:, 256 * g:256 * g + 256],
                                       both(ffU[j % 2], lambda x: x[:, 1024 * g + P * k:1024 * g + P * k + P]),
                                       both(hT2, lambda x: x[:, k, :]), k == 0, k == KD - 1)
                ins.then_inc(s["ff_ps"], 1)

            def ffn_down(f, j):
                pe.wait_ge(s["ff_mid"], f + 1)
                pe.wait_ge(s["loD_ready"], f + 1)
                for b in range(4):
                    ins = split_mm(bank[b][:, :], both(mid2, lambda x: x[:, j % 2, P * (b // 2):P * (b // 2) + P]),
                                   both(ffD[j % 2], lambda x: x[:, 512 * (b % 2):512 * (b % 2) + 512]), False, False)
                ins.then_inc(s["w_used"], 1)

            def ffn_round(f0, n):
                for j in range(n):
                    ffn_up(f0 + j, j)
                    if j:
                        ffn_down(f0 + (j - 1), j - 1)
                ffn_down(f0 + (n - 1), n - 1)

            ffn_round(0, FF_RING)
            with pe.Fori(0, FF_LOOPS - 1) as i:
                ffn_round(i * FF_RING + FF_RING, FF_RING)
            ffn_round(FF_LOOPS * FF_RING, FFC - FF_LOOPS * FF_RING)
            close_banks()

            turn_tokens(3, xn)
            hT_wait(3)
            e = L["c"]
            landed_wait(e)
            for t in range(NT):
                for k in range(KD):
                    ins = mm(bank[4 + t][:, 0:416], hT[:, k, P * t:P * t + P], pv(e)[:, k, :], start=(k == 0), stop=(k == KD - 1))
                ins.then_inc(s["c_ps"], 1)
            for c in range(8):
                e = L["qk", c // 2]
                if c % 2 == 0:
                    landed_wait(e)
                if c >= 2:
                    pe.wait_ge(s["qk_act"] if c % 2 else s["qk_dve"], c // 2)
                for k in range(KD):
                    ins = mm(bank[6 + c % 2][:, 0:256], pv(e)[:, k, P * (c % 2):P * (c % 2) + P], hT[:, k, :],
                             start=(k == 0), stop=(k == KD - 1))
                ins.then_inc(s["qk_ps"], 1)
            landed_wait(L["va"])
            pe.wait_ge(s["qk_act"], 4)
            pe.wait_ge(s["qk_dve"], 4)
            for t in range(NT):
                for k in range(KD):
                    ins = mm(bank[6 + t][:, :], hT[:, k, P * t:P * t + P], pv(L["va"])[:, k, :], start=(k == 0), stop=(k == KD - 1))
                ins.then_inc(s["vn_ps"], 1)
            pe.wait_ge(s["c_ready"], 4)
            pe.wait_ge(s["kpe_ready"], 2)
            for k in range(3):
                for t in range(NT):
                    ins = pe.transpose(bank[4 + k // 2][:, 256 * (k % 2) + P * t:256 * (k % 2) + P * t + P], ctm[:, t, P * k:P * k + P], ident)
                if k == 1:
                    ins.then_inc(s["cT_ps"], 1)
            for t in range(NT):
                ins = pe.transpose(bank[5][0:MQ, 256 + P * t:256 + P * t + P], kpe[:, t, :], ident)
            ins.then_inc(s["cT_ps"], 1)
            pe.wait_ge(s["cT_act"], 2)
            pe.wait_ge(s["cT_dve"], 2)
            pe.wait_ge(s["vn_act"], 1)
            pe.wait_ge(s["vn_dve"], 1)
            landed_wait(L["ukv"])
            wk = pv(L["ukv"])[:, 0, :].rearrange("p (h c) -> p h c", c=NOPE + HD)
            for h in range(MLA_H):
                ins = mm(bank[4 + h // 2][0:NOPE, 256 * (h % 2):256 * (h % 2) + 256], wk[:, h, 0:NOPE], cT[:, 2, :], start=True, stop=True)
                if h % 2:
                    ins.then_inc(s["mk_ps"], 1)
            landed_wait(L["uq"])
            for t in range(NT):
                for hf in range(2):
                    for k in range(2):
                        ins = mm(bank[2 * t + hf][:, 0:384], cT[:, k, P * t:P * t + P], pv(L["uq"])[:, k, 384 * hf:384 * hf + 384],
                                 start=(k == 0), stop=(k == 1))
                    ins.then_inc(s["mq_ps"], 1)
            pe.wait_ge(s["mk_out"], MLA_H)
            for t in range(NT):
                mm(bank[4 + t][:, :], cT[:, 2, P * t:P * t + P], wk[:, :, NOPE:], start=True, stop=True).then_inc(s["mv_ps"], 1)
            pe.wait_ge(s["mq_rot"], 8)
            for i in range(4):
                for h in (2 * i, 2 * i + 1):
                    for t in range(NT):
                        ins = pe.transpose(bank[i][0:MQ, 256 * (h - 2 * i) + P * t:256 * (h - 2 * i) + P * t + P], qtm[:, t, h, :], ident)
                ins.then_inc(s["mqT_ps"], 1)
            pe.wait_ge(s["mqT_out"], 4)
            pe.wait_ge(s["mv_out"], 2)
            pe.wait_ge(s["cT_dve"], 2)

            def ev_scores(u):
                if u >= 2:
                    pe.wait_ge(s["prob_ready"], u - 1)
                for t in range(NT):
                    if u < NA_H:
                        lo = HD * (u % 2)
                        q, k = qkN[lo:lo + HD, u // 2, P * t:P * t + P], qkN[lo:lo + HD, 4 + u // 2, :]
                    else:
                        q, k = qM[0:MQ, u - NA_H, P * t:P * t + P], kM[0:MQ, u - NA_H, :]
                    ins = mm(bank[3 + u % 2][:, 256 * t:256 * t + 256], q, k, start=True, stop=True)
                ins.then_inc(s["s_ps"], 1)

            def turn_probs(u, j, count):
                pe.wait_ge(s["prob_ready"], count)
                if not isinstance(u, int) or u >= 2:
                    pe.wait_ge(s["pT_ready"], u - 1)
                for b in range(4):
                    ins = pe.transpose(bank[5 + j % 2][:, P * b:P * b + P], prob[:, j % 2, P * b:P * b + P], ident)
                ins.then_inc(s["pT_ps"], 1)

            def ev_values(u):
                pe.wait_ge(s["pT_ready"], u + 1)
                k, h = u // 8, u % 8
                v = vN if k == 0 else vM
                for t in range(NT):
                    for c in range(2):
                        ins = mm(bank[OUT_BANK[k][t]][:, HD * h:HD * h + HD], probT[:, u % 2, P * (2 * t + c):P * (2 * t + c) + P],
                                 v[:, c, HD * h:HD * h + HD], start=(c == 0), stop=(c == 1))
                ins.then_inc(s["pv_ps"], 1)

            for u in range(U_OD + 2):
                if u < U_OD:
                    ev_scores(u)
                if 1 <= u <= U_OD:
                    turn_probs(u - 1, u - 1, u)
                if u >= 2:
                    ev_values(u - 2)
            pe.wait_ge(s["o_out"], 4)
            pe.wait_ge(s["pT_ready"], U_OD)
            turn_mixed(1, om)
            out_product(1, [("eo", 0), ("eo", 1)], oT)

            def mlp(l):
                def up(st, j):
                    pe.wait_ge(s["loU_ready"], st + 1)
                    pe.wait_ge(s["ff_mid"], st - 1)
                    for f in range(2):
                        for k in range(KD):
                            ins = split_mm(bank[4 + j % 2][:, 256 * f:256 * f + 256],
                                           both(mlU[j % 2], lambda x: x[:, 256 * k + P * f:256 * k + P * f + P]),
                                           both(hT2, lambda x: x[:, k, :]), k == 0, k == KD - 1)
                    ins.then_inc(s["ff_ps"], 1)

                def down(st, j):
                    pe.wait_ge(s["ff_mid"], st + 1)
                    pe.wait_ge(s["loD_ready"], st + 1)
                    for f in range(2):
                        for b in range(4):
                            at = D * f + 512 * (b % 2)
                            ins = split_mm(bank[b][:, :], both(mid2, lambda x: x[:, j % 2, 256 * f + P * (b // 2):256 * f + P * (b // 2) + P]),
                                           both(mlD[j % 2], lambda x: x[:, at:at + 512]), False, False)
                    ins.then_inc(s["w_used"], 1)

                zero_banks()
                with pe.Fori(0, MLP_LOOPS) as i:
                    st = i * MLP_RING + (FFC + 16 * l)
                    for j in range(MLP_RING):
                        up(st + j, j)
                        if j:
                            down(st + (j - 1), j - 1)
                    down(st + (MLP_RING - 1), MLP_RING - 1)
                close_banks()

            turn_tokens(4, xn)
            pe.wait_ge(s["hT_lo"], 8)
            mlp(0)

            turn_tokens(5, xn)
            pe.wait_ge(s["hT_lo"], 12)

            def od_proj(m, par, g, t):
                if t == 0:
                    pe.wait_ge(s["od_lo"], 3 * m + (g + 1))
                if not isinstance(m, int) or m or g:
                    pe.wait_ge(s["od_v"], 6 * m + (2 * g + t - 1))
                w = both(odW[(3 * par + g) % 2], lambda x: x[:, :].rearrange("p (j k c) -> p k j c", j=3, k=KD))
                for k in range(KD):
                    ins = split_mm(bank[t][:, 0:384], both(hT2, lambda x: x[:, k, P * t:P * t + P]),
                                   both(w, lambda x: x[:, k]), k == 0, k == KD - 1)
                ins.then_inc(s["od_ps"], 1)

            def od_turn(m, par, g):
                pe.wait_ge(s["rot_ready"], 6 * m + (2 * g + 2))
                if not isinstance(m, int) or m or g:
                    pe.wait_ge(s["qkT_out"], 3 * m + g)
                for j in range(2):
                    for t in range(NT):
                        ins = pe.transpose(bank[2][:, 256 * j + P * t:256 * j + P * t + P],
                                           qr[:, (3 * par + g) % 2, t, P * j:P * j + P], ident)
                ins.then_inc(s["qkT_ps"], 1)

            def od_scores(u, par, j):
                pe.wait_ge(s["prob_ready"], u - 1)
                h, t = j // 2, j % 2
                lo = HD * h
                for g, (at, k0, n) in enumerate([(0, 256, 256), (256, 256 + P * t, P), (384, 256 + P * t, P)]):
                    ins = mm(bank[3 + j % 2][:, at:at + n], qkT[lo:lo + HD, par, g, P * t:P * t + P], qkT[lo:lo + HD, par, g, k0:k0 + n],
                             start=True, stop=True)
                ins.then_inc(s["s_ps"], 1)

            def od_attend(u, par, j, n):
                pe.wait_ge(s["pT_ready"], u + 1)
                if j == 0:
                    pe.wait_ge(s["o_out"], n + 4)
                h, t = j // 2, j % 2
                for b, (g, tile) in enumerate([(0, 0), (0, 1), (1, t), (2, t)]):
                    ins = mm(bank[7][:, P * t + HD * h:P * t + HD * h + HD], probT[:, j % 2, P * b:P * b + P],
                             vO[:, par, g, tile, HD * h:HD * h + HD], start=(b == 0), stop=(b == 3))
                ins.then_inc(s["pv_ps"], 1)

            def od_pair(m, n, pm, pn):
                u = None if n is None else 4 * n + U_OD
                if m is not None:
                    od_proj(m, pm, 0, 0)
                    od_proj(m, pm, 0, 1)
                if n is not None:
                    od_turn(n, pn, 2)
                if m is not None:
                    od_proj(m, pm, 1, 0)
                    od_proj(m, pm, 1, 1)
                if n is not None:
                    pe.wait_ge(s["qkT_out"], 3 * n + 3)
                    od_scores(u + 0, pn, 0)
                    od_scores(u + 1, pn, 1)
                if m is not None:
                    od_turn(m, pm, 0)
                    od_proj(m, pm, 2, 0)
                if n is not None:
                    turn_probs(u + 0, 0, u + 1)
                    turn_probs(u + 1, 1, u + 2)
                    od_scores(u + 2, pn, 2)
                    od_scores(u + 3, pn, 3)
                if m is not None:
                    od_proj(m, pm, 2, 1)
                if n is not None:
                    od_attend(u + 0, pn, 0, n)
                    od_attend(u + 1, pn, 1, n)
                    turn_probs(u + 2, 2, u + 3)
                    turn_probs(u + 3, 3, u + 4)
                if m is not None:
                    od_turn(m, pm, 1)
                if n is not None:
                    od_attend(u + 2, pn, 2, n)
                    od_attend(u + 3, pn, 3, n)

            od_pair(0, None, 0, None)
            with pe.Fori(0, OD_PAIRS // 2 - 1) as i:
                od_pair(2 * i + 1, 2 * i, 1, 0)
                od_pair(2 * i + 2, 2 * i + 1, 0, 1)
            od_pair(OD_PAIRS - 1, OD_PAIRS - 2, 1, 0)
            od_pair(None, OD_PAIRS - 1, None, 1)
            pe.wait_ge(s["o_out"], 4 + OD_PAIRS)
            turn_mixed(2, om)
            out_product(2, [("oo", 0), ("oo", 1)], oT)
            turn_tokens(6, xn)
            pe.wait_ge(s["hT_lo"], 16)
            mlp(1)


_INS = ['x', 'c', 'ctx', 'c_ctx', 'mod_w', 'mod_b', 'norm_g', 'ffn_w_in', 'ffn_w_out', 'gla_w_in', 'gla_w_gate',
        'gla_b_gate', 'gla_norm_g', 'gla_w_out', 'norm_mix_2', 'norm_mlp_2', 'norm_final_2', 'ev_w_in_2', 'ev_rpb_2',
        'ev_q_norm_2', 'ev_w_uq_2', 'ev_kv_norm_2', 'ev_w_ukv_2', 'ev_w_o_2', 'od_w_in_2', 'od_w_o_2', 'mlp_w1_2',
        'mlp_w2_2']


def kernel(**inputs):
    import numpy as _np
    import concourse.bacc as _bacc
    from concourse import mybir as _mybir
    from concourse.bass_utils import run_bass_kernel_spmd as _run

    nc = _bacc.Bacc("TRN2", target_bir_lowering=False, num_devices=1)
    arrays, args = {}, {}
    for name in _INS:
        v = _np.ascontiguousarray(inputs[name])
        arrays[f"in_{name}_dram"] = v
        args[name] = nc.dram_tensor(f"in_{name}_dram", v.shape, _mybir.dt.from_np(v.dtype), kind="ExternalInput").ap()
    table = constants()
    arrays["in_consts_dram"] = table
    args["consts"] = nc.dram_tensor("in_consts_dram", table.shape, F32, kind="ExternalInput").ap()
    out = nc.dram_tensor("out_0_dram", (1, SEQ, D), F32, kind="ExternalOutput").ap()
    program(nc, args, out)
    r = _run(nc, [arrays], core_ids=[0])
    return r.results[0]["out_0_dram"]
```

```python
from contextlib import ExitStack

import numpy as np

import concourse.bass as bass
from concourse import mybir

ACT = mybir.ActivationFunctionType
ALU = mybir.AluOpType
F32 = mybir.dt.float32
F32R = mybir.dt.float32r
BF16 = mybir.dt.bfloat16
U32 = mybir.dt.uint32
AX = mybir.AxisListType.X

P = 128
SEQ = 256
NT = SEQ // P
D = 1024
KD = D // P
EPS = 1e-6
GRID = 64

GH, GDK, GDV, RANK, CHUNK = 4, 128, 256, 16, 64
GLA_QK, GLA_V = GH * GDK, GH * GDV
GATE_NORM = 16.0
FF = 2816
FFC = FF // P
FF_RING = 6
FF_LOOPS = 3

HD = 64
NA_H, MLA_H, OD_H = 8, 8, 16
NOPE, ROPE, QR, KVR = 64, 32, 256, 128
MQ = NOPE + ROPE
DFF = 4 * D
MLP_RING = 4
MLP_LOOPS = DFF // 256 // MLP_RING
OD_PAIRS = OD_H // 2
RPB = NA_H * 15 * 31
NEG = -1e30

C_ID, C_GM, C_NM, C_MR, C_OM, C_OR = 0, 128, 384, 896, 1024, 2048
C_ALL = 2304
VA_C, VA_CC, VA_NG, VA_MB, VA_QN, VA_KN, VA_BG, VA_N = 0, 8, 16, 48, 96, 98, 99, 107
VB_MIX, VB_MLP, VB_N = 0, 16, 32
MOD_POOL = (6, 8, 10)
MOD_DVE = 6
POOL = 18432


def constants():
    c = np.zeros((P, C_ALL), np.float32)
    c[:, C_ID:C_ID + P] = np.eye(P)
    j, i = np.meshgrid(np.arange(P), np.arange(P), indexing="ij")
    same = j // CHUNK == i // CHUNK
    c[:, C_GM:C_GM + P] = same & (j <= i)
    c[:, C_GM + P:C_GM + 2 * P] = same & (j >= i)
    tok = np.arange(SEQ)
    start = np.clip(tok % GRID - 8, 0, GRID - 16)
    kc = tok % GRID
    na = np.where((kc[None] >= start[:, None]) & (kc[None] < start[:, None] + 16), 0.0, NEG)
    c[:, C_NM:C_MR] = na.reshape(NT, P, SEQ).transpose(1, 0, 2).reshape(P, -1)

    def rope(pos, dim):
        inv = np.float32(1.0) / (np.float32(10000.0) ** (np.arange(0, dim, 2, dtype=np.float32) / np.float32(dim)))
        ang = pos.astype(np.float32)[:, None] * inv[None]
        co, si = np.cos(ang), np.sin(ang)
        t = np.stack([np.concatenate([co, co], 1), np.concatenate([-si, si], 1)], 1)
        return t.reshape(NT, P, 2 * dim).transpose(1, 0, 2).reshape(P, -1)

    c[:, C_MR:C_OM] = rope(tok, ROPE)
    s, m, a = np.meshgrid(np.arange(4), np.arange(4), np.arange(16), indexing="ij")
    perm = (16 * a + 4 * m + s).reshape(-1)
    dist = perm[None] - perm[:, None]
    wide = np.where(np.abs(dist) <= 64, 0.0, NEG)
    by4 = np.where(dist % 4 == 0, 0.0, NEG)
    by16 = np.where(dist % 16 == 0, 0.0, NEG)
    om = np.zeros((P, NT, 512), np.float32)
    for t in range(NT):
        rows = slice(t * P, t * P + P)
        om[:, t] = np.concatenate([wide[rows], by4[rows, rows], by16[rows, rows]], 1)
    c[:, C_OM:C_OR] = om.reshape(P, -1)
    c[:, C_OR:] = rope(perm, HD)
    return c


def program(nc, a, out):
    with ExitStack() as ctx:
        def sb(name, shape, dt=F32):
            return ctx.enter_context(nc.sbuf_tensor(name, shape, dt))

        def sem(name):
            return ctx.enter_context(nc.semaphore(name))

        bank = [ctx.enter_context(nc.psum_tensor(f"bank{i}", [P, 512], F32)) for i in range(8)]
        areas = {}

        def area(name, words):
            areas[name] = -(-nc.sbuf_base // 32) * 32
            return sb(name, [P, words])

        def over(name, where, at, words):
            return nc.alloc_sbuf_tensor_at(name, [P, words], F32R, offset=areas[where] + 4 * at)

        pool = area("weight_pool", POOL)
        work = area("work", 21504)
        hTs = area("hT", 4096)
        res = sb("residual", [P, NT, D])
        xn = sb("normed", [P, NT, D])
        consts = sb("consts", [P, C_ALL])
        vecA = sb("vecA", [P, P])
        vecB = sb("vecB", [P, VB_N])
        mods = sb("mods", [P, 48, 2])
        eff = sb("eff", [P, 5, KD])
        silc = sb("silc", [P, KD, 2])
        wglr = sb("wglr", [P, KD, 2 * RANK])
        gnrow = sb("gnrow", [P, GDV])
        stat = sb("stat", [P, 192])
        zero = sb("zero", [P, 512], BF16)
        decay = sb("decay", [P, 2 * GH * 8])
        bend = sb("bend", [P, 2 * GH * 8])
        ones = sb("ones", [P, 1])
        rsum = sb("rsum", [P, 48])
        rinv = sb("rinv", [P, 48])

        skew = nc.dram_tensor("bias_copies", (GRID, RPB), F32).ap()
        ident = consts[:, C_ID:C_ID + P]
        eps = stat[:, 90:91]

        def view(t, at, *dims):
            n = 1
            for d in dims:
                n *= d
            v = t[:, at:at + n]
            if len(dims) == 2:
                return v.rearrange("p (a b) -> p a b", b=dims[1])
            if len(dims) == 3:
                return v.rearrange("p (a b c) -> p a b c", b=dims[1], c=dims[2])
            if len(dims) == 4:
                return v.rearrange("p (a b c d) -> p a b c d", b=dims[1], c=dims[2], d=dims[3])
            return v

        def dilated(v):
            return v.rearrange("p (a m s) -> p s m a", m=4, s=4)

        def by_sma(v):
            return v.rearrange("p (s m a) -> p s m a", m=4, s=4)

        def vec_rows(at, n):
            return hTs[at:at + n, 0:P] if at < VA_NG else hTs[at - VA_NG:at - VA_NG + n, P:2 * P]

        hT_all = view(hTs, 0, KD, 512)
        G1 = view(work, 0, 2, GH, 512)
        G2 = view(work, 4096, 2, GH, 512)
        qd = view(work, 8192, 2, GH, SEQ)
        kd = view(work, 10240, 2, GH, SEQ)
        wgate = work[0:2 * RANK, 10240:10240 + 2 * GLA_QK]
        glrT = work[0:2 * RANK, 10240 + 2 * GLA_QK:10240 + 2 * GLA_QK + 512]
        kT = view(work, 12288, GH, 512)
        sT = view(work, 12288, 2, 2, 4, P)
        qT = view(work, 14336, GH, SEQ)
        vG = view(work, 15360, 4, GLA_V)
        rG = view(work, 19456, NT, D)
        keT = view(hTs, 0, 2, GH, 4, P)
        reset = view(work, 19456, 2048)
        states = view(work, 4096, 2, 2, GH, GDV)
        og = view(work, 0, NT, D)
        oT = view(hTs, 2048, KD, SEQ)
        ogT = view(work, 2048, KD, SEQ)
        rows = view(work, 6144, 2, D)
        first_sums = view(work, 4096, 4, 2, 512)

        def late_sum(i):
            return xn[:, (i - 4) // 2, 512 * (i % 2):512 * (i % 2) + 512] if i < 8 else pool[:, 16384 + 512 * (i - 8):16896 + 512 * (i - 8)]

        hT = view(hTs, 0, KD, SEQ)
        normT = view(work, 16384, KD, SEQ)
        act_a = view(work, 16384, 2, 512)
        act_s = view(work, 19456, 2, 512)
        hT2 = [view(over(f"hT_{w}", "hT", 2048 * i, 2048), 0, KD, SEQ) for i, w in enumerate(("high", "low"))]
        mid2 = [view(over(f"hidden_{w}", "work", 17408 + 1024 * i, 1024), 0, 2, 512) for i, w in enumerate(("high", "low"))]
        ffU = [[over(f"ffn_up{j}_{w}", "work", at + 2048 * i, 2048) for i, w in enumerate(("high", "low"))]
               for j, at in enumerate((10240, 0))]
        ffD = [[over(f"ffn_down{j}_{w}", "work", at + 4096 + 1024 * i, 1024) for i, w in enumerate(("high", "low"))]
               for j, at in enumerate((10240, 0))]
        mlU = [[over(f"mlp_up{j}_{w}", "work", 8192 * j + 2048 * i, 2048) for i, w in enumerate(("high", "low"))] for j in range(2)]
        mlD = [[over(f"mlp_down{j}_{w}", "work", 8192 * j + 4096 + 2048 * i, 2048) for i, w in enumerate(("high", "low"))]
               for j in range(2)]
        odW = [[over(f"od_w{j}_{w}", where, at + 3072 * i, 3072) for i, w in enumerate(("high", "low"))]
               for j, (where, at) in enumerate((("weight_pool", 9216), ("work", 6656)))]
        nabias = view(work, 0, NA_H, NT, SEQ)
        qkN = view(work, 4096, 8, SEQ)
        vN = view(work, 6144, NT, NA_H * HD)
        vM = view(work, 7168, NT, MLA_H * HD)
        qM = view(work, 8192, MLA_H, SEQ)
        kM = view(work, 10240, MLA_H, SEQ)
        qtm = view(work, 12288, NT, MLA_H, MQ)
        ctm = view(work, 13824, NT, 416)
        cT = view(work, 14656, 3, SEQ)
        prob = view(work, 15424, 2, 512)
        score = view(work, 16448, 2, 512)
        probT = view(work, 17472, 2, 512)
        om = view(work, 18496, NT, D)
        rt = view(work, 20544, 2, 256)
        kpe = view(hTs, 2048, NT, MQ)
        qkT = view(work, 0, 2, 3, 512)
        vO = view(work, 3072, 2, 3, NT, P)
        qr = view(work, 4608, 2, NT, 256)
        ro = view(work, 5632, 2, 256)
        raw = view(work, 6144, 2, 256)
        frow = consts[:, C_OM:C_OM + D]

        na_mask = view(consts, C_NM, NT, SEQ)
        mrope = view(consts, C_MR, NT, 2, ROPE)
        omask = view(consts, C_OM, NT, 512)
        orope = view(consts, C_OR, NT, 2, HD)
        gmask = consts[:, C_GM:C_GM + 2 * P].bitcast(U32).rearrange("p (z i) -> p z i", z=2)

        names = """c_loaded vecs_loaded consts_loaded x_loaded ctx_loaded small_loaded gate_w_loaded table_copied bias_loaded final_loaded stored
            pool_zeroed zero_ready dve_init vec_ps vec_cols silu_done mod_sum pool_sum mod_used mod_cols eff_ready
            std_ready xn_ready xT_ps hT_act hT_dve
            glr_ps glr_ready gate_ps gate_in gate_ln gate_sum exp_b decay_ready d_ready exp_d kd_ready ke_ready
            proj_ps proj_out silu_r gr_ready keT_ps keT_act keT_dve sT_ps sT_ready upd_ps state_ready inter_ps o_ps o_std og_ready
            ogT_ps ogT_act ogT_dve rows_ps rows_ready y_ps y_half y_std res_ready
            hiU_ready loU_ready hiD_ready loD_ready od_hi od_lo hT_hi hT_lo
            ff_ps ff_act ff_mid
            c_ps c_std c_ready cT_ps cT_act cT_dve kpe_ready qk_ps qk_act qk_dve vn_ps vn_act vn_dve
            mk_ps mk_out mv_ps mv_out mq_ps mq_rot mqT_ps mqT_out bias_ready
            s_ps max_ready prob_ready pT_ps pT_ready pv_ps o_out
            od_ps od_raw od_v rot_ready qkT_ps qkT_out out_ready
            w_used out_used act_chain dve_chain pool_chain""".split()
        s = {n: sem(n) for n in names}

        class Load:
            pass

        loads, landed = [], {}

        def plan(key, at, parts, free, ring=None):
            e = Load()
            size = sum(int(np.prod(sh)) for _, sh, _ in parts)
            assert at + size <= POOL, key
            e.at, e.size, e.parts, e.free = at, size, parts, free
            name = ring or f"w_{key}"
            if name not in landed:
                landed[name] = [sem(name), 0]
            landed[name][1] += 16 * len(parts)
            e.sem, e.value = landed[name][0], landed[name][1]
            e.after = {}
            for b in loads:
                if b.at < at + size and at < b.at + b.size:
                    e.after[b.free[0]] = max(b.free[1], e.after.get(b.free[0], 0))
            loads.append(e)
            return e

        def pv(e, i=0):
            off, sh, _ = e.parts[i]
            return view(pool, e.at + off, *sh)

        mod_v = a["mod_w"][0].rearrange("(k p) (s c) -> p k s c", p=P, c=512)
        gin = a["gla_w_in"][0].rearrange("(k p) n -> p k n", p=P)
        gout = a["gla_w_out"][0].rearrange("(k p) n -> p k n", p=P)
        fin = a["ffn_w_in"][0].rearrange("(k p) (g f c) -> p k g f c", p=P, g=2, c=P)
        fout = a["ffn_w_out"][0].rearrange("(f p) n -> p f n", p=P)
        evin = a["ev_w_in_2"][0].rearrange("(k p) n -> p k n", p=P)
        uq = a["ev_w_uq_2"][0].rearrange("(k p) n -> p k n", p=P)
        ukv = a["ev_w_ukv_2"][0].rearrange("(k p) n -> p k n", p=P)
        evo = a["ev_w_o_2"][0].rearrange("(k p) n -> p k n", p=P)
        odin = a["od_w_in_2"][0].rearrange("(k p) (g j m c) -> p k g j m c", p=P, g=3, j=3, c=P)
        odo = a["od_w_o_2"][0].rearrange("(k p) n -> p k n", p=P)
        w1v = a["mlp_w1_2"].rearrange("l (k p) (s c) -> l p k s c", p=P, c=256)
        w2v = a["mlp_w2_2"].rearrange("l (s f p) n -> l p s f n", p=P, f=2)

        W4 = [0, 4096, 8192, 12288]
        MOD_AT = {4: 2, 5: 2, 6: 3, 7: 2, 9: 0, 11: 1, 8: 3, 10: 3}
        L = {}
        n = 0
        for i in range(4):
            L["mod", i] = plan(f"mod{i}", W4[i], [(0, (KD, 512), mod_v[:, :, i, :])], ("mod_used", i + 1), ring=f"w_ring{i}")
        seq = [("k", 2, 512, 256), ("q", 2, 0, 256), ("v", 2, 1024, 512), ("r", 2, 2048, 512)]
        ofs = 16384
        for key, cnt, col, w in seq:
            for i in range(cnt):
                at = {"k": (16384, 0), "q": (2048, 4096), "v": (8192, 12288), "r": (0, 4096)}[key][i]
                L[key, i] = plan(f"gla_{key}{i}", at, [(0, (KD, w), gin[:, :, col + i * w:col + i * w + w])],
                                 ("proj_ps", {"k": 2, "q": 6, "v": 12, "r": 18}[key] + {"k": 2, "q": 2, "v": 4, "r": 2}[key] * i))

        def summed(i):
            return ("pool_sum", MOD_POOL.index(i) + 1) if i in MOD_POOL else ("mod_sum", i + 1 - sum(g < i for g in MOD_POOL))

        for i, at in MOD_AT.items():
            L["mod", i] = plan(f"mod{i}", W4[at], [(0, (KD, 512), mod_v[:, :, i, :])], summed(i), ring=f"w_ring{at}")
        plan("mod_sums", 16384, [(0, (2048,), None)], ("mod_used", 5))
        for i in range(2):
            L["go", i] = plan(f"gla_out{i}", [8192, 12288][i], [(0, (4, D), gout[:, 4 * i:4 * i + 4, :])], ("out_used", i + 1))
        FB = 3072
        L["ffn"] = []
        for f in range(FFC):
            L["ffn"].append(plan(f"ffn{f % FF_RING}", FB * (f % FF_RING),
                                 [(0, (KD, P), fin[:, :, 0, f, :]), (1024, (KD, P), fin[:, :, 1, f, :]),
                                  (2048, (D,), fout[:, f, :])], ("loD_ready", f + 1), ring=f"w_ffn{f % FF_RING}"))
        L["c"] = plan("ev_c", 12288, [(0, (KD, 416), evin[:, :, 1536:1952])], ("c_ps", 2))
        for i in range(4):
            L["qk", i] = plan(f"ev_qk{i}", (15616, 0, 2048, 4096)[i], [(0, (KD, 256), evin[:, :, 256 * i:256 * i + 256])], ("qk_ps", 2 * i + 2))
        L["va"] = plan("ev_v", 6144, [(0, (KD, 512), evin[:, :, 1024:1536])], ("vn_ps", 2))
        L["ukv"] = plan("ev_ukv", 10240, [(0, (1, 1024), ukv)], ("mv_ps", 2))
        L["uq"] = plan("ev_uq", 11264, [(0, (2, 768), uq)], ("mq_ps", 4))
        for i in range(2):
            L["eo", i] = plan(f"ev_out{i}", [8192, 12288][i], [(0, (4, D), evo[:, 4 * i:4 * i + 4, :])], ("out_used", i + 3))

        def plan_mlp(l):
            L["mlp", l] = []
            for st in range(MLP_RING * MLP_LOOPS):
                L["mlp", l].append(plan(f"mlp{l}_{st}", 4096 * ((st + 2 * l) % MLP_RING),
                                        [(0, (KD, 256), w1v[l][:, :, st, :]), (2048, (2, D), w2v[l][:, st, :, :])],
                                        ("loD_ready", FFC + 16 * l + st + 1),
                                        ring=f"w_mlp{st % MLP_RING}"))

        plan_mlp(0)
        L["od"] = [plan(f"od{g}", 3072 * g, [(1024 * j, (KD, P), odin[:, :, g, j, m, :]) for j in range(3)],
                        ("od_lo", 3 * m + g + 1), ring=f"w_od{g}") for m in range(OD_PAIRS) for g in range(3)]
        plan("od_split", 9216, [(0, (6144,), None)], ("od_ps", 6 * OD_PAIRS))
        for i in range(2):
            L["oo", i] = plan(f"od_out{i}", [0, 4096][i], [(0, (4, D), odo[:, 4 * i:4 * i + 4, :])], ("out_used", i + 5))
        plan_mlp(1)

        class Chain:
            def __init__(self, eng, count):
                self.eng, self.count, self.base, self.k = eng, count, 0, 0

            def __call__(self, ins):
                ins.then_inc(self.count, 1)
                self.k += 1
                self.eng.wait_ge(self.count, self.base + self.k)

            def enter(self, i, per):
                self.saved, self.per = self.base + self.k, per
                self.base, self.k = self.saved + i * per, 0

            def leave(self, times):
                assert self.k == self.per, self.k
                self.base, self.k = self.saved + times * self.per, 0

        OUT_BANK = ((0, 1), (2, 7))

        def turned_bank(n, b):
            return bank[4 * n + b] if n < 2 else bank[(5, 4, 7, 6)[b]]

        K_ORDER = (2, 3, 0, 1, 6, 7, 4, 5)

        def y_done(n):
            return (s["y_ps"], n // 2 + 1) if n % 2 else (s["out_used"], n + 2)

        def chunk_of(z, j):
            return j if z == 0 else (3 - j if j < 4 else 11 - j)

        block = ctx.enter_context(nc.Block())
        NS = 96
        U_OD = NA_H + MLA_H

        @block.sync
        def _(sp):
            def fetch(e):
                for name, value in e.after.items():
                    sp.wait_ge(s[name], value)
                for off, sh, src in e.parts:
                    sp.dma_start(view(pool, e.at + off, *sh), src).then_inc(e.sem, 16)

            def fetch_ring(bundles, ring, parts_of):
                for e in bundles[:ring]:
                    fetch(e)
                rounds = len(bundles) // ring
                with sp.Fori(0, rounds - 1) as i:
                    for j in range(ring):
                        e = bundles[j]
                        sp.wait_ge(s[e.free[0]], i * ring + e.free[1])
                        for (off, sh, _), src in zip(e.parts, parts_of(i + 1, j)):
                            sp.dma_start(view(pool, e.at + off, *sh), src).then_inc(e.sem, 16)
                for e in bundles[rounds * ring:]:
                    fetch(e)

            sp.dma_start(consts[:, 0:P], a["consts"][:, 0:P]).then_inc(s["consts_loaded"], 16)
            sp.wait_ge(s["c_loaded"], 32)
            for i in range(4):
                fetch(L["mod", i])
            for key, cnt, _, _ in seq:
                for i in range(cnt):
                    fetch(L[key, i])
            sp.dma_start(consts[:, P:], a["consts"][:, P:]).then_inc(s["consts_loaded"], 16)
            for i in MOD_AT:
                fetch(L["mod", i])
            for i in range(2):
                fetch(L["go", i])
            fetch_ring(L["ffn"], FF_RING, lambda r, j: (fin[:, :, 0, r * FF_RING + j, :], fin[:, :, 1, r * FF_RING + j, :],
                                                     fout[:, r * FF_RING + j, :]))
            for key in ["c", ("qk", 0), ("qk", 1), ("qk", 2), ("qk", 3), "va", "ukv", "uq", ("eo", 0), ("eo", 1)]:
                fetch(L[key])
            fetch_ring(L["mlp", 0], MLP_RING, lambda r, j: (w1v[0][:, :, r * MLP_RING + j, :], w2v[0][:, r * MLP_RING + j, :, :]))
            fetch_ring(L["od"], 3, lambda m, g: [odin[:, :, g, j, m, :] for j in range(3)])
            fetch(L["oo", 0])
            fetch(L["oo", 1])
            fetch_ring(L["mlp", 1], MLP_RING, lambda r, j: (w1v[1][:, :, r * MLP_RING + j, :], w2v[1][:, r * MLP_RING + j, :, :]))
            for t in range(NT):
                sp.wait_ge(s["out_ready"], t + 1)
                sp.dma_start(out[0, t * P:t * P + P, :], xn[:, t, :]).then_inc(s["stored"], 16)
            sp.wait_ge(s["stored"], 16 * NT)

        @block.gpsimd
        def _(g):
            g.memset(ones[:, :], 1.0).then_inc(s["zero_ready"], 1)
            g.memset(work[0:2 * RANK, 10240:10240 + 2 * GLA_QK], 0.0).then_inc(s["pool_zeroed"], 1)
            g.memset(zero[:, :], 0.0).then_inc(s["zero_ready"], 1)
            g.dma_start(skew, a["ev_rpb_2"].rearrange("o h r c -> o (h r c)").to_broadcast([GRID, RPB])).then_inc(s["table_copied"], 16)

            g.wait_ge(s["silu_done"], 2)
            g.wait_ge(s["xT_ps"], 4)
            for n, i in enumerate(MOD_POOL):
                e = L["mod", i]
                g.wait_ge(e.sem, e.value)
                dst, w = late_sum(i), pv(e)
                steps = [(w, w, silc[:, :, 0:1].to_broadcast([P, KD, 512]), ALU.mult), (w[:, 0:4], w[:, 0:4], w[:, 4:8], ALU.add),
                         (w[:, 0:2], w[:, 0:2], w[:, 2:4], ALU.add), (dst, w[:, 0, :], w[:, 1, :], ALU.add)]
                for k, (to, in0, in1, op) in enumerate(steps):
                    if k:
                        g.wait_ge(s["pool_chain"], 3 * n + k)
                    ins = g.tensor_tensor(to, in0, in1, op)
                    if k < 3:
                        ins.then_inc(s["pool_chain"], 1)
                ins.then_inc(s["pool_sum"], 1)
            g.wait_ge(s["small_loaded"], 32)
            g.wait_ge(s["silu_r"], 4)
            for t in range(NT):
                for h in range(GH):
                    v = rG[:, t, GDV * h:GDV * h + GDV]
                    g.tensor_tensor(v, v, gnrow[:, :], ALU.mult).then_inc(s["gr_ready"], 1)
            g.wait_ge(s["table_copied"], 16)
            g.wait_ge(s["y_ps"], 1)
            for t in range(NT):
                for hf in range(2):
                    r = 2 * t + hf
                    for rk in range(4):
                        src = bass.AP(skew.tensor, (rk - r + 7) * 31 + 15, [[RPB - 1, GRID], [15 * 31, NA_H], [1, GRID]])
                        g.dma_start(nabias[GRID * hf:GRID * hf + GRID, :, t, GRID * rk:GRID * rk + GRID], src)\
                         .then_inc(s["bias_loaded"], 16)
            g.wait_ge(s["bias_loaded"], 16 * 16)
            g.wait_ge(s["consts_loaded"], 32)
            for h in range(NA_H):
                g.tensor_tensor(nabias[:, h], nabias[:, h], na_mask, ALU.add).then_inc(s["bias_ready"], 1)
            g.wait_ge(s["o_out"], 4 + OD_PAIRS)
            g.dma_start(frow, a["norm_final_2"].partition_broadcast(P)).then_inc(s["final_loaded"], 16)

        @block.scalar
        def _(act):
            chain = Chain(act, s["act_chain"])

            for at, src in [(VA_C, a["c"]), (VA_CC, a["c_ctx"].rearrange("(o n) -> o n", o=1)), (VA_NG, a["norm_g"][0]),
                            (VA_MB, a["mod_b"]), (VA_QN, a["ev_q_norm_2"]), (VA_KN, a["ev_kv_norm_2"]),
                            (VA_BG, a["gla_b_gate"][0])]:
                o, n = src.shape
                act.dma_start(vec_rows(at, o * n // P), src.rearrange("o (r p) -> (o r) p", p=P))\
                   .then_inc(s["c_loaded" if at < VA_NG else "vecs_loaded"], 16)
            for at, src in [(VB_MIX, a["norm_mix_2"]), (VB_MLP, a["norm_mlp_2"])]:
                act.dma_start(hTs[at:at + 16, 2 * P:3 * P], src.rearrange("o (r p) -> (o r) p", p=P)).then_inc(s["vecs_loaded"], 16)
            act.dma_start(xn[:, :, :], a["ctx"][0].rearrange("(t p) d -> p t d", p=P)).then_inc(s["ctx_loaded"], 16)
            act.dma_start(res[:, :, :], a["x"][0].rearrange("(t p) d -> p t d", p=P)).then_inc(s["x_loaded"], 16)
            act.dma_start(wglr[:, :, :], gin[:, :, 3072:3104]).then_inc(s["small_loaded"], 16)
            act.dma_start(gnrow[:, :], a["gla_norm_g"][0].partition_broadcast(P)).then_inc(s["small_loaded"], 16)
            act.wait_ge(s["pool_zeroed"], 1)
            for z in range(2):
                act.dma_start(work[z * RANK:(z + 1) * RANK, 10240 + z * GLA_QK:10240 + (z + 1) * GLA_QK],
                              a["gla_w_gate"][0, z]).then_inc(s["gate_w_loaded"], 16)

            act.wait_ge(s["vec_cols"], 1)
            for j in range(2):
                act.activation(silc[:, :, j], vecA[:, 8 * j:8 * j + 8], ACT.Silu).then_inc(s["silu_done"], 1)
            act.wait_ge(s["dve_init"], 1)

            def norm_stats(n, src, ready, count, before=None):
                junk = work[:, 0:D] if n < 2 else work[:, 20480:20480 + D]
                for t in range(NT):
                    if before:
                        before(t)
                    act.wait_ge(ready, count if n < 2 else count - 1 + t)
                    at = NS + 6 * n + t
                    chain(act.activation(junk, src[:, t, :], ACT.Square, accum_out=stat[:, at:at + 1]))
                    act.activation(stat[:, at + 2:at + 3], stat[:, at:at + 1], ACT.Sqrt, bias=eps, scale=1.0 / D).then_inc(s["std_ready"], 1)

            def norm_evac(n, dst, gain, shift, order=by_sma, split=False):
                for b in (0, 2):
                    act.wait_ge(s["xT_ps"], 4 * n + b + 1)
                    for k in (2 * b, 2 * b + 1):
                        src = turned_bank(n, b)[:, 256 * (k - 2 * b):256 * (k - 2 * b) + 256]
                        ins = act.activation(by_sma(dst(k)), order(src), ACT.Identity, scale=gain(k),
                                             bias=shift(k) if shift else 0.0)
                    ins.then_inc(s["hT_act"], 1)
                    if split:
                        for k in (2 * b, 2 * b + 1):
                            src = turned_bank(n, b)[:, 256 * (k - 2 * b):256 * (k - 2 * b) + 256]
                            ins = act.activation(by_sma(hT2[0][:, k, :]), order(src), ACT.Identity, scale=gain(k),
                                                 bias=shift(k) if shift else 0.0)
                        ins.then_inc(s["hT_hi"], 1)

            def high(dst, e, off, landed_at, done):
                act.wait_ge(e.sem, landed_at)
                act.activation(dst[:, :], pool[:, e.at + off:e.at + off + dst.shape[1]], ACT.Copy).then_inc(s[done], 1)

            norm_stats(0, xn, s["ctx_loaded"], 16)
            norm_stats(1, res, s["x_loaded"], 16)
            act.wait_ge(s["eff_ready"], 2)
            norm_evac(0, lambda k: hT_all[:, k, 0:256], lambda k: eff[:, 0, k:k + 1], lambda k: mods[:, k, 1:2])
            norm_evac(1, lambda k: hT_all[:, k, 256:512], lambda k: eff[:, 1, k:k + 1], lambda k: mods[:, k, 0:1])

            for zh in range(8):
                z, h = zh // GH, zh % GH
                act.wait_ge(s["gate_ps"], zh + 1)
                act.activation(G1[:, z, h, :], bank[1 + zh % 4][:, :], ACT.Identity, bias=vecA[:, VA_BG + zh:VA_BG + zh + 1])\
                   .then_inc(s["gate_in"], 1)
            act.wait_ge(s["gate_in"], 8)
            for z in range(2):
                chain(act.activation(G2[:, z], G1[:, z], ACT.Abs))
                chain(act.activation(G2[:, z], G2[:, z], ACT.Exp, scale=-1.0))
                act.activation(G2[:, z], G2[:, z], ACT.Ln, bias=1.0).then_inc(s["gate_ln"], 1)
            for z in range(2):
                act.wait_ge(s["gate_sum"], z + 1)
                act.activation(qd[:, z], G2[:, z, :, 256:512], ACT.Exp, scale=1.0 / GATE_NORM)\
                   .then_inc(s["exp_b"], 1)
                act.activation(kd[:, z], G2[:, z, :, 256:512], ACT.Exp, scale=-1.0 / GATE_NORM).then_inc(s["exp_b"], 1)
                act.activation(decay[:, 32 * z:32 * z + 32], bend[:, 32 * z:32 * z + 32], ACT.Exp, scale=1.0 / GATE_NORM)\
                   .then_inc(s["decay_ready"], 1)
                act.wait_ge(s["d_ready"], z + 1)
                act.activation(G1[:, z], G1[:, z], ACT.Exp, scale=1.0 / GATE_NORM).then_inc(s["exp_d"], 1)
            act.wait_ge(s["gate_sum"], 2)
            for j in range(4):
                act.wait_ge(s["proj_ps"], 17 + j)
                act.activation(rG[:, j % 2, 512 * (j // 2):512 * (j // 2) + 512], bank[5 + (16 + j) % 3][:, :], ACT.Silu)\
                   .then_inc(s["silu_r"], 1)
            for zh in range(1, 8, 2):
                act.wait_ge(s["keT_ps"], zh + 1)
                act.activation(keT[:, zh // GH, zh % GH], bank[zh % 4][:, :].rearrange("p (t d) -> p t d", t=4), ACT.Copy)\
                   .then_inc(s["keT_act"], 1)
            act.wait_ge(s["o_ps"], 1)
            for t in range(NT):
                for h in range(GH):
                    chain(act.activation(work[:, 20480 - 5 * 1024:20480 - 5 * 1024 + GDV],
                                         bank[2 * t + h // 2][:, GDV * (h % 2):GDV * (h % 2) + GDV], ACT.Square,
                                         accum_out=stat[:, 16 + 4 * t + h:17 + 4 * t + h]))
            act.activation(stat[:, 24:32], stat[:, 16:24], ACT.Sqrt, bias=eps, scale=1.0 / GDV).then_inc(s["o_std"], 1)

            def turn_evac(n, dst, order):
                for b in (0, 2):
                    act.wait_ge(s["ogT_ps"], 4 * n + b + 1)
                    for k in (2 * b, 2 * b + 1):
                        ins = act.activation(order(dst[:, k, :]), by_sma(bank[4 + b][:, 256 * (k - 2 * b):256 * (k - 2 * b) + 256]), ACT.Copy)
                    ins.then_inc(s["ogT_act"], 1)

            turn_evac(0, ogT, by_sma)
            ffn = L["ffn"]
            act.wait_ge(s["og_ready"], 2)
            high(ffU[0][0], ffn[0], 0, ffn[0].value, "hiU_ready")
            high(ffD[0][0], ffn[0], 2048, ffn[0].value, "hiD_ready")

            def y_stats(n, t):
                act.wait_ge(*((s["y_half"], n + 1) if t == 0 else y_done(n)))
                for b in (2 * t, 2 * t + 1):
                    chain(act.activation(xn[:, t, 512 * (b % 2):512 * (b % 2) + 512], bank[b][:, :], ACT.Square, accum_out=stat[:, 32 + b:33 + b]))
                chain(act.activation(stat[:, 36 + t:37 + t], stat[:, 33 + 2 * t:34 + 2 * t], ACT.Identity, bias=eps, scale=1.0 / D))
                act.activation(stat[:, 38 + t:39 + t], stat[:, 32 + 2 * t:33 + 2 * t], ACT.Sqrt, bias=stat[:, 36 + t:37 + t], scale=1.0 / D)\
                   .then_inc(s["y_std"], 1)

            norm_stats(2, res, s["res_ready"], 2, before=lambda t: y_stats(0, t))
            act.wait_ge(s["eff_ready"], 5)
            norm_evac(2, lambda k: normT[:, k, :], lambda k: eff[:, 2, k:k + 1], lambda k: mods[:, 3 * KD + k, 0:1], split=True)

            act.wait_ge(s["out_used"], 2)
            high(ffU[1][0], ffn[1], 0, ffn[1].value, "hiU_ready")

            def ffn_step(f, j, n_up, n_down, landed_at):
                act.wait_ge(s["ff_ps"], f + 1)
                if not isinstance(f, int) or f >= 2:
                    act.wait_ge(s["ff_mid"], f - 1)
                act.activation(act_a[:, j % 2, 0:256], bank[4 + j % 2][:, 0:256], ACT.Silu).then_inc(s["ff_act"], 1)
                if n_up:
                    e = ffn[(j + 2) % FF_RING]
                    high(ffU[j % 2][0], e, 0, landed_at + STEP_F * ((j + 2) // FF_RING), "hiU_ready")
                if n_down:
                    if not isinstance(f, int) or f >= 1:
                        act.wait_ge(s["w_used"], f)
                    e = ffn[(j + 1) % FF_RING]
                    high(ffD[(j + 1) % 2][0], e, 2048, landed_at + STEP_F * ((j + 1) // FF_RING), "hiD_ready")

            STEP_F = 16 * 3
            for f in range(FF_RING):
                ffn_step(f, f, True, True, STEP_F)
            with act.Fori(0, FF_LOOPS - 1) as i:
                for j in range(FF_RING):
                    ffn_step(i * FF_RING + (FF_RING + j), j, True, True, i * STEP_F + 2 * STEP_F)
            for f in range(FF_LOOPS * FF_RING, FFC):
                ffn_step(f, f % FF_RING, f + 2 < FFC, f + 1 < FFC, (FF_LOOPS + 1) * STEP_F)

            norm_stats(3, res, s["res_ready"], 4, before=lambda t: y_stats(1, t))
            norm_evac(3, lambda k: hT[:, k, :], lambda k: vecB[:, VB_MIX + k:VB_MIX + k + 1], None)
            for t in range(NT):
                act.wait_ge(s["c_ps"], t + 1)
                chain(act.activation(score[:, 0, 0:256], bank[4 + t][:, 0:QR], ACT.Square, accum_out=stat[:, 40 + t:41 + t]))
                chain(act.activation(score[:, 0, 0:128], bank[4 + t][:, QR:QR + KVR], ACT.Square, accum_out=stat[:, 42 + t:43 + t]))
            act.activation(stat[:, 44:46], stat[:, 40:42], ACT.Sqrt, bias=eps, scale=1.0 / QR).then_inc(s["c_std"], 1)
            act.activation(stat[:, 46:48], stat[:, 42:44], ACT.Sqrt, bias=eps, scale=1.0 / KVR).then_inc(s["c_std"], 1)
            for c in range(1, 8, 2):
                act.wait_ge(s["qk_ps"], c + 1)
                act.activation(qkN[:, c, :], bank[7][:, 0:256], ACT.Copy).then_inc(s["qk_act"], 1)
            act.wait_ge(s["vn_ps"], 2)
            act.activation(vN[:, 1, :], bank[7][:, :], ACT.Copy).then_inc(s["vn_act"], 1)
            act.wait_ge(s["cT_ps"], 1)
            for k in range(2):
                act.activation(cT[:, k, :], bank[4][:, 256 * k:256 * k + 256], ACT.Copy,
                               scale=vecA[:, VA_QN + k:VA_QN + k + 1]).then_inc(s["cT_act"], 1)
            for h in range(MLA_H):
                act.wait_ge(s["mk_ps"], h // 2 + 1)
                act.activation(kM[0:NOPE, h, :], bank[4 + h // 2][0:NOPE, 256 * (h % 2):256 * (h % 2) + 256], ACT.Copy)\
                   .then_inc(s["mk_out"], 1)
            for t in range(NT):
                act.wait_ge(s["mv_ps"], t + 1)
                act.activation(vM[:, t, :], bank[4 + t][:, :], ACT.Copy).then_inc(s["mv_out"], 1)

            def exp_unit(u, j, halves, scale, col):
                act.wait_ge(s["max_ready"], u + 1)
                if not isinstance(u, int) or u >= 2:
                    act.wait_ge(s["pT_ps"], u - 1)
                w = 512 // halves
                for h in range(halves):
                    src = score[:, j % 2, h * w:h * w + w] if scale == 1.0 else bank[3 + j % 2][:, h * w:h * w + w]
                    ins = act.activation(prob[:, j % 2, h * w:h * w + w], src, ACT.Exp, scale=scale,
                                         bias=stat[:, 48 + 2 * (j % 4) + h:49 + 2 * (j % 4) + h], accum_out=col(h))
                ins.then_inc(s["prob_ready"], 1)

            def turned_unit(u, j):
                act.wait_ge(s["pT_ps"], u + 1)
                if not isinstance(u, int) or u >= 2:
                    act.wait_ge(s["pv_ps"], u - 1)
                act.activation(probT[:, j % 2, :], bank[5 + j % 2][:, :], ACT.Copy).then_inc(s["pT_ready"], 1)

            for u in range(U_OD + 1):
                if u < U_OD:
                    exp_unit(u, u, 2, 1.0 if u < NA_H else MQ ** -0.5, lambda h: rsum[:, 16 * h + u:16 * h + u + 1])
                if u >= 1:
                    turned_unit(u - 1, u - 1)
            turn_evac(1, oT, by_sma)

            def mlp_first(l):
                e = L["mlp", l]
                high(mlU[0][0], e[0], 0, e[0].value, "hiU_ready")
                high(mlD[0][0], e[0], 2048, e[0].value, "hiD_ready")
                high(mlU[1][0], e[1], 0, e[1].value, "hiU_ready")

            act.wait_ge(s["o_out"], 4)
            mlp_first(0)
            norm_stats(4, res, s["res_ready"], 6)
            norm_evac(4, lambda k: normT[:, k, :], lambda k: vecB[:, VB_MLP + k:VB_MLP + k + 1], None, split=True)

            def mlp(l):
                first, per = L["mlp", l], 16 * 2

                def step(r, j, n_up, n_down):
                    st = r * MLP_RING + (FFC + 16 * l + j)
                    act.wait_ge(s["ff_ps"], st + 1)
                    act.wait_ge(s["ff_mid"], st - 1)
                    act.activation(act_a[:, j % 2, :], bank[4 + j % 2][:, :], ACT.Relu).then_inc(s["ff_act"], 1)
                    if n_up:
                        e = first[(j + 2) % MLP_RING]
                        high(mlU[j % 2][0], e, 0, r * per + (e.value + per * ((j + 2) // MLP_RING)), "hiU_ready")
                    if n_down:
                        act.wait_ge(s["w_used"], st)
                        e = first[(j + 1) % MLP_RING]
                        high(mlD[(j + 1) % 2][0], e, 2048, r * per + (e.value + per * ((j + 1) // MLP_RING)), "hiD_ready")

                with act.Fori(0, MLP_LOOPS - 1) as i:
                    for j in range(MLP_RING):
                        step(i, j, True, True)
                for j in range(MLP_RING):
                    step(MLP_LOOPS - 1, j, j + 2 < MLP_RING, j + 1 < MLP_RING)

            mlp(0)

            def od_high(m, par, g, free):
                act.wait_ge(s[free[0]], free[1])
                high(odW[(3 * par + g) % 2][0], L["od"][g], 0, 48 * m + 48, "od_hi")

            od_high(0, 0, 0, ("loD_ready", FFC + 16))
            norm_stats(5, res, s["res_ready"], 8)
            norm_evac(5, lambda k: normT[:, k, :], lambda k: vecB[:, VB_MIX + 8 + k:VB_MIX + 9 + k], None, order=dilated, split=True)

            def od_values(m, par, g, t):
                act.wait_ge(s["od_ps"], 6 * m + (2 * g + t + 1))
                if g == 0 and t == 0:
                    act.wait_ge(s["pv_ps"], 4 * m + (U_OD - 4))
                if not isinstance(m, int) or m or g:
                    act.wait_ge(s["rot_ready"], 6 * m + (2 * g + t - 1))
                act.activation(raw[:, t, :], bank[t][:, 0:256], ACT.Copy).then_inc(s["od_raw"], 1)
                act.activation(vO[:, par, g, t, :], bank[t][:, 256:384], ACT.Copy).then_inc(s["od_v"], 1)

            def od_turned(m, par, g):
                act.wait_ge(s["qkT_ps"], 3 * m + (g + 1))
                act.activation(qkT[:, par, g, :], bank[2][:, :], ACT.Copy).then_inc(s["qkT_out"], 1)

            def od_col(par, j):
                return lambda h: rsum[:, 32 + 4 * par + 2 * (j % 2) + j // 2:33 + 4 * par + 2 * (j % 2) + j // 2]

            def od_pair(m, n, pm, pn):
                u = None if n is None else 4 * n + U_OD
                if m is not None:
                    od_high(m, pm, 1, ("w_used", FFC + 16) if isinstance(m, int) and m == 0 else ("od_ps", 6 * m))
                    od_values(m, pm, 0, 0)
                    od_values(m, pm, 0, 1)
                if n is not None:
                    od_turned(n, pn, 2)
                if m is not None:
                    od_high(m, pm, 2, ("od_ps", 6 * m + 2))
                    od_values(m, pm, 1, 0)
                    od_values(m, pm, 1, 1)
                if n is not None:
                    exp_unit(u + 0, 0, 1, 1.0, od_col(pn, 0))
                    exp_unit(u + 1, 1, 1, 1.0, od_col(pn, 1))
                if m is not None:
                    od_turned(m, pm, 0)
                    if not isinstance(m, int) or m < OD_PAIRS - 1:
                        od_high(m + 1, 1 - pm, 0, ("od_ps", 6 * m + 4))
                    od_values(m, pm, 2, 0)
                if n is not None:
                    turned_unit(u + 0, 0)
                    turned_unit(u + 1, 1)
                    exp_unit(u + 2, 2, 1, 1.0, od_col(pn, 2))
                    exp_unit(u + 3, 3, 1, 1.0, od_col(pn, 3))
                if m is not None:
                    od_values(m, pm, 2, 1)
                if n is not None:
                    turned_unit(u + 2, 2)
                    turned_unit(u + 3, 3)
                if m is not None:
                    od_turned(m, pm, 1)

            od_pair(0, None, 0, None)
            with act.Fori(0, OD_PAIRS // 2 - 1) as i:
                od_pair(2 * i + 1, 2 * i, 1, 0)
                od_pair(2 * i + 2, 2 * i + 1, 0, 1)
            od_pair(OD_PAIRS - 1, OD_PAIRS - 2, 1, 0)
            od_pair(None, OD_PAIRS - 1, None, 1)
            turn_evac(2, oT, dilated)
            mlp_first(1)
            norm_stats(6, res, s["res_ready"], 10)
            norm_evac(6, lambda k: normT[:, k, :], lambda k: vecB[:, VB_MLP + 8 + k:VB_MLP + 9 + k], None, split=True)
            mlp(1)
            norm_stats(7, res, s["res_ready"], 12)

        @block.vector
        def _(dve):
            chain = Chain(dve, s["dve_chain"])
            dve.memset(stat[:, 90:91], EPS).then_inc(s["dve_init"], 1)
            dve.wait_ge(s["vec_ps"], 1)
            dve.tensor_copy(vecA[:, 0:VA_NG], bank[4][:, 0:VA_NG]).then_inc(s["vec_cols"], 1)

            def norm_scale(n, src, dst, before=None):
                at = NS + 6 * n
                for t in range(NT):
                    if before:
                        before(t)
                    dve.wait_ge(s["std_ready"], 2 * n + t + 1)
                    chain(dve.reciprocal(stat[:, at + 4 + t:at + 5 + t], stat[:, at + 2 + t:at + 3 + t]))
                    if n > 1 and t == 0:
                        dve.wait_ge(s["xT_ps"], 4 * n)
                    if n == 7:
                        dve.scalar_tensor_tensor(out=dst[:, t, :], in0=src[:, t, :], scalar=stat[:, at + 4 + t:at + 5 + t],
                                                 in1=frow, op0=ALU.mult, op1=ALU.mult).then_inc(s["out_ready"], 1)
                    else:
                        dve.tensor_scalar(dst[:, t, :], src[:, t, :], stat[:, at + 4 + t:at + 5 + t], None, ALU.mult)\
                           .then_inc(s["xn_ready"], 1)

            def norm_evac(n, dst, gain, shift, order=by_sma, split=False):
                for b in (1, 3):
                    dve.wait_ge(s["xT_ps"], 4 * n + b + 1)
                    for high in ((False, True) if split else (False,)):
                        for k in (2 * b, 2 * b + 1):
                            src, to = turned_bank(n, b)[:, 256 * (k - 2 * b):256 * (k - 2 * b) + 256], hT2[0][:, k, :] if high else dst(k)
                            if shift:
                                ins = dve.tensor_scalar(to, src, gain(k), shift(k), ALU.mult, ALU.add)
                            else:
                                ins = dve.tensor_scalar(by_sma(to), order(src), gain(k), None, ALU.mult)
                        if not high:
                            ins.then_inc(s["hT_dve"], 1)
                    if split:
                        chain(ins)
                        low(hT2[1][:, 2 * b:2 * b + 2, :], normT[:, 2 * b:2 * b + 2, :], hT2[0][:, 2 * b:2 * b + 2, :], "hT_lo")
                        r = (2, 4, 5, 6).index(n)
                        dve.wait_ge(s["hT_hi"], 2 * r + (b + 1) // 2)
                        low(hT2[1][:, 2 * b - 2:2 * b, :], normT[:, 2 * b - 2:2 * b, :], hT2[0][:, 2 * b - 2:2 * b, :], "hT_lo")

            def low(dst, whole, high, done):
                dve.tensor_tensor(dst, whole, high.bitcast(F32), ALU.subtract).then_inc(s[done], 1)

            def low_weights(pair, e, off, hi, count, done):
                dve.wait_ge(s[hi], count)
                low(pair[1][:, :], pool[:, e.at + off:e.at + off + pair[1].shape[1]], pair[0][:, :], done)

            def mod_sum(i, chunks, conditions, dst, part=None):
                e = L["mod", i]
                w = pv(e)
                for k in part or range(chunks):
                    if k == 0:
                        dve.wait_ge(e.sem, e.value)
                    for j in range(conditions):
                        if k == 0:
                            ins = dve.tensor_scalar(dst(j), w[:, k, :], silc[:, k, j:j + 1], None, ALU.mult)
                        else:
                            dve.wait_ge(s["dve_chain"], chain.base + chain.k - (conditions - 1))
                            ins = dve.scalar_tensor_tensor(out=dst(j), in0=w[:, k, :], scalar=silc[:, k, j:j + 1], in1=dst(j),
                                                           op0=ALU.mult, op1=ALU.add)
                        if k < chunks - 1 or j < conditions - 1:
                            ins.then_inc(s["dve_chain"], 1)
                            chain.k += 1
                        else:
                            ins.then_inc(s["mod_sum"], 1)

            dve.wait_ge(s["silu_done"], 2)
            for i in range(4):
                mod_sum(i, MOD_DVE, 2, lambda j: first_sums[:, i, j, :])
                if i == 2:
                    norm_scale(0, xn, xn)
            norm_scale(1, res, rG)

            def mod_evac(lo, hi, conditions):
                v = bank[7][:, 0:2 * (hi - lo)].rearrange("p (m j) -> p m j", j=2)[:, :, 0:conditions]
                bias = vecA[:, VA_MB + lo:VA_MB + hi].unsqueeze(2).to_broadcast([P, hi - lo, conditions])
                dve.tensor_tensor(mods[:, lo:hi, 0:conditions], v, bias, ALU.add).then_inc(s["mod_cols"], 1)

            def eff_scale(i, m, j, g):
                dve.scalar_tensor_tensor(out=eff[:, i, :], in0=mods[:, KD * m:KD * m + KD, j], scalar=1.0,
                                         in1=vecA[:, VA_NG + KD * g:VA_NG + KD * g + KD], op0=ALU.add, op1=ALU.mult)\
                   .then_inc(s["eff_ready"], 1)

            dve.wait_ge(s["vec_ps"], 2)
            dve.tensor_copy(vecA[:, VA_NG:VA_N], bank[5][:, 0:VA_N - VA_NG]).then_inc(s["vec_cols"], 1)
            dve.wait_ge(s["vec_ps"], 3)
            dve.tensor_copy(vecB[:, :], bank[6][:, 0:VB_N]).then_inc(s["vec_cols"], 1)
            dve.wait_ge(s["vec_cols"], 3)
            dve.wait_ge(s["mod_used"], 4)
            mod_evac(0, 16, 2)
            dve.wait_ge(s["mod_cols"], 1)
            eff_scale(0, 1, 1, 0)
            eff_scale(1, 1, 0, 0)
            dve.wait_ge(s["eff_ready"], 2)
            norm_evac(0, lambda k: hT_all[:, k, 0:256], lambda k: eff[:, 0, k:k + 1], lambda k: mods[:, k, 1:2])
            norm_evac(1, lambda k: hT_all[:, k, 256:512], lambda k: eff[:, 1, k:k + 1], lambda k: mods[:, k, 0:1])
            dve.wait_ge(s["glr_ps"], 1)
            dve.tensor_copy(glrT, bank[0][0:2 * RANK, :]).then_inc(s["glr_ready"], 1)

            def proj(j):
                dve.wait_ge(s["proj_ps"], j + 1)
                b = bank[5 + j % 3]
                if j < 4:
                    ins = dve.tensor_copy(kT[:, j, :], b[:, :])
                elif j < 8:
                    ins = dve.tensor_scalar(qT[:, j - 4, :], b[:, 0:256], GDK ** -0.5, None, ALU.mult)
                else:
                    half, tile = (j - 8) // 4, (j - 8) % 4
                    ins = dve.tensor_copy(vG[:, tile, 512 * half:512 * half + 512], b[:, :])
                ins.then_inc(s["proj_out"], 1)

            def chunks(v):
                return v.rearrange("p h (c i) -> p (h c) i", i=CHUNK)

            def gates(z):
                dve.wait_ge(s["gate_ln"], z + 1)
                chain(dve.tensor_scalar(G1[:, z], G1[:, z], 0.0, None, ALU.min))
                chain(dve.tensor_tensor(G1[:, z], G1[:, z], G2[:, z], ALU.subtract))
                gin_, gout_ = (G[:, z].rearrange("p h t -> p (h t)") for G in (G1, G2))
                if z:
                    gin_, gout_ = gin_[:, ::-1], gout_[:, ::-1]
                chain(dve.tensor_tensor_scan(gout_, reset, gin_, 0.0, ALU.mult, ALU.add))
                last = 0 if z else CHUNK - 1
                dve.tensor_copy(bend[:, 32 * z:32 * z + 32], chunks(G2[:, z])[:, :, last]).then_inc(s["gate_sum"], 1)
                dve.wait_ge(s["gate_sum"], z + 1)
                dve.tensor_tensor(chunks(G1[:, z]), bend[:, 32 * z:32 * z + 32].unsqueeze(2).to_broadcast([P, 32, CHUNK]),
                                  chunks(G2[:, z]), ALU.subtract).then_inc(s["d_ready"], 1)

            def decayed(z):
                dve.wait_ge(s["exp_b"], 2 * z + 2)
                dve.wait_ge(s["proj_out"], 8)
                dve.tensor_tensor(qd[:, z], qd[:, z], qT, ALU.mult).then_inc(s["kd_ready"], 1)
                dve.tensor_tensor(kd[:, z], kd[:, z], kT[:, :, 256:512], ALU.mult).then_inc(s["kd_ready"], 1)
                dve.wait_ge(s["exp_d"], z + 1)
                dve.tensor_tensor(G1[:, z], G1[:, z], kT, ALU.mult).then_inc(s["ke_ready"], 1)

            for j in range(3):
                proj(j)
            dve.wait_ge(s["xT_ps"], 8)
            chain(dve.memset(reset, 1.0))
            chain(dve.memset(reset[:, ::CHUNK], 0.0))
            gates(0)
            proj(3)
            proj(4)
            gates(1)
            for j in range(5, 10):
                proj(j)
            decayed(0)
            for j in range(10, 12):
                proj(j)
            decayed(1)
            dve.wait_ge(s["ke_ready"], 2)
            dve.wait_ge(s["kd_ready"], 4)
            chain(dve.memset(work[:, 12288:14336], 0.0))
            for j in range(12, 14):
                proj(j)
            mod_sum(4, KD, 1, lambda j: late_sum(4))
            for j in range(14, 16):
                proj(j)
            mod_sum(5, KD, 1, lambda j: late_sum(5))
            dve.wait_ge(s["consts_loaded"], 32)
            for z in range(2):
                for u in range(2):
                    dve.wait_ge(s["sT_ps"], 2 * z + u + 1)
                    mask = consts[:, C_GM + P * z:C_GM + P * z + P].bitcast(U32).unsqueeze(1).to_broadcast([P, 4, P])
                    dve.copy_predicated(sT[:, z, u], mask, bank[4 + 2 * z + u][:, :].rearrange("p (a i) -> p a i", a=4))\
                       .then_inc(s["sT_ready"], 1)
                for zh in (4 * z, 4 * z + 2):
                    dve.wait_ge(s["keT_ps"], zh + 1)
                    dve.tensor_copy(keT[:, zh // GH, zh % GH], bank[zh % 4][:, :].rearrange("p (t d) -> p t d", t=4))\
                       .then_inc(s["keT_dve"], 1)
            for j in range(7):
                for z in range(2):
                    dve.wait_ge(s["upd_ps"], 2 * j + z + 1)
                    if j == 0 and z == 0:
                        dve.wait_ge(s["decay_ready"], 2)
                    if j >= 5:
                        dve.wait_ge(s["inter_ps"], 2 * (j - 5) + z + 1)
                    if j and z == 0:
                        dve.wait_ge(s["state_ready"], 2 * j)
                    for h in range(GH):
                        upd = bank[4 + 2 * z + h // 2][:, GDV * (h % 2):GDV * (h % 2) + GDV]
                        new = states[:, (j + 1) % 2, z, h, :]
                        if j == 0:
                            ins = dve.tensor_copy(new, upd)
                        else:
                            col = 32 * z + 8 * h + chunk_of(z, j)
                            ins = dve.scalar_tensor_tensor(out=new, in0=states[:, j % 2, z, h, :], scalar=decay[:, col:col + 1],
                                                           in1=upd, op0=ALU.mult, op1=ALU.add)
                    ins.then_inc(s["state_ready"], 1)
                for n in range(4 * (j - 1), 4 * j):
                    if j:
                        slot = (7, 9, 11)[n // KD]
                        mod_sum(slot, KD, 1, lambda _: late_sum(slot), part=[n % KD])
            dve.wait_ge(s["mod_used"], 5)
            mod_evac(16, 48, 1)
            dve.wait_ge(s["mod_cols"], 2)
            eff_scale(2, 4, 0, 2)
            for i, m, g in ((3, 2, 1), (4, 5, 3)):
                dve.tensor_tensor(eff[:, i, :], mods[:, KD * m:KD * m + KD, 0], vecA[:, VA_NG + KD * g:VA_NG + KD * g + KD],
                                  ALU.mult).then_inc(s["eff_ready"], 1)
            for b in range(4):
                dve.wait_ge(s["rows_ps"], b + 1)
                dve.tensor_copy(rows[:, b // 2, 512 * (b % 2):512 * (b % 2) + 512], bank[4 + b][:, :]).then_inc(s["rows_ready"], 1)
            dve.wait_ge(s["o_std"], 1)
            chain(dve.reciprocal(stat[:, 8:16], stat[:, 24:32]))
            dve.wait_ge(s["gr_ready"], 8)
            for t in range(NT):
                for h in range(GH):
                    ins = dve.scalar_tensor_tensor(out=og[:, t, GDV * h:GDV * h + GDV],
                                                   in0=bank[2 * t + h // 2][:, GDV * (h % 2):GDV * (h % 2) + GDV],
                                                   scalar=stat[:, 8 + 4 * t + h:9 + 4 * t + h],
                                                   in1=rG[:, t, GDV * h:GDV * h + GDV], op0=ALU.mult, op1=ALU.mult)
                ins.then_inc(s["og_ready"], 1)

            def turn_evac(n, dst, order):
                for b in (1, 3):
                    dve.wait_ge(s["ogT_ps"], 4 * n + b + 1)
                    for k in (2 * b, 2 * b + 1):
                        ins = dve.tensor_copy(order(dst[:, k, :]), by_sma(bank[4 + b][:, 256 * (k - 2 * b):256 * (k - 2 * b) + 256]))
                    ins.then_inc(s["ogT_dve"], 1)

            turn_evac(0, ogT, by_sma)
            ffn = L["ffn"]
            low_weights(ffU[0], ffn[0], 0, "hiU_ready", 1, "loU_ready")
            low_weights(ffD[0], ffn[0], 2048, "hiD_ready", 1, "loD_ready")

            def gated_update(n, t):
                dve.wait_ge(s["y_std"], 2 * n + t + 1)
                chain(dve.reciprocal(stat[:, 86 + t:87 + t], stat[:, 38 + t:39 + t]))
                if n == 0:
                    dve.wait_ge(s["rows_ready"], 4)
                for h in range(2):
                    w = dve.scalar_tensor_tensor(out=xn[:, t, 512 * h:512 * h + 512], in0=bank[2 * t + h][:, :],
                                                 scalar=stat[:, 86 + t:87 + t], in1=rows[:, n, 512 * h:512 * h + 512],
                                                 op0=ALU.mult, op1=ALU.mult)
                    w.then_inc(s["dve_chain"], 1)
                    chain.k += 1
                dve.wait_ge(s["dve_chain"], chain.base + chain.k)
                dve.tensor_tensor(res[:, t, :], res[:, t, :], xn[:, t, :], ALU.add).then_inc(s["res_ready"], 1)
                dve.wait_ge(s["res_ready"], 2 * n + t + 1)

            norm_scale(2, res, xn, before=lambda t: gated_update(0, t))
            norm_evac(2, lambda k: normT[:, k, :], lambda k: eff[:, 2, k:k + 1], lambda k: mods[:, 3 * KD + k, 0:1], split=True)

            low_weights(ffU[1], ffn[1], 0, "hiU_ready", 2, "loU_ready")

            def split_hidden(j, n, product):
                whole, hi, lo = act_s[:, j % 2, 0:n], mid2[0][:, j % 2, 0:n], mid2[1][:, j % 2, 0:n]
                chain(dve.tensor_tensor(whole, *product, ALU.mult))
                chain(dve.tensor_copy(hi, whole))
                low(lo, whole, hi, "ff_mid")

            def ffn_step(f, j, n_up, n_down):
                dve.wait_ge(s["ff_act"], f + 1)
                if not isinstance(f, int) or f >= 2:
                    dve.wait_ge(s["w_used"], f - 1)
                split_hidden(j, 256, (act_a[:, j % 2, 0:256], bank[4 + j % 2][:, 256:512]))
                if n_up:
                    low_weights(ffU[j % 2], ffn[(j + 2) % FF_RING], 0, "hiU_ready", f + 3, "loU_ready")
                if n_down:
                    low_weights(ffD[(j + 1) % 2], ffn[(j + 1) % FF_RING], 2048, "hiD_ready", f + 2, "loD_ready")

            for f in range(FF_RING):
                ffn_step(f, f, True, True)
            with dve.Fori(0, FF_LOOPS - 1) as i:
                chain.enter(i, 2 * FF_RING)
                for j in range(FF_RING):
                    ffn_step(i * FF_RING + (FF_RING + j), j, True, True)
            chain.leave(FF_LOOPS - 1)
            for f in range(FF_LOOPS * FF_RING, FFC):
                ffn_step(f, f % FF_RING, f + 2 < FFC, f + 1 < FFC)

            norm_scale(3, res, xn, before=lambda t: gated_update(1, t))
            norm_evac(3, lambda k: hT[:, k, :], lambda k: vecB[:, VB_MIX + k:VB_MIX + k + 1], None)
            chain(dve.memset(kpe[:, :, 0:NOPE], 0.0))

            def rotate(dst, src, table, heads, w, tmp, last):
                n = heads * w
                a0, b0 = tmp[:, 0, 0:n].rearrange("p (h d) -> p h d", d=w), tmp[:, 1, 0:n]
                cos = table[:, 0, :].unsqueeze(1).to_broadcast([P, heads, w])
                sin = table[:, 1, :].rearrange("p (c d) -> p c d", c=2)
                dve.tensor_tensor(a0, src, cos, ALU.mult).then_inc(s["dve_chain"], 1)
                sw = src.rearrange("p h (c d) -> p h c d", c=2)[:, :, ::-1, :]
                dve.tensor_tensor(b0.rearrange("p (h c d) -> p h c d", c=2, d=w // 2), sw,
                                  sin.unsqueeze(1).to_broadcast([P, heads, 2, w // 2]), ALU.mult).then_inc(s["dve_chain"], 1)
                chain.k += 2
                dve.wait_ge(s["dve_chain"], chain.base + chain.k)
                last(dve.tensor_tensor(dst, a0, b0.rearrange("p (h d) -> p h d", d=w), ALU.add))

            dve.wait_ge(s["c_std"], 2)
            chain(dve.reciprocal(stat[:, 60:64], stat[:, 44:48]))
            for t in range(NT):
                dve.tensor_scalar(ctm[:, t, 0:QR], bank[4 + t][:, 0:QR], stat[:, 60 + t:61 + t], None, ALU.mult)\
                   .then_inc(s["c_ready"], 1)
                dve.tensor_scalar(ctm[:, t, QR:QR + KVR], bank[4 + t][:, QR:QR + KVR], stat[:, 62 + t:63 + t], None, ALU.mult)\
                   .then_inc(s["c_ready"], 1)
                rotate(kpe[:, t:t + 1, NOPE:MQ], bank[4 + t][:, QR + KVR:416].unsqueeze(1), mrope[:, t], 1, ROPE, rt,
                       lambda ins: ins.then_inc(s["kpe_ready"], 1))
                dve.wait_ge(s["kpe_ready"], t + 1)
            for c in range(0, 8, 2):
                dve.wait_ge(s["qk_ps"], c + 1)
                dve.tensor_copy(qkN[:, c, :], bank[6][:, 0:256]).then_inc(s["qk_dve"], 1)
            dve.wait_ge(s["vn_ps"], 1)
            dve.tensor_copy(vN[:, 0, :], bank[6][:, :]).then_inc(s["vn_dve"], 1)
            dve.wait_ge(s["cT_ps"], 2)
            dve.tensor_scalar(cT[:, 2, :], bank[5][:, 0:256], vecA[:, VA_KN:VA_KN + 1], None, ALU.mult).then_inc(s["cT_dve"], 1)
            dve.tensor_copy(kM[NOPE:MQ, :, :], bank[5][NOPE:MQ, 256:512].unsqueeze(1).to_broadcast([ROPE, MLA_H, SEQ]))\
               .then_inc(s["cT_dve"], 1)
            for t in range(NT):
                for hf in range(2):
                    b = 2 * t + hf
                    dve.wait_ge(s["mq_ps"], b + 1)
                    src = bank[b][:, 0:384].rearrange("p (h d) -> p h d", d=MQ)
                    dst = qtm[:, t, 4 * hf:4 * hf + 4, :]
                    dve.tensor_copy(dst[:, :, 0:NOPE], src[:, :, 0:NOPE]).then_inc(s["mq_rot"], 1)
                    rotate(dst[:, :, NOPE:MQ], src[:, :, NOPE:MQ], mrope[:, t], 4, ROPE, rt, lambda ins: ins.then_inc(s["mq_rot"], 1))
                    dve.wait_ge(s["mq_rot"], 2 * b + 2)
            for i in range(4):
                dve.wait_ge(s["mqT_ps"], i + 1)
                dve.tensor_copy(qM[0:MQ, 2 * i:2 * i + 2, :], bank[i][0:MQ, :].rearrange("p (h t) -> p h t", h=2))\
                   .then_inc(s["mqT_out"], 1)

            def neg_max(u, j, src, halves, scale, addend):
                dve.wait_ge(s["s_ps"], u + 1)
                v = bank[3 + j % 2][:, :].rearrange("p (a k) -> p a k", a=halves)
                dst = stat[:, 48 + 2 * (j % 4):48 + 2 * (j % 4) + halves]
                if addend is not None:
                    if not isinstance(u, int) or u >= 2:
                        dve.wait_ge(s["prob_ready"], u - 1)
                    sc = score[:, j % 2, :].rearrange("p (a k) -> p a k", a=halves)
                    chain(dve.scalar_tensor_tensor(out=sc, in0=v, scalar=scale, in1=addend, op0=ALU.mult, op1=ALU.add))
                    dve.tensor_reduce(dst, sc, AX, ALU.max, negate=True).then_inc(s["max_ready"], 1)
                else:
                    chain(dve.tensor_reduce(dst, v, AX, ALU.max, negate=True))
                    dve.tensor_scalar(dst, dst, scale, None, ALU.mult).then_inc(s["max_ready"], 1)

            dve.wait_ge(s["bias_ready"], NA_H)
            for u in range(U_OD):
                if u < NA_H:
                    neg_max(u, u, None, 2, HD ** -0.5, nabias[:, u])
                else:
                    neg_max(u, u, None, 2, MQ ** -0.5, None)
                if u == NA_H + 2 or u == U_OD - 1:
                    k = 0 if u < U_OD - 1 else 1
                    dve.wait_ge(s["pv_ps"], NA_H * (k + 1))
                    r = rsum[:, 0:32].rearrange("p (t h) -> p t h", t=2)[:, :, 8 * k:8 * k + 8]
                    ri = rinv[:, 16 * k:16 * k + 16].rearrange("p (t h) -> p t h", t=2)
                    chain(dve.reciprocal(ri, r))
                    for t in range(NT):
                        dve.tensor_tensor(om[:, t, 512 * k:512 * k + 512].rearrange("p (h d) -> p h d", d=HD),
                                          bank[OUT_BANK[k][t]][:, :].rearrange("p (h d) -> p h d", d=HD),
                                          ri[:, t, :].unsqueeze(2).to_broadcast([P, 8, HD]), ALU.mult).then_inc(s["o_out"], 1)
            turn_evac(1, oT, by_sma)

            def update(n, t):
                dve.wait_ge(*((s["y_half"], n + 1) if t == 0 else y_done(n)))
                for h in range(2):
                    v = res[:, t, 512 * h:512 * h + 512]
                    ins = dve.tensor_tensor(v, v, bank[2 * t + h][:, :], ALU.add)
                ins.then_inc(s["res_ready"], 1)
                dve.wait_ge(s["res_ready"], 2 * n + t + 1)

            def mlp_first(l):
                e, n = L["mlp", l], FFC + 16 * l
                low_weights(mlU[0], e[0], 0, "hiU_ready", n + 1, "loU_ready")
                low_weights(mlD[0], e[0], 2048, "hiD_ready", n + 1, "loD_ready")
                low_weights(mlU[1], e[1], 0, "hiU_ready", n + 2, "loU_ready")

            mlp_first(0)
            norm_scale(4, res, xn, before=lambda t: update(2, t))
            norm_evac(4, lambda k: normT[:, k, :], lambda k: vecB[:, VB_MLP + k:VB_MLP + k + 1], None, split=True)

            def mlp(l):
                first = L["mlp", l]

                def step(r, j, n_up, n_down):
                    st = r * MLP_RING + (FFC + 16 * l + j)
                    dve.wait_ge(s["ff_act"], st + 1)
                    dve.wait_ge(s["w_used"], st - 1)
                    split_hidden(j, 512, (act_a[:, j % 2, :], act_a[:, j % 2, :]))
                    if n_up:
                        low_weights(mlU[j % 2], first[(j + 2) % MLP_RING], 0, "hiU_ready", st + 3, "loU_ready")
                    if n_down:
                        low_weights(mlD[(j + 1) % 2], first[(j + 1) % MLP_RING], 2048, "hiD_ready", st + 2, "loD_ready")

                with dve.Fori(0, MLP_LOOPS - 1) as i:
                    chain.enter(i, 2 * MLP_RING)
                    for j in range(MLP_RING):
                        step(i, j, True, True)
                chain.leave(MLP_LOOPS - 1)
                for j in range(MLP_RING):
                    step(MLP_LOOPS - 1, j, j + 2 < MLP_RING, j + 1 < MLP_RING)

            mlp(0)

            def od_low(m, par, g):
                low_weights(odW[(3 * par + g) % 2], L["od"][g], 0, "od_hi", 3 * m + (g + 1), "od_lo")

            od_low(0, 0, 0)
            norm_scale(5, res, xn, before=lambda t: update(3, t))
            norm_evac(5, lambda k: normT[:, k, :], lambda k: vecB[:, VB_MIX + 8 + k:VB_MIX + 9 + k], None, order=dilated, split=True)

            def od_rotate(m, par, g, t):
                dve.wait_ge(s["od_raw"], 6 * m + (2 * g + t + 1))
                if not isinstance(m, int) or 3 * m + g >= 2:
                    dve.wait_ge(s["qkT_ps"], 3 * m + (g - 1))
                rotate(qr[:, (3 * par + g) % 2, t, :].rearrange("p (h d) -> p h d", d=HD),
                       raw[:, t, :].rearrange("p (h d) -> p h d", d=HD), orope[:, t], 4, HD, ro,
                       lambda ins: ins.then_inc(s["rot_ready"], 1))
                dve.wait_ge(s["rot_ready"], 6 * m + (2 * g + t + 1))

            def od_max(u, j):
                neg_max(u, j, None, 1, HD ** -0.5, omask[:, j % 2, :].unsqueeze(1))

            om5 = om.rearrange("p t (n h d) -> p t n h d", h=2, d=HD)

            def od_out(n, par):
                dve.wait_ge(s["pv_ps"], 4 * n + (U_OD + 4))
                chain(dve.reciprocal(rinv[:, 32 + 4 * par:36 + 4 * par], rsum[:, 32 + 4 * par:36 + 4 * par]))
                for t in range(NT):
                    ins = dve.tensor_tensor(om5[:, t, n, :, :], bank[7][:, P * t:P * t + P].rearrange("p (h d) -> p h d", d=HD),
                                            rinv[:, 32 + 4 * par + 2 * t:34 + 4 * par + 2 * t].unsqueeze(2).to_broadcast([P, 2, HD]),
                                            ALU.mult)
                ins.then_inc(s["o_out"], 1)

            def od_pair(m, n, pm, pn):
                u = None if n is None else 4 * n + U_OD
                if m is not None:
                    od_low(m, pm, 1)
                    od_rotate(m, pm, 0, 0)
                    od_rotate(m, pm, 0, 1)
                    od_low(m, pm, 2)
                    od_rotate(m, pm, 1, 0)
                    od_rotate(m, pm, 1, 1)
                if n is not None:
                    od_max(u + 0, 0)
                    od_max(u + 1, 1)
                if m is not None:
                    if not isinstance(m, int) or m < OD_PAIRS - 1:
                        od_low(m + 1, 1 - pm, 0)
                    od_rotate(m, pm, 2, 0)
                if n is not None:
                    od_max(u + 2, 2)
                    od_max(u + 3, 3)
                if m is not None:
                    od_rotate(m, pm, 2, 1)
                if n is not None:
                    od_out(n, pn)

            od_pair(0, None, 0, None)
            with dve.Fori(0, OD_PAIRS // 2 - 1) as i:
                chain.enter(i, 2 * (6 * 2 + 4 + 1))
                od_pair(2 * i + 1, 2 * i, 1, 0)
                od_pair(2 * i + 2, 2 * i + 1, 0, 1)
            chain.leave(OD_PAIRS // 2 - 1)
            od_pair(OD_PAIRS - 1, OD_PAIRS - 2, 1, 0)
            od_pair(None, OD_PAIRS - 1, None, 1)
            turn_evac(2, oT, dilated)
            mlp_first(1)
            norm_scale(6, res, xn, before=lambda t: update(4, t))
            norm_evac(6, lambda k: normT[:, k, :], lambda k: vecB[:, VB_MLP + 8 + k:VB_MLP + 9 + k], None, split=True)
            mlp(1)
            dve.wait_ge(s["final_loaded"], 16)
            norm_scale(7, res, xn, before=lambda t: update(5, t))

        @block.tensor
        def _(pe):
            mm = pe.matmul

            def landed_wait(e):
                pe.wait_ge(e.sem, e.value)

            pe.wait_ge(s["c_loaded"], 16 * 2)
            pe.wait_ge(s["consts_loaded"], 16)
            pe.transpose(bank[4][:, 0:VA_NG], hTs[0:VA_NG, 0:P], ident[0:VA_NG, 0:VA_NG]).then_inc(s["vec_ps"], 1)

            def turn_tokens(n, src):
                for t in range(NT):
                    pe.wait_ge(s["xn_ready"], 2 * n + t + 1)
                    if t == 0 and n == 1:
                        pe.wait_ge(s["vec_cols"], 3)
                        pe.wait_ge(s["mod_cols"], 1)
                    for b in range(4):
                        for k in (2 * b, 2 * b + 1):
                            ins = pe.transpose(turned_bank(n, b)[:, 256 * (k - 2 * b) + P * t:256 * (k - 2 * b) + P * t + P],
                                               src[:, t, P * k:P * k + P], ident)
                        if t == NT - 1:
                            ins.then_inc(s["xT_ps"], 1)

            def hT_wait(n):
                pe.wait_ge(s["hT_act"], 2 * n + 2)
                pe.wait_ge(s["hT_dve"], 2 * n + 2)

            def mod_direct(i):
                e = L["mod", i]
                landed_wait(e)
                w = pv(e)
                for c in range(4):
                    for k in range(MOD_DVE, KD):
                        mm(bank[7][:, 2 * (4 * i + c):2 * (4 * i + c) + 2], w[:, k, P * c:P * c + P], silc[:, k, :],
                           start=(i == 0 and c == 0 and k == MOD_DVE), stop=False, skip_group_check=True)

            def mod_reduce(i, j, col, src, start):
                for c in range(4):
                    ins = mm(bank[7][:, col + 2 * c + j:col + 2 * c + j + 1], src[:, P * c:P * c + P], ones[:, :],
                             start=(start and c == 0), stop=True, skip_group_check=True)
                return ins

            def mod_first(i):
                pe.wait_ge(s["mod_sum"], i + 1)
                for j in range(2):
                    ins = mod_reduce(i, j, 8 * i, first_sums[:, i, j, :], False)
                ins.then_inc(s["mod_used"], 1)

            pe.wait_ge(s["silu_done"], 2)
            pe.wait_ge(s["zero_ready"], 2)
            for i in range(4):
                mod_direct(i)
                if i:
                    mod_first(i - 1)
            pe.wait_ge(s["vecs_loaded"], 16 * 7)
            n = VA_N - VA_NG
            pe.transpose(bank[5][:, 0:n], hTs[0:n, P:2 * P], ident[0:n, 0:n]).then_inc(s["vec_ps"], 1)
            pe.transpose(bank[6][:, 0:VB_N], hTs[0:VB_N, 2 * P:3 * P], ident[0:VB_N, 0:VB_N]).then_inc(s["vec_ps"], 1)
            turn_tokens(0, xn)
            mod_first(3)
            turn_tokens(1, rG)
            hT_wait(1)
            pe.wait_ge(s["small_loaded"], 32)
            for k in range(KD):
                ins = mm(bank[0][0:2 * RANK, :], wglr[:, k, :], hT_all[:, k, :], start=(k == 0), stop=(k == KD - 1))
            ins.then_inc(s["glr_ps"], 1)
            pe.wait_ge(s["glr_ready"], 1)
            pe.wait_ge(s["gate_w_loaded"], 32)
            for zh in range(8):
                if zh >= 4:
                    pe.wait_ge(s["gate_in"], zh - 3)
                mm(bank[1 + zh % 4][:, :], wgate[:, P * zh:P * zh + P], glrT, start=True, stop=True).then_inc(s["gate_ps"], 1)

            for j in range(20):
                if j >= 3 and j < 19:
                    pe.wait_ge(s["proj_out"], j - 2)
                if j == 19:
                    pe.wait_ge(s["silu_r"], 1)
                b = bank[5 + j % 3]
                if j < 8:
                    e = L["k" if j < 4 else "q", (j % 4) // 2]
                    if j % 2 == 0:
                        landed_wait(e)
                    toks = slice(0, 512) if j < 4 else slice(256, 512)
                    for k in range(KD):
                        ins = mm(b[:, 0:toks.stop - toks.start], pv(e)[:, k, P * (j % 2):P * (j % 2) + P], hT_all[:, k, toks],
                                 start=(k == 0), stop=(k == KD - 1))
                    ins.then_inc(s["proj_ps"], 1)
                else:
                    per = 4 if j < 16 else 2
                    jj = j - (8 if j < 16 else 16)
                    e = L["v" if j < 16 else "r", jj // per]
                    if jj % per == 0:
                        landed_wait(e)
                    tok = P * (jj % per) + (0 if j < 16 else 256)
                    for k in range(KD):
                        ins = mm(b[:, :], hT_all[:, k, tok:tok + P], pv(e)[:, k, :], start=(k == 0), stop=(k == KD - 1))
                    ins.then_inc(s["proj_ps"], 1)
            pe.wait_ge(s["silu_r"], 4)

            pe.wait_ge(s["kd_ready"], 4)
            pe.wait_ge(s["ke_ready"], 2)
            pe.wait_ge(s["proj_out"], 16)
            for z in range(2):
                for u in range(2):
                    for h in range(2):
                        for t in range(NT):
                            ins = mm(bank[4 + 2 * z + u][:, P * (2 * h + t):P * (2 * h + t) + P],
                                     kd[:, z, 2 * u + h, P * t:P * t + P], qd[:, z, 2 * u + h, P * t:P * t + P],
                                     start=True, stop=True)
                    ins.then_inc(s["sT_ps"], 1)
                for h in range(GH):
                    zh = GH * z + h
                    if zh >= 4:
                        pe.wait_ge(s["keT_act"] if zh % 2 else s["keT_dve"], (zh - 4) // 2 + 1)
                    for t in range(4):
                        ins = pe.transpose(bank[zh % 4][:, P * t:P * t + P], G1[:, z, h, P * t:P * t + P], ident)
                    ins.then_inc(s["keT_ps"], 1)
            pe.wait_ge(s["sT_ready"], 4)
            pe.wait_ge(s["keT_act"], 4)
            pe.wait_ge(s["keT_dve"], 4)

            def state_update(j, z):
                if j:
                    pe.wait_ge(s["state_ready"], 2 * (j - 1) + z + 1)
                ch = chunk_of(z, j)
                lo = CHUNK * (ch % 2)
                for h in range(GH):
                    ins = mm(bank[4 + 2 * z + h // 2][:, GDV * (h % 2):GDV * (h % 2) + GDV], keT[lo:lo + CHUNK, z, h, ch // 2, :],
                             vG[lo:lo + CHUNK, ch // 2, GDV * h:GDV * h + GDV], start=True, stop=True)
                ins.then_inc(s["upd_ps"], 1)

            def from_state(j, z):
                pe.wait_ge(s["state_ready"], 2 * j + z + 1)
                cl = j - 3 if z == 0 else 6 - j
                lo = CHUNK * (cl % 2)
                for h in range(GH):
                    ins = mm(bank[2 * (cl // 2) + h // 2][lo:lo + CHUNK, GDV * (h % 2):GDV * (h % 2) + GDV],
                             qd[:, z, h, CHUNK * cl:CHUNK * cl + CHUNK], states[:, (j + 1) % 2, z, h, :],
                             start=False, stop=False, skip_group_check=True)
                ins.then_inc(s["inter_ps"], 1)

            state_update(0, 0)
            state_update(0, 1)
            for t in range(NT):
                for u in range(2):
                    for h in range(2):
                        for z in range(2):
                            mm(bank[2 * t + u][:, GDV * h:GDV * h + GDV], sT[:, z, u, 2 * h + t, :],
                               vG[:, 2 + t, GDV * (2 * u + h):GDV * (2 * u + h) + GDV], start=(h == 0 and z == 0), stop=False,
                               skip_group_check=True)
            for j in range(1, 7):
                for z in range(2):
                    state_update(j, z)
                if j > 3:
                    for z in range(2):
                        from_state(j - 1, z)
            for z in range(2):
                from_state(6, z)
            pe.wait_ge(s["zero_ready"], 2)
            for b in range(4):
                ins = mm(bank[b][:, 0:512], zero[:, 0:P], zero[:, :], start=False, stop=True, skip_group_check=True)
            ins.then_inc(s["o_ps"], 1)
            pe.wait_ge(s["mod_sum"], 12 - len(MOD_POOL))
            pe.wait_ge(s["pool_sum"], len(MOD_POOL))
            pe.wait_ge(s["state_ready"], 14)
            for i in range(4, 12):
                ins = mod_reduce(i, 0, 8 * (i - 4), late_sum(i), i == 4)
            ins.then_inc(s["mod_used"], 1)
            pe.wait_ge(s["state_ready"], 14)
            pe.wait_ge(s["eff_ready"], 5)
            for b in range(4):
                for k in range(4):
                    kk = 4 * (b % 2) + k
                    ins = mm(bank[4 + b][:, P * k:P * k + P], eff[:, 3 + b // 2, kk:kk + 1].to_broadcast([P, P]), ident,
                             start=True, stop=True)
                ins.then_inc(s["rows_ps"], 1)

            def turn_mixed(n, src):
                for b in range(4):
                    for k in (2 * b, 2 * b + 1):
                        for t in range(NT):
                            ins = pe.transpose(bank[4 + b][:, 256 * (k - 2 * b) + P * t:256 * (k - 2 * b) + P * t + P],
                                               src[:, t, P * k:P * k + P], ident)
                    ins.then_inc(s["ogT_ps"], 1)

            def out_product(n, keys, srcT):
                pe.wait_ge(s["ogT_act"], 2 * n + 2)
                pe.wait_ge(s["ogT_dve"], 2 * n + 2)
                def part(e, i, b, kk):
                    k = 4 * i + kk
                    return mm(bank[b][:, :], srcT[:, k, P * (b // 2):P * (b // 2) + P], pv(e)[:, kk, 512 * (b % 2):512 * (b % 2) + 512],
                              start=(k == 0), stop=(k == KD - 1))

                e = L[keys[0]]
                landed_wait(e)
                for kk in range(4):
                    for b in range(4):
                        ins = part(e, 0, b, kk)
                ins.then_inc(s["out_used"], 1)
                e = L[keys[1]]
                landed_wait(e)
                for b in range(4):
                    for kk in range(4):
                        ins = part(e, 1, b, kk)
                    if b == 1:
                        ins.then_inc(s["y_half"], 1)
                ins.then_inc(s["out_used"], 1)

            pe.wait_ge(s["rows_ready"], 4)
            pe.wait_ge(s["og_ready"], 2)
            turn_mixed(0, og)
            out_product(0, [("go", 0), ("go", 1)], ogT)
            turn_tokens(2, xn)

            def zero_banks():
                for b in range(4):
                    mm(bank[b][:, :], zero[:, 0:P], zero[:, :], start=True, stop=False, skip_group_check=True)

            def close_banks(t):
                for b in (2 * t, 2 * t + 1):
                    ins = mm(bank[b][:, :], zero[:, 0:P], zero[:, :], start=False, stop=True, skip_group_check=True)
                ins.then_inc(s["y_ps" if t else "y_half"], 1)

            zero_banks()

            def split_mm(out_, left, right, start, stop):
                flag = {"skip_group_check": True} if not (start or stop) else {}
                mm(out_, left[0], right[0], start=start, stop=False, **flag)
                mm(out_, left[0], right[1], start=False, stop=False, **flag)
                return mm(out_, left[1], right[0], start=False, stop=stop, **flag)

            def both(pair, pick):
                return [pick(x) for x in pair]

            def ffn_up(f, j):
                pe.wait_ge(s["loU_ready"], f + 1)
                if not isinstance(f, int) or f >= 2:
                    pe.wait_ge(s["ff_mid"], f - 1)
                for g in range(2):
                    for n, k in enumerate(K_ORDER):
                        if n % 2 == 0 and g == 0:
                            pe.wait_ge(s["hT_lo"], n // 2 + 1)
                        ins = split_mm(bank[4 + j % 2][:, 256 * g:256 * g + 256],
                                       both(ffU[j % 2], lambda x: x[:, 1024 * g + P * k:1024 * g + P * k + P]),
                                       both(hT2, lambda x: x[:, k, :]), n == 0, n == KD - 1)
                ins.then_inc(s["ff_ps"], 1)

            def ffn_down(f, j, last=False):
                pe.wait_ge(s["ff_mid"], f + 1)
                pe.wait_ge(s["loD_ready"], f + 1)
                for b in range(4):
                    ins = split_mm(bank[b][:, :], both(mid2, lambda x: x[:, j % 2, P * (b // 2):P * (b // 2) + P]),
                                   both(ffD[j % 2], lambda x: x[:, 512 * (b % 2):512 * (b % 2) + 512]), False, False)
                    if last and b == 1:
                        close_banks(0)
                ins.then_inc(s["w_used"], 1)

            def ffn_round(f0, n, last=False):
                for j in range(n):
                    ffn_up(f0 + j, j)
                    if j:
                        ffn_down(f0 + (j - 1), j - 1)
                ffn_down(f0 + (n - 1), n - 1, last)

            ffn_round(0, FF_RING)
            with pe.Fori(0, FF_LOOPS - 1) as i:
                ffn_round(i * FF_RING + FF_RING, FF_RING)
            ffn_round(FF_LOOPS * FF_RING, FFC - FF_LOOPS * FF_RING, last=True)
            close_banks(1)

            turn_tokens(3, xn)
            hT_wait(3)
            e = L["c"]
            landed_wait(e)
            for t in range(NT):
                for k in range(KD):
                    ins = mm(bank[4 + t][:, 0:416], hT[:, k, P * t:P * t + P], pv(e)[:, k, :], start=(k == 0), stop=(k == KD - 1))
                ins.then_inc(s["c_ps"], 1)
            for c in range(8):
                e = L["qk", c // 2]
                if c % 2 == 0:
                    landed_wait(e)
                if c >= 2:
                    pe.wait_ge(s["qk_act"] if c % 2 else s["qk_dve"], c // 2)
                for k in range(KD):
                    ins = mm(bank[6 + c % 2][:, 0:256], pv(e)[:, k, P * (c % 2):P * (c % 2) + P], hT[:, k, :],
                             start=(k == 0), stop=(k == KD - 1))
                ins.then_inc(s["qk_ps"], 1)
            landed_wait(L["va"])
            pe.wait_ge(s["qk_act"], 4)
            pe.wait_ge(s["qk_dve"], 4)
            for t in range(NT):
                for k in range(KD):
                    ins = mm(bank[6 + t][:, :], hT[:, k, P * t:P * t + P], pv(L["va"])[:, k, :], start=(k == 0), stop=(k == KD - 1))
                ins.then_inc(s["vn_ps"], 1)
            pe.wait_ge(s["c_ready"], 4)
            pe.wait_ge(s["kpe_ready"], 2)
            for k in range(3):
                for t in range(NT):
                    ins = pe.transpose(bank[4 + k // 2][:, 256 * (k % 2) + P * t:256 * (k % 2) + P * t + P], ctm[:, t, P * k:P * k + P], ident)
                if k == 1:
                    ins.then_inc(s["cT_ps"], 1)
            for t in range(NT):
                ins = pe.transpose(bank[5][0:MQ, 256 + P * t:256 + P * t + P], kpe[:, t, :], ident)
            ins.then_inc(s["cT_ps"], 1)
            pe.wait_ge(s["cT_act"], 2)
            pe.wait_ge(s["cT_dve"], 2)
            pe.wait_ge(s["vn_act"], 1)
            pe.wait_ge(s["vn_dve"], 1)
            landed_wait(L["ukv"])
            wk = pv(L["ukv"])[:, 0, :].rearrange("p (h c) -> p h c", c=NOPE + HD)
            for h in range(MLA_H):
                ins = mm(bank[4 + h // 2][0:NOPE, 256 * (h % 2):256 * (h % 2) + 256], wk[:, h, 0:NOPE], cT[:, 2, :], start=True, stop=True)
                if h % 2:
                    ins.then_inc(s["mk_ps"], 1)
            landed_wait(L["uq"])
            for t in range(NT):
                for hf in range(2):
                    for k in range(2):
                        ins = mm(bank[2 * t + hf][:, 0:384], cT[:, k, P * t:P * t + P], pv(L["uq"])[:, k, 384 * hf:384 * hf + 384],
                                 start=(k == 0), stop=(k == 1))
                    ins.then_inc(s["mq_ps"], 1)
            pe.wait_ge(s["mk_out"], MLA_H)
            for t in range(NT):
                mm(bank[4 + t][:, :], cT[:, 2, P * t:P * t + P], wk[:, :, NOPE:], start=True, stop=True).then_inc(s["mv_ps"], 1)
            pe.wait_ge(s["mq_rot"], 8)
            for i in range(4):
                for h in (2 * i, 2 * i + 1):
                    for t in range(NT):
                        ins = pe.transpose(bank[i][0:MQ, 256 * (h - 2 * i) + P * t:256 * (h - 2 * i) + P * t + P], qtm[:, t, h, :], ident)
                ins.then_inc(s["mqT_ps"], 1)
            pe.wait_ge(s["mqT_out"], 4)
            pe.wait_ge(s["mv_out"], 2)
            pe.wait_ge(s["cT_dve"], 2)

            def ev_scores(u):
                if u >= 2:
                    pe.wait_ge(s["prob_ready"], u - 1)
                for t in range(NT):
                    if u < NA_H:
                        lo = HD * (u % 2)
                        q, k = qkN[lo:lo + HD, u // 2, P * t:P * t + P], qkN[lo:lo + HD, 4 + u // 2, :]
                    else:
                        q, k = qM[0:MQ, u - NA_H, P * t:P * t + P], kM[0:MQ, u - NA_H, :]
                    ins = mm(bank[3 + u % 2][:, 256 * t:256 * t + 256], q, k, start=True, stop=True)
                ins.then_inc(s["s_ps"], 1)

            def turn_probs(u, j, count):
                pe.wait_ge(s["prob_ready"], count)
                if not isinstance(u, int) or u >= 2:
                    pe.wait_ge(s["pT_ready"], u - 1)
                for b in range(4):
                    ins = pe.transpose(bank[5 + j % 2][:, P * b:P * b + P], prob[:, j % 2, P * b:P * b + P], ident)
                ins.then_inc(s["pT_ps"], 1)

            def ev_values(u):
                pe.wait_ge(s["pT_ready"], u + 1)
                k, h = u // 8, u % 8
                v = vN if k == 0 else vM
                for t in range(NT):
                    for c in range(2):
                        ins = mm(bank[OUT_BANK[k][t]][:, HD * h:HD * h + HD], probT[:, u % 2, P * (2 * t + c):P * (2 * t + c) + P],
                                 v[:, c, HD * h:HD * h + HD], start=(c == 0), stop=(c == 1))
                ins.then_inc(s["pv_ps"], 1)

            for u in range(U_OD + 2):
                if u < U_OD:
                    ev_scores(u)
                if 1 <= u <= U_OD:
                    turn_probs(u - 1, u - 1, u)
                if u >= 2:
                    ev_values(u - 2)
            pe.wait_ge(s["o_out"], 4)
            pe.wait_ge(s["pT_ready"], U_OD)
            turn_mixed(1, om)
            out_product(1, [("eo", 0), ("eo", 1)], oT)

            def mlp(l):
                def up(st, j):
                    pe.wait_ge(s["loU_ready"], st + 1)
                    pe.wait_ge(s["ff_mid"], st - 1)
                    for f in range(2):
                        for n, k in enumerate(K_ORDER):
                            if n % 2 == 0 and f == 0:
                                pe.wait_ge(s["hT_lo"], 4 + 8 * l + n // 2 + 1)
                            ins = split_mm(bank[4 + j % 2][:, 256 * f:256 * f + 256],
                                           both(mlU[j % 2], lambda x: x[:, 256 * k + P * f:256 * k + P * f + P]),
                                           both(hT2, lambda x: x[:, k, :]), n == 0, n == KD - 1)
                    ins.then_inc(s["ff_ps"], 1)

                def down(st, j, last=False):
                    pe.wait_ge(s["ff_mid"], st + 1)
                    pe.wait_ge(s["loD_ready"], st + 1)
                    for t in range(NT):
                        for f, b in ((0, 2 * t), (0, 2 * t + 1), (1, 2 * t), (1, 2 * t + 1)):
                            at = D * f + 512 * (b % 2)
                            ins = split_mm(bank[b][:, :], both(mid2, lambda x: x[:, j % 2, 256 * f + P * (b // 2):256 * f + P * (b // 2) + P]),
                                           both(mlD[j % 2], lambda x: x[:, at:at + 512]), False, False)
                        if last and t == 0:
                            close_banks(0)
                    ins.then_inc(s["w_used"], 1)

                zero_banks()
                def round_of(st, last=False):
                    for j in range(MLP_RING):
                        up(st + j, j)
                        if j:
                            down(st + (j - 1), j - 1)
                    down(st + (MLP_RING - 1), MLP_RING - 1, last)

                with pe.Fori(0, MLP_LOOPS - 1) as i:
                    round_of(i * MLP_RING + (FFC + 16 * l))
                round_of((MLP_LOOPS - 1) * MLP_RING + (FFC + 16 * l), last=True)
                close_banks(1)

            turn_tokens(4, xn)
            mlp(0)

            turn_tokens(5, xn)

            def od_proj(m, par, g, t):
                if t == 0:
                    pe.wait_ge(s["od_lo"], 3 * m + (g + 1))
                if not isinstance(m, int) or m or g:
                    pe.wait_ge(s["od_v"], 6 * m + (2 * g + t - 1))
                w = both(odW[(3 * par + g) % 2], lambda x: x[:, :].rearrange("p (j k c) -> p k j c", j=3, k=KD))
                for n, k in enumerate(K_ORDER):
                    if n % 2 == 0 and isinstance(m, int) and m == 0 and g == 0 and t == 0:
                        pe.wait_ge(s["hT_lo"], 8 + n // 2 + 1)
                    ins = split_mm(bank[t][:, 0:384], both(hT2, lambda x: x[:, k, P * t:P * t + P]),
                                   both(w, lambda x: x[:, k]), n == 0, n == KD - 1)
                ins.then_inc(s["od_ps"], 1)

            def od_turn(m, par, g):
                pe.wait_ge(s["rot_ready"], 6 * m + (2 * g + 2))
                if not isinstance(m, int) or m or g:
                    pe.wait_ge(s["qkT_out"], 3 * m + g)
                for j in range(2):
                    for t in range(NT):
                        ins = pe.transpose(bank[2][:, 256 * j + P * t:256 * j + P * t + P],
                                           qr[:, (3 * par + g) % 2, t, P * j:P * j + P], ident)
                ins.then_inc(s["qkT_ps"], 1)

            def od_scores(u, par, j):
                pe.wait_ge(s["prob_ready"], u - 1)
                h, t = j // 2, j % 2
                lo = HD * h
                for g, (at, k0, n) in enumerate([(0, 256, 256), (256, 256 + P * t, P), (384, 256 + P * t, P)]):
                    ins = mm(bank[3 + j % 2][:, at:at + n], qkT[lo:lo + HD, par, g, P * t:P * t + P], qkT[lo:lo + HD, par, g, k0:k0 + n],
                             start=True, stop=True)
                ins.then_inc(s["s_ps"], 1)

            def od_attend(u, par, j, n):
                pe.wait_ge(s["pT_ready"], u + 1)
                if j == 0:
                    pe.wait_ge(s["o_out"], n + 4)
                h, t = j // 2, j % 2
                for b, (g, tile) in enumerate([(0, 0), (0, 1), (1, t), (2, t)]):
                    ins = mm(bank[7][:, P * t + HD * h:P * t + HD * h + HD], probT[:, j % 2, P * b:P * b + P],
                             vO[:, par, g, tile, HD * h:HD * h + HD], start=(b == 0), stop=(b == 3))
                ins.then_inc(s["pv_ps"], 1)

            def od_pair(m, n, pm, pn):
                u = None if n is None else 4 * n + U_OD
                if m is not None:
                    od_proj(m, pm, 0, 0)
                    od_proj(m, pm, 0, 1)
                if n is not None:
                    od_turn(n, pn, 2)
                if m is not None:
                    od_proj(m, pm, 1, 0)
                    od_proj(m, pm, 1, 1)
                if n is not None:
                    pe.wait_ge(s["qkT_out"], 3 * n + 3)
                    od_scores(u + 0, pn, 0)
                    od_scores(u + 1, pn, 1)
                if m is not None:
                    od_turn(m, pm, 0)
                    od_proj(m, pm, 2, 0)
                if n is not None:
                    turn_probs(u + 0, 0, u + 1)
                    turn_probs(u + 1, 1, u + 2)
                    od_scores(u + 2, pn, 2)
                    od_scores(u + 3, pn, 3)
                if m is not None:
                    od_proj(m, pm, 2, 1)
                if n is not None:
                    od_attend(u + 0, pn, 0, n)
                    od_attend(u + 1, pn, 1, n)
                    turn_probs(u + 2, 2, u + 3)
                    turn_probs(u + 3, 3, u + 4)
                if m is not None:
                    od_turn(m, pm, 1)
                if n is not None:
                    od_attend(u + 2, pn, 2, n)
                    od_attend(u + 3, pn, 3, n)

            od_pair(0, None, 0, None)
            with pe.Fori(0, OD_PAIRS // 2 - 1) as i:
                od_pair(2 * i + 1, 2 * i, 1, 0)
                od_pair(2 * i + 2, 2 * i + 1, 0, 1)
            od_pair(OD_PAIRS - 1, OD_PAIRS - 2, 1, 0)
            od_pair(None, OD_PAIRS - 1, None, 1)
            pe.wait_ge(s["o_out"], 4 + OD_PAIRS)
            turn_mixed(2, om)
            out_product(2, [("oo", 0), ("oo", 1)], oT)
            turn_tokens(6, xn)
            mlp(1)


_INS = ['x', 'c', 'ctx', 'c_ctx', 'mod_w', 'mod_b', 'norm_g', 'ffn_w_in', 'ffn_w_out', 'gla_w_in', 'gla_w_gate',
        'gla_b_gate', 'gla_norm_g', 'gla_w_out', 'norm_mix_2', 'norm_mlp_2', 'norm_final_2', 'ev_w_in_2', 'ev_rpb_2',
        'ev_q_norm_2', 'ev_w_uq_2', 'ev_kv_norm_2', 'ev_w_ukv_2', 'ev_w_o_2', 'od_w_in_2', 'od_w_o_2', 'mlp_w1_2',
        'mlp_w2_2']


def kernel(**inputs):
    import numpy as _np
    import concourse.bacc as _bacc
    from concourse import mybir as _mybir
    from concourse.bass_utils import run_bass_kernel_spmd as _run

    nc = _bacc.Bacc("TRN2", target_bir_lowering=False, num_devices=1)
    arrays, args = {}, {}
    for name in _INS:
        v = _np.ascontiguousarray(inputs[name])
        arrays[f"in_{name}_dram"] = v
        args[name] = nc.dram_tensor(f"in_{name}_dram", v.shape, _mybir.dt.from_np(v.dtype), kind="ExternalInput").ap()
    table = constants()
    arrays["in_consts_dram"] = table
    args["consts"] = nc.dram_tensor("in_consts_dram", table.shape, F32, kind="ExternalInput").ap()
    out = nc.dram_tensor("out_0_dram", (1, SEQ, D), F32, kind="ExternalOutput").ap()
    program(nc, args, out)
    r = _run(nc, [arrays], core_ids=[0])
    return r.results[0]["out_0_dram"]
```
